# Optimizing a Trainium2 kernel written in Bass

```python
import jax, jax.numpy as jnp
from jax import lax
import numpy as np
import math

D_MODEL = 1024
BATCH = 1
SEQ = 1024
DEPTH = 1

MLA_HEADS = 8
MLA_NOPE = 64
MLA_ROPE = 32
MLA_V = 64
MLA_QK = MLA_NOPE + MLA_ROPE
MLA_Q_RANK = 256
MLA_KV_RANK = 128
RET_HEADS = 4
RET_DK = 64
RET_DV = 128
CHUNK = 128
Q_BLOCK = 128
D_FF = 4 * D_MODEL
ROPE_BASE = 10000.0
EPS = 1e-5
MLA_WIDTH = MLA_HEADS * MLA_V
RET_WIDTH = RET_HEADS * RET_DV
MIX_WIDTH = MLA_WIDTH + RET_WIDTH
ALPHA = (2.0 * DEPTH) ** 0.25
BETA = (8.0 * DEPTH) ** -0.25
IN_SPLITS = (MLA_Q_RANK, MLA_KV_RANK, MLA_ROPE,
             RET_HEADS * RET_DK, RET_HEADS * RET_DK, RET_WIDTH, RET_WIDTH)
IN_WIDTH = sum(IN_SPLITS)
IN_OFFSETS = tuple(int(v) for v in np.cumsum(IN_SPLITS)[:-1])


def layer_norm(x, g, b):
    xf = x.astype(jnp.float32)
    mu = jnp.mean(xf, -1, keepdims=True)
    var = jnp.mean(jnp.square(xf - mu), -1, keepdims=True)
    return ((xf - mu) * lax.rsqrt(var + EPS) * g.astype(jnp.float32) + b.astype(jnp.float32)).astype(x.dtype)

def rms_norm(x, g):
    xf = x.astype(jnp.float32)
    ms = jnp.mean(jnp.square(xf), -1, keepdims=True)
    return (xf * lax.rsqrt(ms + EPS) * g.astype(jnp.float32)).astype(x.dtype)

def rotary(x, pos):
    half = x.shape[-1] // 2
    inv = ROPE_BASE ** (-jnp.arange(half, dtype=jnp.float32) / half)
    ang = pos.astype(jnp.float32)[..., None] * inv
    cos = jnp.cos(ang)[:, :, None, :]
    sin = jnp.sin(ang)[:, :, None, :]
    x1 = x[..., :half].astype(jnp.float32)
    x2 = x[..., half:].astype(jnp.float32)
    return jnp.concatenate([x1 * cos - x2 * sin, x2 * cos + x1 * sin], -1).astype(x.dtype)

def causal_block_attention(q, k, v):
    b, s, h, dq = q.shape
    dv = v.shape[-1]
    nb = s // Q_BLOCK
    scale = dq ** -0.5
    qb = q.reshape(b, nb, Q_BLOCK, h, dq).transpose(1, 0, 3, 2, 4)
    kt = k.transpose(0, 2, 1, 3)
    vt = v.transpose(0, 2, 1, 3)
    k_idx = jnp.arange(s)

    def one_block(args):
        q_blk, i = args
        sc = jnp.einsum('bhqd,bhkd->bhqk', q_blk, kt,
                        preferred_element_type=jnp.float32) * scale
        q_idx = i * Q_BLOCK + jnp.arange(Q_BLOCK)
        mask = k_idx[None, :] <= q_idx[:, None]
        p = jax.nn.softmax(jnp.where(mask, sc, -jnp.inf), axis=-1)
        return jnp.einsum('bhqk,bhkd->bhqd', p.astype(vt.dtype), vt)

    out = lax.map(one_block, (qb, jnp.arange(nb)))
    return out.transpose(1, 0, 3, 2, 4).reshape(b, s, h * dv)

def mla_mixer(q_c, kv_c, k_r, pos, g_q, w_uq, g_kv, w_ukv):
    b, s, _ = q_c.shape
    q = (rms_norm(q_c, g_q) @ w_uq).reshape(b, s, MLA_HEADS, MLA_QK)
    q = jnp.concatenate([q[..., :MLA_NOPE], rotary(q[..., MLA_NOPE:], pos)], -1)
    kv = (rms_norm(kv_c, g_kv) @ w_ukv).reshape(b, s, MLA_HEADS, MLA_NOPE + MLA_V)
    k_nope, v = kv[..., :MLA_NOPE], kv[..., MLA_NOPE:]
    k_rope = rotary(k_r[:, :, None, :], pos)
    k = jnp.concatenate([k_nope, jnp.broadcast_to(k_rope, (b, s, MLA_HEADS, MLA_ROPE))], -1)
    return causal_block_attention(q, k, v)

def retention_mixer(q, k, v, g, pos, gn_g, gn_b):
    b, s, _ = q.shape
    n = s // CHUNK
    q = rotary(q.reshape(b, s, RET_HEADS, RET_DK), pos)
    k = rotary(k.reshape(b, s, RET_HEADS, RET_DK), pos) * (RET_DK ** -0.5)
    v = v.reshape(b, s, RET_HEADS, RET_DV)
    qc = q.reshape(b, n, CHUNK, RET_HEADS, RET_DK).transpose(0, 3, 1, 2, 4)
    kc = k.reshape(b, n, CHUNK, RET_HEADS, RET_DK).transpose(0, 3, 1, 2, 4)
    vc = v.reshape(b, n, CHUNK, RET_HEADS, RET_DV).transpose(0, 3, 1, 2, 4)

    log_g = jnp.log(1.0 - 2.0 ** (-5.0 - jnp.arange(RET_HEADS, dtype=jnp.float32)))
    idx = jnp.arange(CHUNK, dtype=jnp.float32)
    diff = idx[:, None] - idx[None, :]
    decay = jnp.where(diff >= 0, jnp.exp(log_g[:, None, None] * jnp.maximum(diff, 0.0)), 0.0)
    zeta = jnp.exp(log_g[:, None] * (CHUNK - 1 - idx))
    xi = jnp.exp(log_g[:, None] * (idx + 1.0))

    scores = jnp.einsum('bhnid,bhnjd->bhnij', qc, kc) * decay[None, :, None]
    inner = jnp.einsum('bhnij,bhnjv->bhniv', scores, vc)
    chunk_kv = jnp.einsum('bhnjd,hj,bhnjv->bhndv', kc, zeta, vc)
    g_chunk = jnp.exp(log_g * CHUNK).astype(chunk_kv.dtype)[None, :, None, None]

    def step(state, kv_n):
        return state * g_chunk + kv_n, state

    init = jnp.zeros((b, RET_HEADS, RET_DK, RET_DV), chunk_kv.dtype)
    _, prev = lax.scan(step, init, chunk_kv.transpose(2, 0, 1, 3, 4))
    prev = prev.transpose(1, 2, 0, 3, 4)
    cross = jnp.einsum('bhnid,bhndv->bhniv', qc, prev) * xi[None, :, None, :, None]

    o = (inner + cross).transpose(0, 2, 3, 1, 4).reshape(b, s, RET_HEADS, RET_DV)
    of = o.astype(jnp.float32)
    mu = jnp.mean(of, -1, keepdims=True)
    var = jnp.mean(jnp.square(of - mu), -1, keepdims=True)
    on = ((of - mu) * lax.rsqrt(var + EPS)).reshape(b, s, RET_WIDTH)
    on = on * gn_g.astype(jnp.float32) + gn_b.astype(jnp.float32)
    return (on * jax.nn.silu(g.astype(jnp.float32))).astype(g.dtype)

def first_inputs(seed: int = 0) -> dict:
    key = jax.random.key(seed)
    ks = jax.random.split(key, 24)
    f32 = jnp.float32
    nrm = lambda k, shape, fan: jax.random.normal(k, shape, f32) * (fan ** -0.5)
    gain = lambda k, shape: 1.0 + 0.05 * jax.random.normal(k, shape, f32)
    bias = lambda k, shape: 0.02 * jax.random.normal(k, shape, f32)

    x = jax.random.normal(ks[0], (BATCH, SEQ, D_MODEL), f32)
    c = jax.random.normal(ks[1], (BATCH, D_MODEL), f32)
    offset = jax.random.randint(ks[2], (BATCH, 1), 0, 1024, dtype=jnp.int32)
    positions = (offset + jnp.arange(SEQ, dtype=jnp.int32)[None, :]).astype(jnp.int32)

    in_col_scale = jnp.concatenate([
        jnp.ones((IN_WIDTH - 2 * RET_WIDTH,), f32),
        jnp.full((RET_WIDTH,), BETA, f32),
        jnp.ones((RET_WIDTH,), f32)])
    ukv_col_scale = jnp.tile(jnp.concatenate([jnp.ones((MLA_NOPE,), f32),
                                              jnp.full((MLA_V,), BETA, f32)]), MLA_HEADS)
    return {
        "x": x,
        "c": c,
        "positions": positions,
        "ln_in_g": gain(ks[3], (D_MODEL,)),
        "ln_in_b": bias(ks[4], (D_MODEL,)),
        "w_ada": nrm(ks[5], (DEPTH, D_MODEL, 6 * D_MODEL), D_MODEL) * 0.5,
        "b_ada": bias(ks[6], (DEPTH, 6 * D_MODEL)),
        "w_in": nrm(ks[7], (DEPTH, D_MODEL, IN_WIDTH), D_MODEL) * in_col_scale,
        "mla_q_norm": gain(ks[8], (DEPTH, MLA_Q_RANK)),
        "w_uq": nrm(ks[9], (DEPTH, MLA_Q_RANK, MLA_HEADS * MLA_QK), MLA_Q_RANK),
        "mla_kv_norm": gain(ks[10], (DEPTH, MLA_KV_RANK)),
        "w_ukv": nrm(ks[11], (DEPTH, MLA_KV_RANK, MLA_HEADS * (MLA_NOPE + MLA_V)), MLA_KV_RANK) * ukv_col_scale,
        "ret_gn_g": gain(ks[12], (DEPTH, RET_WIDTH)),
        "ret_gn_b": bias(ks[13], (DEPTH, RET_WIDTH)),
        "w_out": nrm(ks[14], (DEPTH, MIX_WIDTH, D_MODEL), MIX_WIDTH) * BETA,
        "ln1_g": gain(ks[15], (DEPTH, D_MODEL)),
        "ln1_b": bias(ks[16], (DEPTH, D_MODEL)),
        "w_ff1": nrm(ks[17], (DEPTH, D_MODEL, D_FF), D_MODEL) * BETA,
        "w_ff2": nrm(ks[18], (DEPTH, D_FF, D_MODEL), D_FF) * BETA,
        "ln2_g": gain(ks[19], (DEPTH, D_MODEL)),
        "ln2_b": bias(ks[20], (DEPTH, D_MODEL)),
    }

def first_block(x, c, positions, ln_in_g, ln_in_b, w_ada, b_ada, w_in, mla_q_norm, w_uq,
              mla_kv_norm, w_ukv, ret_gn_g, ret_gn_b, w_out, ln1_g, ln1_b,
              w_ff1, w_ff2, ln2_g, ln2_b):
    x = layer_norm(x, ln_in_g, ln_in_b)
    c_act = jax.nn.silu(c)
    for l in range(DEPTH):
        mod = c_act @ w_ada[l] + b_ada[l]
        sh1, sc1, gt1, sh2, sc2, gt2 = [m[:, None, :] for m in jnp.split(mod, 6, axis=-1)]

        h = x * (1.0 + sc1) + sh1
        proj = h @ w_in[l]
        q_c, kv_c, k_r, r_q, r_k, r_v, r_g = jnp.split(proj, IN_OFFSETS, axis=-1)
        a = mla_mixer(q_c, kv_c, k_r, positions, mla_q_norm[l], w_uq[l], mla_kv_norm[l], w_ukv[l])
        r = retention_mixer(r_q, r_k, r_v, r_g, positions, ret_gn_g[l], ret_gn_b[l])
        y = jnp.concatenate([a, r], axis=-1) @ w_out[l]
        x = layer_norm(ALPHA * x + gt1 * y, ln1_g[l], ln1_b[l])

        h = x * (1.0 + sc2) + sh2
        f = jnp.square(jax.nn.relu(h @ w_ff1[l])) @ w_ff2[l]
        x = layer_norm(ALPHA * x + gt2 * f, ln2_g[l], ln2_b[l])
    return x


CHUNK_2 = 64
MEM_LEN = 256
EPS_2 = 1e-6

DA_HEADS = 4
DA_QK_DIM = D_MODEL // 16
DA_V_DIM = 2 * DA_QK_DIM
DA_QK_COLS = DA_HEADS * 2 * DA_QK_DIM
DA_WIDTH = DA_HEADS * DA_V_DIM

GLA_HEADS = 4
GLA_K_DIM = D_MODEL // 16
GLA_V_DIM = D_MODEL // 8
GLA_QK_COLS = GLA_HEADS * GLA_K_DIM
GLA_WIDTH = GLA_HEADS * GLA_V_DIM
GLA_GATE_RANK = 16
GLA_TAU = 16.0

MIX_WIDTH_2 = DA_WIDTH + GLA_WIDTH
IN_WIDTH_2 = 2 * DA_QK_COLS + DA_WIDTH + 2 * GLA_QK_COLS + 2 * GLA_WIDTH + GLA_GATE_RANK

CROSS_HEADS = 4
CROSS_DIM = D_MODEL // CROSS_HEADS

N_GROUPS = 4
EXPERTS_PER_GROUP = 8
N_EXPERTS = N_GROUPS * EXPERTS_PER_GROUP
TOP_K = 2
D_EXPERT = D_MODEL // 2
EXPERT_BLOCK = 128


def _rmsnorm(t, g):
    tf = t.astype(jnp.float32)
    tf = tf * lax.rsqrt(jnp.mean(tf * tf, axis=-1, keepdims=True) + EPS_2)
    return (tf * g.astype(jnp.float32)).astype(t.dtype)

def _split_heads(t, n):
    b, s, _ = t.shape
    return t.reshape(b, s, n, -1).transpose(0, 2, 1, 3)

def _merge_heads(t):
    b, h, s, d = t.shape
    return t.transpose(0, 2, 1, 3).reshape(b, s, h * d)

def _diff_attention(q1, q2, k1, k2, v, lam):
    b, h, s, d = q1.shape
    n_blocks = s // Q_BLOCK
    scale = d ** -0.5
    key_chunk = jnp.arange(s) // CHUNK_2

    def to_blocks(t):
        return t.reshape(b, h, n_blocks, Q_BLOCK, d).transpose(2, 0, 1, 3, 4)

    def one_block(args):
        qb1, qb2, bi = args
        q_chunk = (bi * Q_BLOCK + jnp.arange(Q_BLOCK)) // CHUNK_2
        mask = key_chunk[None, :] <= q_chunk[:, None]

        def probs(qb, kk):
            sc = jnp.einsum('bhqd,bhkd->bhqk', qb, kk).astype(jnp.float32) * scale
            return jax.nn.softmax(jnp.where(mask, sc, -jnp.inf), axis=-1)

        p = probs(qb1, k1) - lam * probs(qb2, k2)
        return jnp.einsum('bhqk,bhkv->bhqv', p.astype(v.dtype), v)

    o = lax.map(one_block, (to_blocks(q1), to_blocks(q2), jnp.arange(n_blocks)))
    return o.transpose(1, 2, 0, 3, 4).reshape(b, h, s, v.shape[-1])

def _gla_chunked(q, k, v, log_a):
    b, h, s, dk = q.shape
    dv = v.shape[-1]
    nc = s // CHUNK_2
    q = q.reshape(b, h, nc, CHUNK_2, dk)
    k = k.reshape(b, h, nc, CHUNK_2, dk)
    v = v.reshape(b, h, nc, CHUNK_2, dv)
    L = jnp.cumsum(log_a.reshape(b, h, nc, CHUNK_2, dk), axis=3)
    L_end = L[:, :, :, -1, :]
    Lc = L - L[:, :, :, CHUNK_2 // 2 - 1:CHUNK_2 // 2, :]
    e_pos, e_neg = jnp.exp(Lc), jnp.exp(-Lc)
    a_past = jnp.einsum('bhnid,bhnjd->bhnij', q * e_pos, k * e_neg)
    a_fut = jnp.einsum('bhnid,bhnjd->bhnij', q * e_neg, k * e_pos)
    lower = jnp.tril(jnp.ones((CHUNK_2, CHUNK_2), dtype=bool))
    a = jnp.where(lower, a_past, a_fut)
    o_intra = jnp.einsum('bhnij,bhnjv->bhniv', a, v)
    u = jnp.einsum('bhnjd,bhnjv->bhndv', k * jnp.exp(L_end[:, :, :, None, :] - L), v)
    decay = jnp.exp(L_end)

    def step(state, inp):
        d_c, u_c = inp
        return state * d_c[..., None] + u_c, state

    _, s_prev = lax.scan(step, jnp.zeros((b, h, dk, dv), jnp.float32),
                         (jnp.moveaxis(decay, 2, 0), jnp.moveaxis(u, 2, 0)))
    s_prev = jnp.moveaxis(s_prev, 0, 2)
    o_inter = jnp.einsum('bhnid,bhndv->bhniv', q * jnp.exp(L), s_prev)
    return (o_intra + o_inter).reshape(b, h, s, dv)

def _mixer(h, norm_g, w_in, da_qn, da_kn, lq1, lk1, lq2, lk2, da_on, gate_w, gate_b, gla_on, w_o, lam_init):
    b, s, _ = h.shape
    f32 = jnp.float32
    u = _rmsnorm(h, norm_g)
    p = u @ w_in
    widths = (DA_QK_COLS, DA_QK_COLS, DA_WIDTH, GLA_QK_COLS, GLA_QK_COLS, GLA_WIDTH, GLA_WIDTH, GLA_GATE_RANK)
    parts = []
    off = 0
    for w in widths:
        parts.append(p[..., off:off + w])
        off += w
    dq, dk, dv, gq, gk, gv, gg, gr = parts

    dq = dq.reshape(b, s, DA_HEADS, 2, DA_QK_DIM).transpose(0, 2, 3, 1, 4)
    dk = dk.reshape(b, s, DA_HEADS, 2, DA_QK_DIM).transpose(0, 2, 3, 1, 4)
    dq = _rmsnorm(dq, da_qn)
    dk = _rmsnorm(dk, da_kn)
    dvh = _split_heads(dv, DA_HEADS)
    lam = (jnp.exp(jnp.sum(lq1.astype(f32) * lk1.astype(f32)))
           - jnp.exp(jnp.sum(lq2.astype(f32) * lk2.astype(f32))) + lam_init)
    da = _diff_attention(dq[:, :, 0], dq[:, :, 1], dk[:, :, 0], dk[:, :, 1], dvh, lam)
    da = _rmsnorm(da, da_on) * (1.0 - lam_init)
    da_out = _merge_heads(da)

    qg = _split_heads(gq, GLA_HEADS).astype(f32) * (GLA_K_DIM ** -0.5)
    kg = _split_heads(gk, GLA_HEADS).astype(f32)
    vg = _split_heads(gv, GLA_HEADS).astype(f32)
    z = gr.astype(f32) @ gate_w.astype(f32) + gate_b.astype(f32)
    log_a = _split_heads(jax.nn.log_sigmoid(z) / GLA_TAU, GLA_HEADS)
    og = _gla_chunked(qg, kg, vg, log_a)
    og = _rmsnorm(og, gla_on)
    gla_out = (_merge_heads(og) * jax.nn.silu(gg.astype(f32))).astype(h.dtype)

    return jnp.concatenate([da_out.astype(h.dtype), gla_out], axis=-1) @ w_o

def _cross_attention(h, mem, norm_g, norm_m, w_q, w_kv, qn, kn, w_out):
    b, s, d = h.shape
    m = mem.shape[1]
    u = _rmsnorm(h, norm_g)
    mn = _rmsnorm(mem, norm_m)
    q = _rmsnorm((u @ w_q).reshape(b, s, CROSS_HEADS, CROSS_DIM), qn)
    kv = mn @ w_kv
    k = _rmsnorm(kv[..., :d].reshape(b, m, CROSS_HEADS, CROSS_DIM), kn)
    v = kv[..., d:].reshape(b, m, CROSS_HEADS, CROSS_DIM)
    sc = jnp.einsum('bshd,bmhd->bhsm', q, k).astype(jnp.float32) * (CROSS_DIM ** -0.5)
    pr = jax.nn.softmax(sc, axis=-1).astype(v.dtype)
    o = jnp.einsum('bhsm,bmhd->bshd', pr, v).reshape(b, s, d)
    return o @ w_out

def _hier_moe(h, norm_g, w_group, b_group, w_expert, b_expert, w_gate, w_up, w_down):
    b, s, d = h.shape
    t = b * s
    f32 = jnp.float32
    xf = _rmsnorm(h, norm_g).reshape(t, d)
    xr = xf.astype(f32)
    p_group = jax.nn.softmax(xr @ w_group.astype(f32) + b_group.astype(f32), axis=-1)
    g_sel = jnp.argmax(p_group, axis=-1)
    p_g = jnp.take_along_axis(p_group, g_sel[:, None], axis=-1)
    e_logits = (xr @ w_expert.astype(f32) + b_expert.astype(f32)).reshape(t, N_GROUPS, EXPERTS_PER_GROUP)
    e_logits = jnp.take_along_axis(e_logits, g_sel[:, None, None], axis=1)[:, 0]
    top_p, top_i = lax.top_k(jax.nn.softmax(e_logits, axis=-1), TOP_K)
    gate = p_g * top_p / jnp.sum(top_p, axis=-1, keepdims=True)
    flat_id = (g_sel[:, None] * EXPERTS_PER_GROUP + top_i).reshape(-1).astype(jnp.int32)
    flat_gate = gate.reshape(-1)
    n_assign = t * TOP_K
    order = jnp.argsort(flat_id)
    sorted_id = flat_id[order]
    token_of = order // TOP_K
    sizes = jnp.bincount(flat_id, length=N_EXPERTS)
    padded = (sizes + EXPERT_BLOCK - 1) // EXPERT_BLOCK * EXPERT_BLOCK
    start = jnp.cumsum(sizes) - sizes
    padded_end = jnp.cumsum(padded)
    padded_start = padded_end - padded
    dest = padded_start[sorted_id] + jnp.arange(n_assign) - start[sorted_id]
    n_rows = n_assign + N_EXPERTS * EXPERT_BLOCK
    n_blocks = n_rows // EXPERT_BLOCK
    x_pad = jnp.zeros((n_rows, d), xf.dtype).at[dest].set(xf[token_of])
    block_expert = jnp.minimum(
        jnp.searchsorted(padded_end, jnp.arange(n_blocks) * EXPERT_BLOCK, side='right'), N_EXPERTS - 1)

    def expert_block(args):
        xb, e = args
        hid = jax.nn.silu(xb @ w_gate[e]) * (xb @ w_up[e])
        return hid @ w_down[e]

    out_pad = lax.map(expert_block, (x_pad.reshape(n_blocks, EXPERT_BLOCK, d), block_expert)).reshape(n_rows, d)
    out = out_pad[dest] * flat_gate[order][:, None].astype(out_pad.dtype)
    y = jnp.zeros((t, d), out.dtype).at[token_of].add(out)
    return y.reshape(b, s, d).astype(h.dtype)

def second_inputs(seed: int = 0) -> dict:
    key = jax.random.key(seed)
    ks = iter(jax.random.split(key, 40))
    f32 = jnp.float32
    D = D_MODEL

    def nrm(shape, scale):
        return scale * jax.random.normal(next(ks), shape, f32)

    def gain(n):
        return 1.0 + 0.02 * jax.random.normal(next(ks), (DEPTH, n), f32)

    return {
        'x': nrm((BATCH, SEQ, D), 1.0),
        'mem': nrm((BATCH, MEM_LEN, D), 1.0),
        'norm_mix': gain(D),
        'w_in': nrm((DEPTH, D, IN_WIDTH_2), D ** -0.5),
        'da_q_norm': gain(DA_QK_DIM),
        'da_k_norm': gain(DA_QK_DIM),
        'lambda_q1': nrm((DEPTH, DA_QK_DIM), 0.1),
        'lambda_k1': nrm((DEPTH, DA_QK_DIM), 0.1),
        'lambda_q2': nrm((DEPTH, DA_QK_DIM), 0.1),
        'lambda_k2': nrm((DEPTH, DA_QK_DIM), 0.1),
        'da_out_norm': gain(DA_V_DIM),
        'gla_gate_w': nrm((DEPTH, GLA_GATE_RANK, GLA_QK_COLS), GLA_GATE_RANK ** -0.5),
        'gla_gate_b': nrm((DEPTH, GLA_QK_COLS), 0.1),
        'gla_out_norm': gain(GLA_V_DIM),
        'w_o': nrm((DEPTH, MIX_WIDTH_2, D), MIX_WIDTH_2 ** -0.5),
        'norm_cross': gain(D),
        'norm_mem': gain(D),
        'w_cq': nrm((DEPTH, D, D), D ** -0.5),
        'w_ckv': nrm((DEPTH, D, 2 * D), D ** -0.5),
        'cross_q_norm': gain(CROSS_DIM),
        'cross_k_norm': gain(CROSS_DIM),
        'w_co': nrm((DEPTH, D, D), D ** -0.5),
        'norm_ffn': gain(D),
        'w_group': nrm((DEPTH, D, N_GROUPS), D ** -0.5),
        'b_group': nrm((DEPTH, N_GROUPS), 0.01),
        'w_expert': nrm((DEPTH, D, N_EXPERTS), D ** -0.5),
        'b_expert': nrm((DEPTH, N_EXPERTS), 0.01),
        'w_e_gate': nrm((DEPTH, N_EXPERTS, D, D_EXPERT), D ** -0.5),
        'w_e_up': nrm((DEPTH, N_EXPERTS, D, D_EXPERT), D ** -0.5),
        'w_e_down': nrm((DEPTH, N_EXPERTS, D_EXPERT, D), D_EXPERT ** -0.5),
    }

def second_block(x, mem, norm_mix, w_in, da_q_norm, da_k_norm, lambda_q1, lambda_k1, lambda_q2, lambda_k2,
              da_out_norm, gla_gate_w, gla_gate_b, gla_out_norm, w_o, norm_cross, norm_mem, w_cq, w_ckv,
              cross_q_norm, cross_k_norm, w_co, norm_ffn, w_group, b_group, w_expert, b_expert,
              w_e_gate, w_e_up, w_e_down):
    h = x
    for l in range(DEPTH):
        lam_init = 0.8 - 0.6 * math.exp(-0.3 * l)
        h = h + _mixer(h, norm_mix[l], w_in[l], da_q_norm[l], da_k_norm[l], lambda_q1[l], lambda_k1[l],
                       lambda_q2[l], lambda_k2[l], da_out_norm[l], gla_gate_w[l], gla_gate_b[l],
                       gla_out_norm[l], w_o[l], lam_init)
        h = h + _cross_attention(h, mem, norm_cross[l], norm_mem[l], w_cq[l], w_ckv[l],
                                 cross_q_norm[l], cross_k_norm[l], w_co[l])
        h = h + _hier_moe(h, norm_ffn[l], w_group[l], b_group[l], w_expert[l], b_expert[l],
                          w_e_gate[l], w_e_up[l], w_e_down[l])
    return h


def setup_inputs(seed=0):
    out = dict(first_inputs(seed))
    for name, value in second_inputs(seed + 1).items():
        if name != "x":
            out[name + "_2"] = value
    return out


def reference(
    x, c, positions, ln_in_g, ln_in_b, w_ada, b_ada, w_in, mla_q_norm, w_uq, mla_kv_norm, w_ukv,
    ret_gn_g, ret_gn_b, w_out, ln1_g, ln1_b, w_ff1, w_ff2, ln2_g, ln2_b, mem_2, norm_mix_2,
    w_in_2, da_q_norm_2, da_k_norm_2, lambda_q1_2, lambda_k1_2, lambda_q2_2, lambda_k2_2,
    da_out_norm_2, gla_gate_w_2, gla_gate_b_2, gla_out_norm_2, w_o_2, norm_cross_2, norm_mem_2,
    w_cq_2, w_ckv_2, cross_q_norm_2, cross_k_norm_2, w_co_2, norm_ffn_2, w_group_2, b_group_2,
    w_expert_2, b_expert_2, w_e_gate_2, w_e_up_2, w_e_down_2,
):
    x = first_block(
        x, c, positions, ln_in_g, ln_in_b, w_ada, b_ada, w_in, mla_q_norm, w_uq, mla_kv_norm,
        w_ukv, ret_gn_g, ret_gn_b, w_out, ln1_g, ln1_b, w_ff1, w_ff2, ln2_g, ln2_b,
    )
    return second_block(
        x, mem_2, norm_mix_2, w_in_2, da_q_norm_2, da_k_norm_2, lambda_q1_2, lambda_k1_2,
        lambda_q2_2, lambda_k2_2, da_out_norm_2, gla_gate_w_2, gla_gate_b_2, gla_out_norm_2,
        w_o_2, norm_cross_2, norm_mem_2, w_cq_2, w_ckv_2, cross_q_norm_2, cross_k_norm_2,
        w_co_2, norm_ffn_2, w_group_2, b_group_2, w_expert_2, b_expert_2, w_e_gate_2, w_e_up_2,
        w_e_down_2,
    )


_drawn_inputs = setup_inputs


def setup_inputs(seed=0):
    import zlib

    import numpy as np

    out = dict(_drawn_inputs(seed))
    spreads = {}
    factors = {'mla_q_norm': 8.0,
     'w_uq': 3.151,
     'mla_kv_norm': 5.114,
     'ret_gn_g': 4.909,
     'ret_gn_b': 5.673,
     'da_q_norm_2': 3.379,
     'da_k_norm_2': 3.148,
     'da_out_norm_2': 3.391,
     'gla_out_norm_2': 3.862,
     'norm_cross_2': 5.33,
     'norm_mem_2': 7.755,
     'cross_q_norm_2': 6.221,
     'cross_k_norm_2': 8.0,
     'b_group_2': 47.416,
     'b_expert_2': 33.08,
     'norm_ffn_2': 8.0}
    for name, (base, spread) in spreads.items():
        noise = np.random.default_rng([zlib.crc32(name.encode()), seed]).standard_normal(out[name].shape)
        drawn = base * np.exp(spread * noise) if base else spread * noise
        out[name] = __import__('jax').numpy.asarray(drawn.astype(out[name].dtype))
    for name, factor in factors.items():
        out[name] = (out[name] * factor).astype(out[name].dtype)
    return out
```

```python
import math
from contextlib import ExitStack, contextmanager

import numpy as np

import concourse.bass as bass
from concourse import mybir

F32 = mybir.dt.float32
I32 = mybir.dt.int32
U32 = mybir.dt.uint32
ALU = mybir.AluOpType
ACT = mybir.ActivationFunctionType
AX = mybir.AxisListType.X

NEG = -3.0e38
ALPHA = 2.0 ** 0.25
EPS = 1e-5
EPS2 = 1e-6
NBLK = 47
NOVF = 15
SL = 4096

CONSTS = {}


def const_table():
    p = np.arange(128)
    j, i = p[:, None], p[None, :]
    same = (j // 64) == (i // 64)
    lg = np.log(1.0 - 2.0 ** (-5.0 - np.arange(4)))
    past = (same & (j <= i)).astype(np.float64)
    mid = (i // 64) * 64 + 31
    pmid = (same & (j <= mid)).astype(np.float64)
    parts = {
        "ident": np.eye(128),
        "caus": np.where(i <= j, 0.0, NEG),
        "chm": np.where(i // 64 <= j // 64, 0.0, NEG),
        "dec": np.concatenate([np.where(i >= j, np.exp(g * np.maximum(i - j, 0)), 0.0) * 0.125 for g in lg], 1),
        "zet": np.exp(lg[None, :] * (127 - j)) * 0.125,
        "xi": np.exp(lg[None, :] * (j + 1)),
        "gc": np.tile(np.exp(lg * 128)[None, :], (128, 1)),
        "tri": np.concatenate([past, past - pmid, (same & (j > i)).astype(float)], 1) / 16.0,
        "mp": past,
        "mf": (same & (j > i)).astype(float),
        "inv": np.tile(np.concatenate([10000.0 ** (-np.arange(32) / 32), 10000.0 ** (-np.arange(16) / 16)])[None], (128, 1)),
        "su": (j < i).astype(float),
        "one": np.ones((128, 128)),
        "io": np.tile(np.arange(32.0)[None], (128, 1)),
        "tok": j + 128.0 * np.arange(8)[None],
    }
    at = 0
    for k, v in parts.items():
        CONSTS[k] = (at, v.shape[1])
        at += v.shape[1]
    return np.ascontiguousarray(np.concatenate(list(parts.values()), 1).astype(np.float32))


class Queue:

    def __init__(self, eng, sem):
        self.eng, self.sem, self.n, self.seen = eng, sem, 0, {}

    def wait(self, *tokens):
        for t in tokens:
            if t is None:
                continue
            if isinstance(t, list):
                self.wait(*t)
                continue
            sem, v = t
            if v > self.seen.get(id(sem), 0):
                self.eng.wait_ge(sem, v)
                self.seen[id(sem)] = v

    def mark(self, ins):
        ins.then_inc(self.sem, 1)
        self.n += 1
        return (self.sem, self.n)

    @property
    def last(self):
        return (self.sem, self.n) if self.n else None


def program(nc, X, out, cst, scr):
    ctx = ExitStack()
    with ctx:
        def sem(name):
            return ctx.enter_context(nc.semaphore(name))

        BIG = ctx.enter_context(nc.sbuf_tensor("BIG", [128, 11 * SL], F32))
        NC_ = cst.shape[1]
        CT = ctx.enter_context(nc.sbuf_tensor("CT", [128, NC_], F32))
        BC = ctx.enter_context(nc.sbuf_tensor("BC", [128, 4 * 1024], F32))
        ST = ctx.enter_context(nc.sbuf_tensor("ST", [128, 1344], F32))
        PS = ctx.enter_context(nc.psum_tensor("PS", [128, 8, 512], F32))

        P = Queue(nc.tensor, sem("pe"))
        V = Queue(nc.vector, sem("dve"))
        A = Queue(nc.scalar, sem("act"))
        G = Queue(nc.gpsimd, sem("pool"))
        S = Queue(nc.sync, sem("sp"))

        class DmaSem:
            def __init__(self, name):
                self.sem, self.n = sem(name), 0

        dsems = {}

        branch = [""]

        def dma(q, slot, o, i, after=()):
            slot = branch[0] + slot
            if slot not in dsems:
                dsems[slot] = DmaSem("d_" + slot)
            d = dsems[slot]
            if d.n:
                q.wait((d.sem, 16 * d.n))
            q.wait(*after)
            q.eng.dma_start(o, i).then_inc(d.sem, 16)
            d.n += 1
            return (d.sem, 16 * d.n)

        @contextmanager
        def branch_of(cond):
            qs = (P, V, A, G, S)
            kept = [(q.sem, q.n, dict(q.seen)) for q in qs]
            kept_free = (list(bank_free), dict(slot_free))
            branch[0] = "b_"
            with nc.If(cond):
                for q, nm in zip(qs, ("pe_b", "dve_b", "act_b", "pool_b", "sp_b")):
                    q.sem, q.n = sem(nm), 0
                yield
                ends = now() + [(d.sem, 16 * d.n) for nm, d in dsems.items() if nm.startswith("b_")]
                for q in qs:
                    q.wait(*ends)
            for q, (s_, n_, seen) in zip(qs, kept):
                q.sem, q.n, q.seen = s_, n_, seen
            bank_free[:] = kept_free[0]
            slot_free.clear()
            slot_free.update(kept_free[1])
            branch[0] = ""

        def now():
            return [q.last for q in (P, V, A, G)]

        def slot(i, n=1):
            return BIG[:, i * SL:(i + n) * SL]

        def C(name):
            a, n = CONSTS[name]
            return CT[:, a:a + n]

        def v(fn, *a, after=(), **k):
            V.wait(*after)
            return V.mark(fn(*a, **k))

        def a_(fn, *a, after=(), **k):
            A.wait(*after)
            return A.mark(fn(*a, **k))

        def g_(fn, *a, after=(), **k):
            G.wait(*after)
            return G.mark(fn(*a, **k))

        def vc(fn, *a, after=(), **k):
            return v(fn, *a, after=[V.last, *after], **k)

        def ac(fn, *a, after=(), **k):
            return a_(fn, *a, after=[A.last, *after], **k)

        bank_free = [None] * 8

        def mm(bank, o, pairs, after=(), start=True):
            P.wait(bank_free[bank], *after)
            for n, (l, r) in enumerate(pairs):
                ins = nc.tensor.matmul(o, l, r, start=(start and n == 0), stop=(n == len(pairs) - 1),
                                       skip_group_check=True)
            return P.mark(ins)

        def tr(bank, outs_ins, after=()):
            P.wait(bank_free[bank], *after)
            for o, i in outs_ins:
                k = i.shape[0]
                ins = nc.tensor.transpose(o, i, C("ident")[0:k, 0:k])
            return P.mark(ins)

        slot_free = {i: None for i in range(11)}

        def wload(s, src, n=None, off=0, after=()):
            k, n = src.shape[0] // 128, src.shape[1]
            view = BIG[:, s * SL + off:s * SL + off + k * n].rearrange("p (k n) -> p k n", k=k)
            t = dma(S, f"s{s}_{off}", view, src.rearrange("(k p) n -> p k n", p=128), [slot_free[s], *after])
            return view, t

        st_at = [0]
        st_names = {}

        def st(name, n):
            if name not in st_names:
                st_names[name] = (st_at[0], n)
                st_at[0] += n
                assert st_at[0] <= 1344, st_at
            a, m = st_names[name]
            assert m == n
            return ST[:, a:a + n]

        XRES = slot(0, 2).rearrange("p (t d) -> p t d", t=8)
        XT = slot(2, 2).rearrange("p (c n) -> p c n", c=8)
        U = slot(4, 2).rearrange("p (t d) -> p t d", t=8)

        def bc(i):
            return BC[:, i * 1024:(i + 1) * 1024]

        t_cst = dma(A, "cst", CT[:, :], cst)
        cols, col_at, t_cols = {}, 0, []
        ROWS = slot(10)[:, 3072:3200]
        COLS = st("cols", 83)
        x_in = X["x"][0].rearrange("(t p) d -> p t d", p=128)
        t_x = [dma(A, f"x{t}", XRES[:, t, :], x_in[:, t, :]) for t in range(8)]
        for name, src in (("c", X["c"][0]), ("lng", X["ln_in_g"]), ("lnb", X["ln_in_b"]), ("l1g", X["ln1_g"][0]),
                          ("l1b", X["ln1_b"][0]), ("nmix", X["norm_mix_2"][0]), ("ncr", X["norm_cross_2"][0]),
                          ("nmem", X["norm_mem_2"][0]), ("nffn", X["norm_ffn_2"][0]), ("gq", X["mla_q_norm"][0]),
                          ("gkv", X["mla_kv_norm"][0]), ("cqn", X["cross_q_norm_2"][0]),
                          ("ckn", X["cross_k_norm_2"][0]), ("daon", X["da_out_norm_2"][0]),
                          ("glon", X["gla_out_norm_2"][0])):
            k = src.shape[0] // 128
            t_cols.append(dma(S, "col_" + name, ROWS[col_at:col_at + k, :], src.rearrange("(k p) -> k p", p=128)))
            cols[name] = COLS[:, col_at:col_at + k]
            col_at += k
        for name, src in (("daq", "da_q_norm_2"), ("dak", "da_k_norm_2")):
            for h in range(2):
                t_cols.append(dma(S, f"col_{name}{h}", ROWS[col_at:col_at + 1, 64 * h:64 * h + 64],
                                  X[src][0].rearrange("(k p) -> k p", k=1)))
            cols[name] = COLS[:, col_at:col_at + 1]
            col_at += 1
        POSI = slot(10)[0:8, 3200:3328].bitcast(I32)
        POSR = slot(10)[0:8, 3328:3456]
        t_pos = dma(S, "pos", POSI, X["positions"][0].rearrange("(t p) -> t p", p=128))
        lam4 = BC[:, 2048:2048 + 256].rearrange("p (a n) -> p a n", a=4)
        t_lam = [dma(G, f"lam{n}", lam4[:, n, :], X[s][0].partition_broadcast(128))
                 for n, s in enumerate(("lambda_q1_2", "lambda_k1_2", "lambda_q2_2", "lambda_k2_2"))]
        posf = st("posf", 8)
        P.wait(t_cst, *t_cols)
        nc.tensor.transpose(PS[:, 7, 0:83], ROWS[0:83, :], C("ident")[0:83, 0:83])
        r = v(nc.vector.tensor_copy, POSR, POSI, after=[t_pos])
        p_ = tr(7, [(PS[:, 7, 128:136], POSR)], after=[r])
        v(nc.vector.tensor_copy, COLS, PS[:, 7, 0:83], after=[p_])
        bank_free[7] = v(nc.vector.tensor_copy, posf, PS[:, 7, 128:136])
        V.wait(t_cst, *t_lam, V.last)
        A.wait(t_cst, V.last)

        lamp = BC[:, 3072:3072 + 128].rearrange("p (a n) -> p a n", a=2)
        ls = st("ls", 2)
        v(nc.vector.tensor_tensor, lamp, lam4[:, 0:4:2, :], lam4[:, 1:4:2, :], ALU.mult)
        vc(nc.vector.tensor_reduce, ls, lamp, AX, ALU.add)
        le = st("le", 2)
        a_(nc.scalar.activation, le, ls, ACT.Exp, after=[V.last])
        nlam = st("nlam", 1)
        v(nc.vector.tensor_scalar, nlam, le[:, 1:2], le[:, 0:1], -0.2, ALU.subtract, ALU.add, after=[A.last])

        ce, cs = st("ce", 8), st("cs", 8)
        a_(nc.scalar.activation, ce, cols["c"], ACT.Exp, scale=-1.0)
        v(nc.vector.tensor_scalar, ce, ce, 1.0, None, ALU.add, after=[A.last])
        vc(nc.vector.reciprocal, ce, ce)
        vc(nc.vector.tensor_tensor, cs, ce, cols["c"], ALU.mult)
        CB = slot(10)[:, 0:1024].rearrange("p (k n) -> p k n", k=8)
        t_cb = vc(nc.vector.tensor_copy, CB, cs.unsqueeze(2).to_broadcast([128, 8, 128]))

        RA = slot(9)[:, 0:384].rearrange("p (t n) -> p t n", t=8)
        RK = slot(9)[:, 384:768].rearrange("p (t n) -> p t n", t=8)
        CSN = ctx.enter_context(nc.sbuf_tensor("CSN", [128, 768], F32))
        COS = CSN[:, 0:384].rearrange("p (t n) -> p t n", t=8)
        SIN = CSN[:, 384:768].rearrange("p (t n) -> p t n", t=8)
        V.wait(V.last)
        for t in range(8):
            v(nc.vector.tensor_scalar, RA[:, t, :], C("inv"), posf[:, t:t + 1], None, ALU.mult)
        MAGIC = 12582912.0
        vc(nc.vector.tensor_scalar, RK, RA, 1.0 / (2 * math.pi), MAGIC, ALU.mult, ALU.add)
        vc(nc.vector.tensor_scalar, RK, RK, MAGIC, None, ALU.subtract)
        C1 = 6.28125
        C2 = float(np.float32(np.floor((2 * math.pi - C1) * 2 ** 20) / 2 ** 20))
        C3 = float(np.float32(2 * math.pi - C1 - C2))
        for c in (C1, C2, C3):
            vc(nc.vector.scalar_tensor_tensor, out=RA, in0=RK, scalar=-c, in1=RA, op0=ALU.mult, op1=ALU.add)
        PI = float(np.float32(3.1415925))
        vc(nc.vector.tensor_scalar, RA, RA, PI, -PI, ALU.min, ALU.max)
        t_ra = V.last
        a_(nc.scalar.activation, SIN[:, :, :], RA, ACT.Sin, after=[t_ra])
        vc(nc.vector.scalar_tensor_tensor, out=RK, in0=RA, scalar=-1.0, in1=RA, op0=ALU.mult, op1=ALU.max)
        vc(nc.vector.tensor_scalar, RK, RK, -1.0, math.pi / 2, ALU.mult, ALU.add)
        t_cos = a_(nc.scalar.activation, COS[:, :, :], RK, ACT.Sin, after=[V.last])
        COSR, SINR = COS[:, :, 0:32], SIN[:, :, 0:32]
        COSM, SINM = COS[:, :, 32:48], SIN[:, :, 32:48]

        def rsqrt(o, x, scale, eps, after=()):
            t = v(nc.vector.tensor_scalar, o, x, scale, eps, ALU.mult, ALU.add, after=after)
            t = a_(nc.scalar.activation, o, o, ACT.Sqrt, after=[t])
            return v(nc.vector.reciprocal, o, o, after=[t])

        bst = st("bst", 12).rearrange("p (a n) -> p a n", a=2)
        mv = st("mv", 16).rearrange("p (t n) -> p t n", t=8)
        rst = st("rst", 8)

        def layer_norm_z(ready):
            for t in range(8):
                for h in range(2):
                    v(nc.vector.bn_stats, bst[:, h, :], XRES[:, t, 512 * h:512 * h + 512],
                      after=[ready[t], V.last])
                vc(nc.vector.bn_aggr, mv[:, t, :], bst)
            r = rsqrt(rst, mv[:, :, 1], 1.0, EPS, [V.last])
            return [v(nc.vector.tensor_scalar, XRES[:, t, :], XRES[:, t, :], mv[:, t, 0:1], rst[:, t:t + 1],
                      ALU.subtract, ALU.mult, after=[r]) for t in range(8)]

        def to_fm(src, scales, biases, ready, banks=(0, 1, 2, 3)):
            toks, ptoks, n = [], [], 0
            for th in range(2):
                for c in range(8):
                    b = banks[n % len(banks)]
                    t = tr(b, [(PS[:, b, 128 * u:128 * u + 128], src(4 * th + u, c)) for u in range(4)],
                           after=[ready[4 * th + u] for u in range(4)])
                    ptoks.append(t)
                    o = XT[:, c, 512 * th:512 * th + 512]
                    if n % 2 == 0:
                        kw = {"scale": scales(c)}
                        if biases:
                            kw["bias"] = biases(c)
                        r = a_(nc.scalar.activation, o, PS[:, b, :], ACT.Identity, after=[t], **kw)
                    elif biases:
                        r = v(nc.vector.tensor_scalar, o, PS[:, b, :], scales(c), biases(c), ALU.mult, ALU.add,
                              after=[t])
                    else:
                        r = v(nc.vector.tensor_scalar, o, PS[:, b, :], scales(c), None, ALU.mult, after=[t])
                    bank_free[b] = r
                    toks.append(r)
                    n += 1
            return toks, ptoks

        MODT = st("modt", 32)
        GT1, GT2 = bc(0), bc(1)
        w_ada, b_ada = X["w_ada"][0], X["b_ada"][0]
        BADA = slot(10)[:, 1024:1024 + 1024].rearrange("p (b n) -> p b n", b=2)
        MROW = slot(10)[:, 2048:2048 + 1024].rearrange("p (b n) -> p b n", b=2)
        mrow_free = [None, None]
        bada_free = [None, None]
        for n, ch in enumerate([0, 1, 2, 3, 4, 5, 6, 7, 8, 9, 10, 11]):
            sl = 6 + n % 3
            w, tw = wload(sl, w_ada[:, 512 * ch:512 * ch + 512])
            tb = dma(A, f"bada{n % 2}", BADA[:, n % 2, :], b_ada[512 * ch:512 * ch + 512].partition_broadcast(128),
                     after=[bada_free[n % 2]])
            b = 4 + n % 2
            t = mm(b, PS[:, b, :], [(CB[:, k, :], w[:, k, :]) for k in range(8)], after=[tw, t_cb])
            slot_free[sl] = t
            vec, half = ch // 2, ch % 2
            if vec in (2, 5):
                o = (GT1 if vec == 2 else GT2)[:, 512 * half:512 * half + 512]
                r = v(nc.vector.tensor_tensor, o, PS[:, b, :], BADA[:, n % 2, :], ALU.add, after=[t, tb])
                bank_free[b] = bada_free[n % 2] = r
            else:
                o = MROW[:, n % 2, :]
                r = v(nc.vector.tensor_tensor, o, PS[:, b, :], BADA[:, n % 2, :], ALU.add,
                      after=[t, tb, mrow_free[n % 2]])
                bank_free[b] = bada_free[n % 2] = r
                t = tr(6, [(PS[:, 6, 128 * u:128 * u + 128], o[:, 128 * u:128 * u + 128]) for u in range(4)], after=[r])
                mrow_free[n % 2] = t
                at = 8 * {0: 0, 1: 1, 3: 2, 4: 3}[vec] + 4 * half
                bank_free[6] = v(nc.vector.tensor_copy, MODT[:, at:at + 4], PS[:, 6, 0:512:128], after=[t])

        def mod_cols(tag, g, b, sh, sc):
            A1, B1 = st("A" + tag, 8), st("B" + tag, 8)
            one_sc = st("osc" + tag, 8)
            vc(nc.vector.tensor_scalar, one_sc, sc, 1.0, None, ALU.add)
            vc(nc.vector.tensor_tensor, A1, g, one_sc, ALU.mult)
            vc(nc.vector.tensor_tensor, B1, b, one_sc, ALU.mult)
            vc(nc.vector.tensor_tensor, B1, B1, sh, ALU.add)
            return A1, B1

        A1, B1 = mod_cols("1", cols["lng"], cols["lnb"], MODT[:, 0:8], MODT[:, 8:16])
        A2, B2 = mod_cols("2", cols["l1g"], cols["l1b"], MODT[:, 16:24], MODT[:, 24:32])

        z = layer_norm_z(t_x)
        t_bc2 = dma(G, "bc2", bc(2), X["ln_in_g"].partition_broadcast(128), after=now())
        t_bc3 = dma(G, "bc3", bc(3), X["ln_in_b"].partition_broadcast(128), after=now())
        xt1, xt1p = to_fm(lambda t, c: XRES[:, t, 128 * c:128 * c + 128], lambda c: A1[:, c:c + 1],
                          lambda c: B1[:, c:c + 1], z + [])

        def affine_pool(ready, gb, gbt, bb, bbt):
            toks = []
            G.wait(*ready)
            for t in range(8):
                r = g_(nc.gpsimd.tensor_tensor, XRES[:, t, :], XRES[:, t, :], gb, ALU.mult, after=[gbt])
                toks.append(g_(nc.gpsimd.tensor_tensor, XRES[:, t, :], XRES[:, t, :], bb, ALU.add, after=[r, bbt]))
            return toks

        x0 = affine_pool(xt1p, bc(2), t_bc2, bc(3), t_bc3)

        w_in = X["w_in"][0]
        LAT = slot(10)[:, 0:8 * 416].rearrange("p (t n) -> p t n", t=8)
        V.wait(*now())
        A.wait(*now())
        w, tw = wload(6, w_in[:, 0:416])
        lss = st("lss", 16).rearrange("p (t n) -> p t n", t=8)
        TMP = slot(9)[:, 0:2048]
        for t in range(8):
            b = t % 4
            tk = mm(b, PS[:, b, 0:416], [(XT[:, k, 128 * t:128 * t + 128], w[:, k, :]) for k in range(8)],
                    after=[tw, xt1])
            a_(nc.scalar.activation, TMP[:, 0:256], PS[:, b, 0:256], ACT.Square, accum_out=lss[:, t, 0:1],
               after=[tk, A.last])
            r1 = ac(nc.scalar.activation, TMP[:, 0:128], PS[:, b, 256:384], ACT.Square, accum_out=lss[:, t, 1:2])
            r2 = v(nc.vector.tensor_copy, LAT[:, t, :], PS[:, b, 0:416], after=[tk, r1])
            bank_free[b] = r2
        slot_free[6] = P.last
        lr = st("lr", 16).rearrange("p (t n) -> p t n", t=8)
        v(nc.vector.tensor_scalar, lr[:, :, 0], lss[:, :, 0], 1.0 / 256, EPS, ALU.mult, ALU.add, after=[A.last])
        v(nc.vector.tensor_scalar, lr[:, :, 1], lss[:, :, 1], 1.0 / 128, EPS, ALU.mult, ALU.add)
        a_(nc.scalar.activation, lr, lr, ACT.Sqrt, after=[V.last])
        v(nc.vector.reciprocal, lr, lr, after=[A.last])
        V.wait(V.last)
        for t in range(8):
            v(nc.vector.tensor_scalar, LAT[:, t, 0:256], LAT[:, t, 0:256], lr[:, t, 0:1], None, ALU.mult)
            v(nc.vector.tensor_scalar, LAT[:, t, 256:384], LAT[:, t, 256:384], lr[:, t, 1:2], None, ALU.mult)
        t_latn = V.last
        KR = st("kr", 256).rearrange("p (t n) -> p t n", t=8)
        T1 = TMP[:, 256:384].rearrange("p (t n) -> p t n", t=8)
        T2 = TMP[:, 384:512].rearrange("p (t n) -> p t n", t=8)
        V.wait(t_cos)

        def rotate(o1, o2, x1, x2, co, si, t1, t2, after=()):
            v(nc.vector.tensor_tensor, t1, x1, co, ALU.mult, after=[V.last, *after])
            v(nc.vector.tensor_tensor, t2, x2, si, ALU.mult)
            vc(nc.vector.tensor_tensor, o1, t1, t2, ALU.subtract)
            v(nc.vector.tensor_tensor, t1, x2, co, ALU.mult, after=[V.last])
            v(nc.vector.tensor_tensor, t2, x1, si, ALU.mult)
            return vc(nc.vector.tensor_tensor, o2, t1, t2, ALU.add)

        t_kr = rotate(KR[:, :, 0:16], KR[:, :, 16:32], LAT[:, :, 384:400], LAT[:, :, 400:416], COSM, SINM, T1, T2)

        wqk, tqk = wload(7, w_in[:, 416:928])
        wv, twv = wload(8, w_in[:, 928:1440])
        wg, twg = wload(6, w_in[:, 1440:1952])
        SG = slot(4).rearrange("p (t n) -> p t n", t=8)
        RO = slot(5).rearrange("p (t n) -> p t n", t=8)
        R = slot(9)
        QK, RQK = R[:, 0:512], R[:, 512:1024]
        TA, TB = R[:, 1024:1280], R[:, 1280:1536]
        QKT = R[0:64, 1536:2560]
        SC = R[:, 2560:3072]
        KZ = R[:, 3072:3328]
        STA = R[0:64, 3328:3840]
        VT = slot(10)[:, 3328:3840]
        V.wait(V.last)
        v(nc.vector.memset, STA, 0.0)
        mvr = st("mvr", 64).rearrange("p (t n) -> p t n", t=8)
        bs4 = st("bs4", 24).rearrange("p (h n) -> p h n", h=4)
        st_free = [None]

        def b4(ap, n, parts=128):
            return ap.unsqueeze(2).to_broadcast([parts, ap.shape[1], n])

        def silu_into(o, ps, after):
            t = a_(nc.scalar.activation, o, ps, ACT.Exp, scale=-1.0, after=after)
            t = v(nc.vector.tensor_scalar, o, o, 1.0, None, ALU.add, after=[t])
            t = v(nc.vector.reciprocal, o, o, after=[t])
            return v(nc.vector.tensor_tensor, o, o, ps, ALU.mult, after=[t])

        t_inner = t_kvm = None
        for t in range(8):
            xt = [XT[:, k, 128 * t:128 * t + 128] for k in range(8)]
            p0 = mm(0, PS[:, 0, :], [(xt[k], wqk[:, k, :]) for k in range(8)], after=[tqk])
            p1 = mm(1, PS[:, 1, :], [(xt[k], wv[:, k, :]) for k in range(8)], after=[twv])
            p2 = mm(2, PS[:, 2, :], [(xt[k], wg[:, k, :]) for k in range(8)], after=[twg])
            bank_free[0] = a_(nc.scalar.copy, QK, PS[:, 0, :], after=[p0, V.last])
            tqk_ = bank_free[0]
            tv = bank_free[1] = a_(nc.scalar.copy, VT, PS[:, 1, :], after=[p1, t_inner, t_kvm])
            q3 = QK.rearrange("p (h n) -> p h n", h=8)
            r3 = RQK.rearrange("p (h n) -> p h n", h=8)
            co = COSR[:, t, :].unsqueeze(1).to_broadcast([128, 8, 32])
            si = SINR[:, t, :].unsqueeze(1).to_broadcast([128, 8, 32])
            ta = TA.rearrange("p (h n) -> p h n", h=8)
            tb = TB.rearrange("p (h n) -> p h n", h=8)
            tr_ = rotate(r3[:, :, 0:32], r3[:, :, 32:64], q3[:, :, 0:32], q3[:, :, 32:64], co, si, ta, tb,
                         after=[tqk_, P.last])
            pq = tr(3, [(PS[0:64, 3, 128 * h:128 * h + 128], RQK[:, 64 * h:64 * h + 64]) for h in range(4)], [tr_])
            pk = tr(4, [(PS[0:64, 4, 128 * h:128 * h + 128], RQK[:, 256 + 64 * h:320 + 64 * h]) for h in range(4)])
            bank_free[3] = eq = a_(nc.scalar.copy, QKT[:, 0:512], PS[0:64, 3, :], after=[pq])
            bank_free[4] = ek = a_(nc.scalar.copy, QKT[:, 512:1024], PS[0:64, 4, :], after=[pk])
            tkz = v(nc.vector.tensor_tensor, KZ.rearrange("p (h n) -> p h n", h=4),
                    RQK[:, 256:512].rearrange("p (h n) -> p h n", h=4), b4(C("zet"), 64), ALU.mult, after=[t_kvm, tr_])
            for h in range(4):
                ps_ = mm(5, PS[:, 5, 128 * h:128 * h + 128],
                         [(QKT[:, 512 + 128 * h:640 + 128 * h], QKT[:, 128 * h:128 * h + 128])], after=[eq, ek])
            for h in range(4):
                pc = mm(6, PS[:, 6, 128 * h:128 * h + 128],
                        [(QKT[:, 128 * h:128 * h + 128], STA[:, 128 * h:128 * h + 128])], after=[st_free[0], V.last])
            tsc = bank_free[5] = v(nc.vector.tensor_tensor, SC, PS[:, 5, :], C("dec"), ALU.mult, after=[ps_])
            for h in range(4):
                t_kvm = mm(3, PS[0:64, 3, 128 * h:128 * h + 128],
                           [(KZ[:, 64 * h:64 * h + 64], VT[:, 128 * h:128 * h + 128])], after=[tkz, tv])
            for h in range(4):
                t_inner = mm(7, PS[:, 7, 128 * h:128 * h + 128],
                             [(SC[:, 128 * h:128 * h + 128], VT[:, 128 * h:128 * h + 128])], after=[tsc])
            s4 = STA.rearrange("p (h n) -> p h n", h=4)
            v(nc.vector.tensor_tensor, s4, s4, b4(C("gc")[0:64, :], 128, 64), ALU.mult, after=[pc, V.last])
            st_free[0] = bank_free[3] = vc(nc.vector.tensor_tensor, STA, STA, PS[0:64, 3, :], ALU.add, after=[t_kvm])
            o3 = RO[:, t, :].rearrange("p (h n) -> p h n", h=4)
            bank_free[6] = v(nc.vector.tensor_tensor, o3, PS[:, 6, :].rearrange("p (h n) -> p h n", h=4),
                             b4(C("xi"), 128), ALU.mult, after=[pc])
            bank_free[7] = vc(nc.vector.tensor_tensor, RO[:, t, :], RO[:, t, :], PS[:, 7, :], ALU.add,
                              after=[t_inner])
            V.wait(V.last)
            for h in range(4):
                v(nc.vector.bn_stats, bs4[:, h, :], o3[:, h, :])
            V.wait(V.last)
            for h in range(4):
                v(nc.vector.bn_aggr, mvr[:, t, 2 * h:2 * h + 2], bs4[:, h, :])
            bank_free[2] = silu_into(SG[:, t, :], PS[:, 2, :], [p2])
        slot_free[6] = slot_free[7] = slot_free[8] = P.last
        t_xt_free = P.last
        rsr = st("rsr", 32)
        mvr2 = mvr.rearrange("p t (h n) -> p (t h) n", n=2)
        tr_ = rsqrt(rsr, mvr2[:, :, 1], 1.0, EPS, [V.last])
        G.wait(*x0)
        t_gn = [dma(G, "bc2", bc(2)[:, 0:512], X["ret_gn_g"][0].partition_broadcast(128), after=x0),
                dma(G, "gnb", bc(2)[:, 512:1024], X["ret_gn_b"][0].partition_broadcast(128), after=x0)]
        for t in range(8):
            o3 = RO[:, t, :].rearrange("p (h n) -> p h n", h=4)
            m = mvr2[:, 4 * t:4 * t + 4, 0]
            vc(nc.vector.tensor_tensor, o3, o3, b4(m, 128), ALU.subtract)
            vc(nc.vector.tensor_tensor, o3, o3, b4(rsr[:, 4 * t:4 * t + 4], 128), ALU.mult)
            vc(nc.vector.tensor_tensor, RO[:, t, :], RO[:, t, :], bc(2)[:, 0:512], ALU.mult, after=t_gn)
            vc(nc.vector.tensor_tensor, RO[:, t, :], RO[:, t, :], bc(2)[:, 512:1024], ALU.add)
            vc(nc.vector.tensor_tensor, RO[:, t, :], RO[:, t, :], SG[:, t, :], ALU.mult)
        t_ro = V.last

        QNT = slot(9)[:, 0:2048].rearrange("p (c n) -> p c n", c=2)
        VA = slot(9)[:, 2048:4096].rearrange("p (t n) -> p t n", t=8)
        KVT = bc(3)
        QT = slot(2).rearrange("p (h n) -> p h n", h=4)
        KT = slot(3).rearrange("p (h n) -> p h n", h=4)
        A.wait(*now())
        V.wait(*now())
        n = 0
        lat_t = []
        for c in range(3):
            for th in range(2):
                b = n % 2
                t = tr(b, [(PS[:, b, 128 * u:128 * u + 128], LAT[:, 4 * th + u, 128 * c:128 * c + 128])
                           for u in range(4)], after=[t_latn])
                o = (QNT[:, c, :] if c < 2 else KVT)[:, 512 * th:512 * th + 512]
                sc = cols["gq"][:, c:c + 1] if c < 2 else cols["gkv"][:, 0:1]
                bank_free[b] = a_(nc.scalar.activation, o, PS[:, b, :], ACT.Copy, scale=sc, after=[t])
                lat_t.append(A.last)
                n += 1
        wu = BIG[:, 6 * SL:6 * SL + 1536].rearrange("p (k n) -> p k n", k=2)
        twu = dma(S, "s6_0", wu, X["w_uq"][0].rearrange("(k p) n -> p k n", p=128), [slot_free[6]])
        wk = BIG[:, 6 * SL + 1536:6 * SL + 2560]
        twk = dma(S, "s6_b", wk, X["w_ukv"][0], [slot_free[6]])
        QTM = slot(10)[:, 0:384].rearrange("p (h n) -> p h n", h=4)
        KTM = slot(10)[:, 384:768].rearrange("p (h n) -> p h n", h=4)
        MT1 = slot(10)[:, 768:832].rearrange("p (h n) -> p h n", h=4)
        MT2 = slot(10)[:, 832:896].rearrange("p (h n) -> p h n", h=4)
        PB = [slot(10)[:, 0:1024], slot(10)[:, 1024:2048]]
        PTB = [slot(10)[:, 2048:3072], slot(10)[:, 3072:4096]]
        AO = slot(4).rearrange("p (t n) -> p t n", t=8)

        sm = st("sm", 32)

        def attention(items, qk, mask, scale, PBUF, PTBUF, vsrc, ov, out_fn, nmap=1, combine=None):
            p_free = [[None] * nmap, [None] * nmap]
            pt_free = [None, None]
            S_t, P_t, T_t = {}, {}, {}
            sm_n = [0]
            for n in range(len(items) + 2):
                if n < len(items):
                    h, i = items[n]
                    nk = 128 * (i + 1)
                    P_t[n] = []
                    for m in range(nmap):
                        sb = 2 * (n % 2) if nmap == 1 else 2 * m
                        tq = None
                        for c0 in range(0, nk, 512):
                            c1 = min(nk, c0 + 512)
                            b = sb + c0 // 512
                            tq = mm(b, PS[:, b, 0:c1 - c0], [qk(h, i, m, c0, c1)])
                        flat = PS[:, sb:sb + 2, :].rearrange("p b n -> p (b n)")
                        d = flat[:, nk - 128:nk]
                        t = v(nc.vector.tensor_tensor, d, d, mask, ALU.add, after=[tq])
                        k = 4 * (sm_n[0] % 8)
                        sm_n[0] += 1
                        mx, bi, rs, ri = (sm[:, k + z:k + z + 1] for z in range(4))
                        vc(nc.vector.tensor_reduce, mx, flat[:, 0:nk], AX, ALU.max)
                        t = vc(nc.vector.tensor_scalar, bi, mx, -scale, None, ALU.mult)
                        pb = PBUF[n % 2][m]
                        t = a_(nc.scalar.activation, pb[:, 0:nk], flat[:, 0:nk], ACT.Exp, bias=bi, scale=scale,
                               accum_out=rs, after=[t, p_free[n % 2][m]])
                        bank_free[sb] = bank_free[sb + 1] = t
                        t = v(nc.vector.reciprocal, ri, rs, after=[t])
                        P_t[n].append((t, ri))
                    if combine:
                        src, t = combine(n, nk, P_t[n])
                    else:
                        src, t = PBUF[n % 2][0], P_t[n][0][0]
                    S_t[n] = (src, t)
                if 1 <= n <= len(items):
                    k = n - 1
                    h, i = items[k]
                    src, ts = S_t[k]
                    T_t[k] = []
                    for g0 in range(0, i + 1, 4):
                        g1 = min(i + 1, g0 + 4)
                        b = 4 + (g0 // 4)
                        t = tr(b, [(PS[:, b, 128 * (j - g0):128 * (j - g0) + 128], src[:, 128 * j:128 * j + 128])
                                   for j in range(g0, g1)], after=[ts])
                        o = PTBUF[k % 2][:, 128 * g0:128 * g1]
                        w_ = 128 * (g1 - g0)
                        if g0 == 0:
                            r = a_(nc.scalar.copy, o, PS[:, b, 0:w_], after=[t, pt_free[k % 2]])
                        else:
                            r = v(nc.vector.tensor_copy, o, PS[:, b, 0:w_], after=[t, pt_free[k % 2]])
                        bank_free[b] = r
                        T_t[k].append(r)
                    for m in range(nmap):
                        p_free[k % 2][m] = P.last
                    if combine:
                        combine.free[k % 2] = P.last
                if n >= 2:
                    k = n - 2
                    h, i = items[k]
                    b = 6 + k % 2
                    t = mm(b, PS[:, b, 0:ov], [(PTBUF[k % 2][:, 128 * j:128 * j + 128], vsrc(h, j))
                                               for j in range(i + 1)], after=[T_t[k]])
                    pt_free[k % 2] = t
                    bank_free[b] = out_fn(h, i, PS[:, b, 0:ov], t, P_t[k])

        for g in range(2):
            A.wait(*now())
            V.wait(*now())
            tm_free = None
            for t in range(8):
                pq = mm(0, PS[:, 0, 0:384], [(QNT[:, k, 128 * t:128 * t + 128], wu[:, k, 384 * g:384 * g + 384])
                                            for k in range(2)], after=[twu, lat_t])
                pk = mm(1, PS[:, 1, :], [(KVT[:, 128 * t:128 * t + 128], wk[:, 512 * g:512 * g + 512])], after=[twk])
                q3 = PS[:, 0, 0:384].rearrange("p (h n) -> p h n", h=4)
                k3 = PS[:, 1, :].rearrange("p (h n) -> p h n", h=4)
                a_(nc.scalar.copy, QTM[:, :, 0:64], q3[:, :, 0:64], after=[pq, tm_free])
                a_(nc.scalar.copy, KTM[:, :, 0:64], k3[:, :, 0:64], after=[pk])
                a_(nc.scalar.copy, KTM[:, :, 64:96], KR[:, t, :].unsqueeze(1).to_broadcast([128, 4, 32]), after=[t_kr])
                bank_free[1] = a_(nc.scalar.copy, VA[:, t, :].rearrange("p (h n) -> p h n", h=4),
                                        k3[:, :, 64:128])
                co = COSM[:, t, :].unsqueeze(1).to_broadcast([128, 4, 16])
                si = SINM[:, t, :].unsqueeze(1).to_broadcast([128, 4, 16])
                r = rotate(QTM[:, :, 64:80], QTM[:, :, 80:96], q3[:, :, 64:80], q3[:, :, 80:96], co, si, MT1, MT2,
                           after=[pq, A.last, tm_free])
                bank_free[0] = r
                p1 = tr(2, [(PS[0:96, 2, 128 * h:128 * h + 128], QTM[:, h, :]) for h in range(4)], after=[r, A.last])
                p2 = tr(3, [(PS[0:96, 3, 128 * h:128 * h + 128], KTM[:, h, :]) for h in range(4)])
                tm_free = p2
                bank_free[2] = a_(nc.scalar.copy, QT[0:96, :, 128 * t:128 * t + 128],
                                  PS[0:96, 2, :].rearrange("p (h n) -> p h n", h=4), after=[p1])
                bank_free[3] = v(nc.vector.tensor_copy, KT[0:96, :, 128 * t:128 * t + 128],
                                 PS[0:96, 3, :].rearrange("p (h n) -> p h n", h=4), after=[p2])
            A.wait(*now())
            V.wait(*now())
            P.wait(*now())

            def mla_qk(h, i, m, c0, c1):
                return (QT[0:96, h, 128 * i:128 * i + 128], KT[0:96, h, c0:c1])

            def mla_out(h, i, o, t, pt):
                o = o[:, 64 * (h % 2):64 * (h % 2) + 64]
                return v(nc.vector.tensor_scalar, AO[:, i, 256 * g + 64 * h:256 * g + 64 * h + 64], o, pt[0][1], None,
                         ALU.mult, after=[t, pt[0][0]])

            attention([(h, i) for h in range(4) for i in range(8)], mla_qk, C("caus"), 96.0 ** -0.5,
                      [[PB[0]], [PB[1]]], PTB, lambda h, j: VA[:, j, 128 * (h // 2):128 * (h // 2) + 128], 128, mla_out)
        slot_free[6] = P.last

        def project(wd, src_t, evac, ready, slots=(6, 7, 8), banks=(4, 5, 6, 7)):
            n_ = 0
            last = {}
            for n in range(wd.shape[1] // 512):
                s = slots[n % len(slots)]
                w, tw = wload(s, wd[:, 512 * n:512 * n + 512])
                for t in range(8):
                    b = banks[n_ % len(banks)]
                    n_ += 1
                    tk = mm(b, PS[:, b, :], [(src_t(k, t), w[:, k, :]) for k in range(8)], after=[tw, ready])
                    last[t] = bank_free[b] = evac(t, n, PS[:, b, :], tk)
                slot_free[s] = P.last
            return [last[t] for t in range(8)]

        A.wait(*now())
        V.wait(*now())
        MIX = [slot(4).rearrange("p (t n) -> p t n", t=8), slot(5).rearrange("p (t n) -> p t n", t=8)]
        one1 = C("one")[:, 0:1]
        mt, _ = to_fm(lambda t, c: MIX[c // 4][:, t, 128 * (c % 4):128 * (c % 4) + 128], lambda c: one1, None,
                      [now()] * 8)
        PT_ = [slot(10)[:, 512 * i:512 * i + 512] for i in range(4)]

        def residual(gt, alpha, ready):
            k = [0]

            def f(t, n, ps, tk):
                x = XRES[:, t, 512 * n:512 * n + 512]
                o = PT_[k[0] % 4]
                k[0] += 1
                r = v(nc.vector.tensor_tensor, o, ps, gt[:, 512 * n:512 * n + 512], ALU.mult, after=[tk, ready])
                if alpha is None:
                    vc(nc.vector.tensor_tensor, x, x, o, ALU.add)
                else:
                    vc(nc.vector.scalar_tensor_tensor, out=x, in0=x, scalar=alpha, in1=o, op0=ALU.mult, op1=ALU.add)
                return V.last
            return f

        xr = project(X["w_out"][0], lambda k, t: XT[:, k, 128 * t:128 * t + 128], residual(GT1, ALPHA, x0), mt)
        z = layer_norm_z(xr)
        t_bc2 = dma(G, "bc2", bc(2), X["ln1_g"][0].partition_broadcast(128), after=now())
        t_bc3 = dma(G, "bc3", bc(3), X["ln1_b"][0].partition_broadcast(128), after=now())
        A.wait(P.last)
        V.wait(P.last)
        xt2, xt2p = to_fm(lambda t, c: XRES[:, t, 128 * c:128 * c + 128], lambda c: A2[:, c:c + 1],
                          lambda c: B2[:, c:c + 1], z)
        x1 = affine_pool(xt2p, bc(2), t_bc2, bc(3), t_bc3)

        HT = slot(4, 2).rearrange("p (c n) -> p c n", c=8)
        w1, w2 = X["w_ff1"][0], X["w_ff2"][0]
        ZT = slot(10)[:, 2048:3072]
        g_(nc.gpsimd.memset, ZT, 0.0, after=now())
        t_zy = dma(G, "zy", scr[2][32 * 128:, :].rearrange("(b p) d -> p b d", p=128),
                   ZT.unsqueeze(1).to_broadcast([128, NOVF, 1024]), after=[G.last])
        ring = [6, 7, 8, 9]
        rn = 0
        V.wait(*now())
        for g in range(4):
            h_t = []
            for cc in range(2):
                s = ring[rn % 4]
                rn += 1
                w, tw = wload(s, w1[:, 1024 * g + 512 * cc:1024 * g + 512 * cc + 512])
                for fb in range(4):
                    for th in range(2):
                        b = (fb * 2 + th) % 4
                        tk = mm(b, PS[:, b, :], [(w[:, k, 128 * fb:128 * fb + 128], XT[:, k, 512 * th:512 * th + 512])
                                                for k in range(8)], after=[tw, xt2])
                        o = HT[:, 4 * cc + fb, 512 * th:512 * th + 512]
                        r = a_(nc.scalar.activation, o, PS[:, b, :], ACT.Relu, after=[tk])
                        bank_free[b] = r
                        r = g_(nc.gpsimd.tensor_tensor, o, o, o, ALU.mult, after=[r])
                        h_t.append(r)
                slot_free[s] = P.last
            A.wait(*now())
            for n in range(2):
                s = ring[rn % 4]
                rn += 1
                w, tw = wload(s, w2[1024 * g:1024 * g + 1024, 512 * n:512 * n + 512])
                ev = residual(GT2, ALPHA if g == 0 else None, x1)
                for t in range(8):
                    b = 4 + t % 4
                    tk = mm(b, PS[:, b, :], [(HT[:, k, 128 * t:128 * t + 128], w[:, k, :]) for k in range(8)],
                            after=[tw, h_t])
                    bank_free[b] = ev(t, n, PS[:, b, :], tk)
                slot_free[s] = P.last
            A.wait(P.last)
        z = layer_norm_z([V.last] * 8)
        t_bc2 = dma(G, "bc2", bc(2), X["ln2_g"][0].partition_broadcast(128), after=now())
        t_bc3 = dma(G, "bc3", bc(3), X["ln2_b"][0].partition_broadcast(128), after=now())
        x2 = []
        for t in range(8):
            v(nc.vector.tensor_tensor, XRES[:, t, :], XRES[:, t, :], bc(2), ALU.mult, after=[z[t], t_bc2])
            x2.append(vc(nc.vector.tensor_tensor, XRES[:, t, :], XRES[:, t, :], bc(3), ALU.add, after=[t_bc3]))

        ss8 = st("ss8", 8)

        def rms_u(ready, eps):
            A.wait(*now())
            V.wait(*now())
            for t in range(8):
                a_(nc.scalar.activation, U[:, t, :], XRES[:, t, :], ACT.Square, accum_out=ss8[:, t:t + 1],
                   after=[ready[t], A.last])
            r = rsqrt(ss8, ss8, 1.0 / 1024, eps, [A.last])
            return [v(nc.vector.tensor_scalar, U[:, t, :], XRES[:, t, :], ss8[:, t:t + 1], None, ALU.mult, after=[r])
                    for t in range(8)]

        V.wait(t_zy)
        u = rms_u(x2, EPS2)
        nm = cols["nmix"]
        xt3, _ = to_fm(lambda t, c: U[:, t, 128 * c:128 * c + 128], lambda c: nm[:, c:c + 1], None, u)

        wi2 = X["w_in_2"][0]
        wqk, tqk = wload(6, wi2[:, 1536:2048])
        wv, twv = wload(7, wi2[:, 2048:2560])
        wg, twg = wload(8, wi2[:, 2560:3072])
        WGR = st("wgr", 128).rearrange("p (k n) -> p k n", k=8)
        twr = dma(G, "wgr", WGR, wi2[:, 3072:3088].rearrange("(k p) n -> p k n", p=128))
        GW = bc(1)[0:17, 512:768]
        tgw = [dma(G, "gw", GW[0:16, :], X["gla_gate_w_2"][0], after=now()),
               dma(G, "gwb", GW[16:17, :], X["gla_gate_b_2"][0].rearrange("(a n) -> a n", a=1))]
        A.wait(*now())
        V.wait(*now())
        GQ = slot(9)[0:64, :].rearrange("p (h n) -> p h n", h=4)
        GK = slot(10)[0:64, :].rearrange("p (h n) -> p h n", h=4)
        for fb in range(4):
            dst = GQ if fb < 2 else GK
            scl = 0.125 if fb < 2 else 1.0
            for th in range(2):
                b = 4 + (2 * fb + th) % 4
                tk = mm(b, PS[:, b, :], [(wqk[:, k, 128 * fb:128 * fb + 128], XT[:, k, 512 * th:512 * th + 512])
                                        for k in range(8)], after=[tqk, xt3])
                h0 = 2 * (fb % 2)
                a_(nc.scalar.activation, dst[:, h0, 512 * th:512 * th + 512], PS[0:64, b, :], ACT.Copy, scale=scl,
                   after=[tk])
                bank_free[b] = v(nc.vector.tensor_scalar, dst[:, h0 + 1, 512 * th:512 * th + 512], PS[64:128, b, :],
                                 scl, None, ALU.mult, after=[tk, A.last])
        GR = bc(0)[0:17, :]
        v(nc.vector.memset, GR, 1.0)
        for th in range(2):
            tk = mm(4 + th, PS[0:16, 4 + th, :], [(WGR[:, k, :], XT[:, k, 512 * th:512 * th + 512]) for k in range(8)],
                    after=[twr])
            bank_free[4 + th] = v(nc.vector.tensor_copy, GR[0:16, 512 * th:512 * th + 512], PS[0:16, 4 + th, :],
                                  after=[tk, V.last])
        R6 = slot(6)
        EL, EP, EN, EE = (R6[0:64, 512 * i:512 * i + 512] for i in range(4))
        K2, K3, SS0, SS1 = (R6[0:64, 512 * i:512 * i + 512] for i in range(4, 8))
        Q1, Q2, Q3, K4 = EL, EP, EN, EE
        ELD = st("eld", 8)[0:64, :].rearrange("p (h c) -> p h c", h=4)
        LA, KE = bc(2)[:, 0:256], bc(2)[:, 256:512]
        LB = bc(2)[:, 512:768]
        AT = bc(3)[:, 0:512]
        SQ = bc(3)[:, 512:1024]
        SS = [SS0, SS1]
        VG = bc(1)[:, 0:512]
        A.wait(*now())
        V.wait(*now())
        v(nc.vector.memset, AT, 0.0)
        v(nc.vector.memset, SS[0], 0.0)
        MPI = C("mp").bitcast(I32).unsqueeze(1).to_broadcast([128, 4, 128])
        MFI = C("mf").bitcast(I32).unsqueeze(1).to_broadcast([128, 4, 128])
        gss = st("gss", 32)
        SG = slot(4).rearrange("p (t n) -> p t n", t=8)
        GO = slot(5).rearrange("p (t n) -> p t n", t=8)
        V.wait(V.last)

        def h4(ap):
            return ap.rearrange("p (h n) -> p h n", h=4)

        for t in range(8):
            xt = [XT[:, k, 128 * t:128 * t + 128] for k in range(8)]
            tp = now()
            pz = mm(2, PS[:, 2, 0:256], [(GR[:, 128 * t:128 * t + 128], GW)], after=[tgw, V.last])
            p0 = mm(0, PS[:, 0, :], [(xt[k], wv[:, k, :]) for k in range(8)], after=[twv])
            p1 = mm(1, PS[:, 1, :], [(xt[k], wg[:, k, :]) for k in range(8)], after=[twg])
            a_(nc.scalar.activation, LB, PS[:, 2, 0:256], ACT.Abs, after=[pz, tp])
            ac(nc.scalar.activation, LB, LB, ACT.Exp, scale=-1.0)
            ac(nc.scalar.activation, LB, LB, ACT.Ln, bias=1.0)
            tla = bank_free[2] = v(nc.vector.scalar_tensor_tensor, out=LA, in0=PS[:, 2, 0:256], scalar=0.0, in1=LB,
                                   op0=ALU.min, op1=ALU.subtract, after=[A.last, *tp])
            pl = []
            for k3 in range(3):
                for h in range(4):
                    x_ = mm(3 + k3, PS[0:64, 3 + k3, 128 * h:128 * h + 128],
                            [(LA[:, 64 * h:64 * h + 64], C("tri")[:, 128 * k3:128 * k3 + 128])], after=[tla])
                pl.append(x_)
            a_(nc.scalar.activation, EL, PS[0:64, 3, :], ACT.Exp, after=[pl[0], tp])
            bank_free[3] = A.last
            a_(nc.scalar.activation, EP, PS[0:64, 4, :], ACT.Exp, after=[pl[1]])
            a_(nc.scalar.activation, EN, PS[0:64, 4, :], ACT.Exp, scale=-1.0)
            bank_free[4] = A.last
            a_(nc.scalar.activation, EE, PS[0:64, 5, :], ACT.Exp, after=[pl[2]])
            bank_free[5] = A.last
            tv = bank_free[0] = a_(nc.scalar.copy, VG, PS[:, 0, :], after=[p0])
            gq = GQ[:, :, 128 * t:128 * t + 128]
            gk = GK[:, :, 128 * t:128 * t + 128]
            tk4 = v(nc.vector.tensor_tensor, h4(K4), gk, h4(EE), ALU.mult, after=[tv])
            v(nc.vector.tensor_copy, ELD, h4(EL)[:, :, 63:128:64])
            v(nc.vector.tensor_tensor, h4(K3), gk, h4(EP), ALU.mult)
            v(nc.vector.tensor_tensor, h4(K2), gk, h4(EN), ALU.mult)
            V.wait(V.last)
            v(nc.vector.tensor_tensor, h4(Q2), gq, h4(EP), ALU.mult)
            tpast = V.last
            v(nc.vector.tensor_tensor, h4(Q3), gq, h4(EN), ALU.mult)
            tfut = V.last
            tq1 = v(nc.vector.tensor_tensor, h4(Q1), gq, h4(EL), ALU.mult)
            pke = tr(2, [(PS[:, 2, 64 * h:64 * h + 64], K4[:, 128 * h:128 * h + 128]) for h in range(4)], after=[tk4])
            for h in range(4):
                pp = mm(6, PS[:, 6, 128 * h:128 * h + 128],
                        [(K2[:, 128 * h:128 * h + 128], Q2[:, 128 * h:128 * h + 128])], after=[tpast])
            for h in range(4):
                pf = mm(7, PS[:, 7, 128 * h:128 * h + 128],
                        [(K3[:, 128 * h:128 * h + 128], Q3[:, 128 * h:128 * h + 128])], after=[tfut])
            tke = bank_free[2] = a_(nc.scalar.copy, KE, PS[:, 2, 0:256], after=[pke])
            bank_free[6] = v(nc.vector.copy_predicated, h4(AT), MPI, h4(PS[:, 6, :]), after=[pp])
            tat = bank_free[7] = vc(nc.vector.copy_predicated, h4(AT), MFI, h4(PS[:, 7, :]), after=[pf])
            for h in range(4):
                pu0 = mm(4, PS[0:64, 4, 128 * h:128 * h + 128],
                         [(KE[0:64, 64 * h:64 * h + 64], VG[0:64, 128 * h:128 * h + 128])], after=[tke, tv])
            for h in range(4):
                pu1 = mm(5, PS[0:64, 5, 128 * h:128 * h + 128],
                         [(KE[64:128, 64 * h:64 * h + 64], VG[64:128, 128 * h:128 * h + 128])])
            v(nc.vector.tensor_tensor, h4(SS[1]), h4(SS[0]), ELD[:, :, 0:1].to_broadcast([64, 4, 128]), ALU.mult)
            ts1 = bank_free[4] = vc(nc.vector.tensor_tensor, SS[1], SS[1], PS[0:64, 4, :], ALU.add, after=[pu0])
            for h in range(4):
                o = PS[:, 3, 128 * h:128 * h + 128]
                mm(3, o, [(AT[:, 128 * h:128 * h + 128], VG[:, 128 * h:128 * h + 128])], after=[tat])
                mm(3, PS[0:64, 3, 128 * h:128 * h + 128],
                   [(Q1[:, 128 * h:128 * h + 64], SS[0][:, 128 * h:128 * h + 128])], after=[tq1], start=False)
                po = mm(3, PS[64:128, 3, 128 * h:128 * h + 128],
                        [(Q1[:, 128 * h + 64:128 * h + 128], SS[1][:, 128 * h:128 * h + 128])], after=[ts1],
                        start=False)
            v(nc.vector.tensor_tensor, h4(SS[0]), h4(SS[1]), ELD[:, :, 1:2].to_broadcast([64, 4, 128]), ALU.mult,
              after=[po])
            bank_free[5] = vc(nc.vector.tensor_tensor, SS[0], SS[0], PS[0:64, 5, :], ALU.add, after=[pu1])
            a_(nc.scalar.activation, SQ, PS[:, 3, :], ACT.Square, after=[po])
            v(nc.vector.tensor_reduce, gss[:, 4 * t:4 * t + 4], h4(SQ), AX, ALU.add, after=[A.last])
            bank_free[3] = v(nc.vector.tensor_copy, GO[:, t, :], PS[:, 3, :])
            bank_free[1] = silu_into(SG[:, t, :], PS[:, 1, :], [p1])
        slot_free[6] = slot_free[7] = slot_free[8] = now()
        r = rsqrt(gss, gss, 1.0 / 128, EPS2, [V.last])
        for t in range(8):
            o3 = h4(GO[:, t, :])
            vc(nc.vector.tensor_tensor, o3, o3, b4(gss[:, 4 * t:4 * t + 4], 128), ALU.mult)
            vc(nc.vector.tensor_tensor, GO[:, t, :], GO[:, t, :], SG[:, t, :], ALU.mult)

        ws = [wload(6 + n, wi2[:, 512 * n:512 * n + 512]) for n in range(3)]
        DQ = slot(9).rearrange("p (h n) -> p h n", h=4)
        DK = slot(10).rearrange("p (h n) -> p h n", h=4)
        DV = slot(4).rearrange("p (t n) -> p t n", t=8)
        DQT = [bc(0)[:, 0:512], bc(0)[:, 512:1024]]
        A.wait(*now())
        V.wait(*now())
        dss = st("dss", 16)
        tm_free = [None, None]
        for t in range(8):
            xt = [XT[:, k, 128 * t:128 * t + 128] for k in range(8)]
            for n in range(3):
                pr = mm(n, PS[:, n, :], [(xt[k], ws[n][0][:, k, :]) for k in range(8)], after=[ws[n][1]])
                if n == 2:
                    bank_free[2] = a_(nc.scalar.copy, DV[:, t, :], PS[:, 2, :], after=[pr])
                    continue
                sq = bc(1)[:, 512 * n:512 * n + 512]
                d8 = dss[:, 8 * n:8 * n + 8]
                x_ = a_(nc.scalar.activation, sq, PS[:, n, :], ACT.Square, after=[pr, V.last])
                v(nc.vector.tensor_reduce, d8, sq.rearrange("p (h n) -> p h n", h=8), AX, ALU.add, after=[x_])
                r = rsqrt(d8, d8, 1.0 / 64, EPS2, [V.last])
                o = DQT[n]
                bank_free[n] = r = v(nc.vector.tensor_tensor, o.rearrange("p (h n) -> p h n", h=8),
                                     PS[:, n, :].rearrange("p (h n) -> p h n", h=8), b4(d8, 64), ALU.mult,
                                     after=[r, tm_free[n]])
                b = 3 + n
                tm_free[n] = p_ = tr(b, [(PS[:, b, 128 * h:128 * h + 128], o[:, 128 * h:128 * h + 128])
                                         for h in range(4)], after=[r])
                dst = (DQ, DK)[n][:, :, 128 * t:128 * t + 128]
                bank_free[b] = a_(nc.scalar.activation, dst, h4(PS[:, b, :]), ACT.Copy,
                                  scale=cols[("daq", "dak")[n]], after=[p_])
        A.wait(*now())
        V.wait(*now())
        P.wait(*now())
        slot_free[7] = slot_free[8] = now()
        DO = slot(6).rearrange("p (t n) -> p t n", t=8)
        s23 = slot(2, 2)
        PB1 = [[s23[:, 0:1024], s23[:, 1024:2048]], [s23[:, 2048:3072], s23[:, 3072:4096]]]
        PC = [s23[:, 4096:5120], s23[:, 5120:6144]]
        PT2 = [s23[:, 6144:7168], s23[:, 7168:8192]]

        def da_qk(h, i, m, c0, c1):
            return (DQ[64 * m:64 * m + 64, h, 128 * i:128 * i + 128], DK[64 * m:64 * m + 64, h, c0:c1])

        class Combine:
            free = [None, None]

            def __call__(self, n, nk, pt):
                (t1, r1), (t2, r2) = pt
                c2 = st(f"c2{n % 2}", 1)
                v(nc.vector.tensor_tensor, c2, r2, nlam, ALU.mult, after=[t1, t2])
                pc = PC[n % 2][:, 0:nk]
                vc(nc.vector.tensor_scalar, pc, PB1[n % 2][1][:, 0:nk], c2, None, ALU.mult, after=[self.free[n % 2]])
                t = vc(nc.vector.scalar_tensor_tensor, out=pc, in0=PB1[n % 2][0][:, 0:nk], scalar=r1, in1=pc,
                       op0=ALU.mult, op1=ALU.add)
                return PC[n % 2], t

        dos = st("dos", 32).rearrange("p (t h) -> p t h", t=8)
        SQD = bc(1)[:, 0:128]

        def da_out(h, i, o, t, pt):
            x_ = a_(nc.scalar.activation, SQD, o, ACT.Square, accum_out=dos[:, i, h:h + 1], after=[t, A.last])
            return v(nc.vector.tensor_copy, DO[:, i, 128 * h:128 * h + 128], o, after=[x_])

        attention([(h, i) for h in range(4) for i in range(8)], da_qk, C("chm"), 64.0 ** -0.5, PB1, PT2,
                  lambda h, j: DV[:, j, 128 * h:128 * h + 128], 128, da_out, nmap=2, combine=Combine())
        dosf = dos.rearrange("p t h -> p (t h)")
        rsqrt(dosf, dosf, 1.0 / 128, EPS2, now())
        for t in range(8):
            vc(nc.vector.tensor_tensor, h4(DO[:, t, :]), h4(DO[:, t, :]), b4(dos[:, t, :], 128), ALU.mult)
        dag = st("dag", 1)
        vc(nc.vector.tensor_scalar, dag, cols["daon"], 0.8, None, ALU.mult)

        MIX2 = [DO, GO]
        A.wait(*now())
        V.wait(*now())
        mt, _ = to_fm(lambda t, c: MIX2[c // 4][:, t, 128 * (c % 4):128 * (c % 4) + 128],
                      lambda c: dag if c < 4 else cols["glon"], None, [now()] * 8)

        def add_res(t, n, ps, tk):
            x = XRES[:, t, 512 * n:512 * n + 512]
            return v(nc.vector.tensor_tensor, x, x, ps, ALU.add, after=[tk])

        xr = project(X["w_o_2"][0], lambda k, t: XT[:, k, 128 * t:128 * t + 128], add_res, mt, slots=(7, 8))
        slot_free[6] = now()

        MEM = slot(9)[:, 0:2048].rearrange("p (t d) -> p t d", t=2)
        MEMT = slot(9)[:, 2048:4096].rearrange("p (c n) -> p c n", c=8)
        CK = slot(10)[:, 0:2048].rearrange("p (c n) -> p c n", c=8)
        CV = slot(10)[:, 2048:4096].rearrange("p (t d) -> p t d", t=2)
        tmem = dma(G, "mem", MEM, X["mem_2"][0].rearrange("(t p) d -> p t d", p=128), after=now())
        mss = st("mss", 2)
        SQC = bc(0)
        for t in range(2):
            a_(nc.scalar.activation, SQC, MEM[:, t, :], ACT.Square, accum_out=mss[:, t:t + 1],
               after=[tmem, V.last, A.last])
        r = rsqrt(mss, mss, 1.0 / 1024, EPS2, [A.last])
        for t in range(2):
            v(nc.vector.tensor_scalar, MEM[:, t, :], MEM[:, t, :], mss[:, t:t + 1], None, ALU.mult, after=[r])
        tm = V.last
        tmt = []
        for c in range(8):
            b = c % 4
            p_ = tr(b, [(PS[:, b, 128 * t:128 * t + 128], MEM[:, t, 128 * c:128 * c + 128]) for t in range(2)],
                    after=[tm])
            bank_free[b] = a_(nc.scalar.activation, MEMT[:, c, :], PS[:, b, 0:256], ACT.Copy,
                              scale=cols["nmem"][:, c:c + 1], after=[p_])
            tmt.append(bank_free[b])
        wkv = X["w_ckv_2"][0]
        css = st("css", 4)
        KTM2 = bc(1)[:, 0:512]
        ktm_free = None
        A.wait(*now())
        V.wait(*now())
        for n in range(4):
            s = 6 + n % 3
            w, tw = wload(s, wkv[:, 512 * n:512 * n + 512])
            for t in range(2):
                b = 4 + t
                p_ = mm(b, PS[:, b, :], [(MEMT[:, k, 128 * t:128 * t + 128], w[:, k, :]) for k in range(8)],
                        after=[tw, tmt])
                if n >= 2:
                    bank_free[b] = a_(nc.scalar.copy, CV[:, t, 512 * (n - 2):512 * (n - 2) + 512], PS[:, b, :],
                                      after=[p_])
                    continue
                for hh in range(2):
                    a_(nc.scalar.activation, SQC[:, 0:256], PS[:, b, 256 * hh:256 * hh + 256], ACT.Square,
                       accum_out=css[:, hh:hh + 1], after=[p_, A.last, V.last])
                r = rsqrt(css[:, 0:2], css[:, 0:2], 1.0 / 256, EPS2, [A.last])
                bank_free[b] = r = v(nc.vector.tensor_tensor, KTM2.rearrange("p (h n) -> p h n", h=2),
                                     PS[:, b, :].rearrange("p (h n) -> p h n", h=2), b4(css[:, 0:2], 256), ALU.mult,
                                     after=[r, ktm_free])
                ktm_free = p_ = tr(6, [(PS[:, 6, 128 * c:128 * c + 128], KTM2[:, 128 * c:128 * c + 128])
                                       for c in range(4)], after=[r])
                for dc in range(2):
                    o = CK[:, 4 * dc + 2 * n:4 * dc + 2 * n + 2, 128 * t:128 * t + 128]
                    i_ = PS[:, 6, :].rearrange("p (h d n) -> p h d n", h=2, d=2)[:, :, dc, :]
                    bank_free[6] = a_(nc.scalar.activation, o, i_, ACT.Copy, scale=cols["ckn"][:, dc:dc + 1],
                                      after=[p_])
            slot_free[s] = P.last
        u = rms_u(xr, EPS2)
        nc_ = cols["ncr"]
        V.wait(P.last)
        A.wait(P.last)
        xt4, _ = to_fm(lambda t, c: U[:, t, 128 * c:128 * c + 128], lambda c: nc_[:, c:c + 1], None, u)
        wq_, twq_ = zip(*[wload(6 + n, X["w_cq_2"][0][:, 512 * n:512 * n + 512]) for n in range(2)])
        A.wait(*now())
        V.wait(*now())
        G.wait(*now())
        CQ = bc(0)
        CQT = bc(1).rearrange("p (d h n) -> p d h n", d=2, h=4)
        CP = bc(2).rearrange("p (h n) -> p h n", h=4)
        CPT = bc(3).rearrange("p (m h n) -> p m h n", m=2, h=4)
        cm, cr = st("cm", 4), st("cr", 4)
        for t in range(8):
            xt = [XT[:, k, 128 * t:128 * t + 128] for k in range(8)]
            tp = now()
            pqs = [mm(n, PS[:, n, :], [(xt[k], wq_[n][:, k, :]) for k in range(8)], after=[twq_[n], xt4])
                   for n in range(2)]
            for h in range(4):
                a_(nc.scalar.activation, CP[:, h, :], PS[:, h // 2, 256 * (h % 2):256 * (h % 2) + 256], ACT.Square,
                   accum_out=css[:, h:h + 1], after=[pqs[h // 2], A.last, tp])
            r = rsqrt(css, css, 1.0 / 256, EPS2, [A.last])
            bank_free[0] = bank_free[1] = r = v(
                nc.vector.tensor_tensor, CQ.rearrange("p (h n) -> p h n", h=4),
                PS[:, 0:2, :].rearrange("p b n -> p (b n)").rearrange("p (h n) -> p h n", h=4), b4(css, 256), ALU.mult,
                after=[r, tp])
            for dc in range(2):
                p_ = tr(2 + dc, [(PS[:, 2 + dc, 128 * h:128 * h + 128], CQ[:, 256 * h + 128 * dc:256 * h + 128 * dc + 128])
                                 for h in range(4)], after=[r])
                bank_free[2 + dc] = a_(nc.scalar.activation, CQT[:, dc, :, :], h4(PS[:, 2 + dc, :]), ACT.Copy,
                                       scale=cols["cqn"][:, dc:dc + 1], after=[p_])
            tq = A.last
            for h in range(4):
                b = 4 + h // 2
                ps_ = mm(b, PS[:, b, 256 * (h % 2):256 * (h % 2) + 256],
                         [(CQT[:, dc, h, :], CK[:, 4 * dc + h, :]) for dc in range(2)], after=[tq])
            s4_ = PS[:, 4:6, :].rearrange("p b n -> p (b n)").rearrange("p (h n) -> p h n", h=4)
            v(nc.vector.tensor_reduce, cm, s4_, AX, ALU.max, after=[ps_])
            r = vc(nc.vector.tensor_scalar, cm, cm, -1.0 / 16, None, ALU.mult)
            for h in range(4):
                a_(nc.scalar.activation, CP[:, h, :], s4_[:, h, :], ACT.Exp, bias=cm[:, h:h + 1], scale=1.0 / 16,
                   accum_out=cr[:, h:h + 1], after=[r])
            te = bank_free[4] = bank_free[5] = A.last
            r = v(nc.vector.reciprocal, cr, cr, after=[te])
            for m in range(2):
                p_ = tr(6 + m, [(PS[:, 6 + m, 128 * h:128 * h + 128], CP[:, h, 128 * m:128 * m + 128])
                                for h in range(4)], after=[te])
                bank_free[6 + m] = v(nc.vector.tensor_copy, CPT[:, m, :, :], h4(PS[:, 6 + m, :]), after=[p_])
            tpt = V.last
            for h in range(4):
                b = 2 + h // 2
                po = mm(b, PS[:, b, 256 * (h % 2):256 * (h % 2) + 256],
                        [(CPT[:, m, h, :], CV[:, m, 256 * h:256 * h + 256]) for m in range(2)], after=[tpt])
            bank_free[2] = bank_free[3] = v(
                nc.vector.tensor_tensor, U[:, t, :].rearrange("p (h n) -> p h n", h=4),
                PS[:, 2:4, :].rearrange("p b n -> p (b n)").rearrange("p (h n) -> p h n", h=4), b4(cr, 256), ALU.mult,
                after=[po])
        slot_free[6] = slot_free[7] = P.last
        A.wait(*now())
        V.wait(*now())
        mt, _ = to_fm(lambda t, c: U[:, t, 128 * c:128 * c + 128], lambda c: one1, None, [now()] * 8)
        xr = project(X["w_co_2"][0], lambda k, t: XT[:, k, 128 * t:128 * t + 128], add_res, mt, slots=(8, 6, 7))

        XZ, TOKS, YO = scr
        u = rms_u(xr, EPS2)
        A.wait(P.last)
        V.wait(P.last)
        t_xz = [dma(A, f"x{t}", XZ.rearrange("(t p) d -> p t d", p=128)[:, t, :], U[:, t, :], after=[u[t]])
                for t in range(8)]
        nf = cols["nffn"]
        WRT = slot(9)[:, 0:288].rearrange("p (k n) -> p k n", k=8)
        twr = [dma(G, "wr0", WRT[:, :, 0:4], X["w_group_2"][0].rearrange("(k p) n -> p k n", p=128), after=now()),
               dma(G, "wr1", WRT[:, :, 4:36], X["w_expert_2"][0].rearrange("(k p) n -> p k n", p=128))]
        BR = slot(9)[:, 288:324]
        tbr = [dma(G, "br0", BR[:, 0:4], X["b_group_2"][0].partition_broadcast(128)),
               dma(G, "br1", BR[:, 4:36], X["b_expert_2"][0].partition_broadcast(128))]
        ZI = slot(9)[:, 1024:1024 + 752].bitcast(I32)
        v(nc.vector.memset, ZI, 0, after=now())
        t_z = dma(G, "tz", TOKS.rearrange("(p b) w -> p (b w)", p=128), ZI, after=[V.last])
        xt5, _ = to_fm(lambda t, c: U[:, t, 128 * c:128 * c + 128], lambda c: nf[:, c:c + 1], None, u)
        for t in range(8):
            pr = mm(4, PS[:, 4, 36 * t:36 * t + 36], [(XT[:, k, 128 * t:128 * t + 128], WRT[:, k, :])
                                                     for k in range(8)], after=[twr, xt5])
        W9 = slot(10)
        wat = [0]

        def wk_(n):
            a = wat[0]
            wat[0] += n
            assert wat[0] <= 4096
            return W9[:, a:a + n]

        V.wait(*now())
        TT = nc.vector.tensor_tensor
        TS = nc.vector.tensor_scalar
        LG = wk_(288).rearrange("p (t n) -> p t n", t=8)
        bank_free[4] = vc(TT, LG, PS[:, 4, 0:288].rearrange("p (t n) -> p t n", t=8),
                          BR.unsqueeze(1).to_broadcast([128, 8, 36]), ALU.add, after=[pr, *tbr])
        io = C("io")

        def bt(ap, n):
            return ap.unsqueeze(2).to_broadcast([128, 8, n])

        def first_max(x, n):
            m_, i_ = wk_(8), wk_(8)
            eq = wk_(8 * n).rearrange("p (t n) -> p t n", t=8)
            vc(nc.vector.tensor_reduce, m_, x, AX, ALU.max)
            vc(TT, eq, x, bt(m_, n), ALU.is_equal)
            vc(TS, eq, eq, -100.0, 100.0, ALU.mult, ALU.add)
            vc(TT, eq, eq, io[:, 0:n].unsqueeze(1).to_broadcast([128, 8, n]), ALU.add)
            vc(nc.vector.tensor_reduce, i_, eq, AX, ALU.min)
            return m_, i_

        def one_hot(i_, n):
            o = wk_(8 * n).rearrange("p (t n) -> p t n", t=8)
            vc(TT, o, io[:, 0:n].unsqueeze(1).to_broadcast([128, 8, n]), bt(i_, n), ALU.is_equal)
            return o

        gm, gi = first_max(LG[:, :, 0:4], 4)
        ge = wk_(32).rearrange("p (t n) -> p t n", t=8)
        vc(TT, ge, LG[:, :, 0:4], bt(gm, 4), ALU.subtract)
        t = a_(nc.scalar.activation, ge, ge, ACT.Exp, after=[V.last])
        pg = wk_(8)
        v(nc.vector.tensor_reduce, pg, ge, AX, ALU.add, after=[t])
        vc(nc.vector.reciprocal, pg, pg)
        o4 = one_hot(gi, 4)
        em = wk_(256)
        EM = em.rearrange("p (t g e) -> p t g e", t=8, g=4)
        for gg in range(4):
            vc(TT, EM[:, :, gg, :], LG[:, :, 4 + 8 * gg:12 + 8 * gg], o4[:, :, gg:gg + 1].to_broadcast([128, 8, 8]),
               ALU.mult)
        ELG = wk_(64).rearrange("p (t n) -> p t n", t=8)
        vc(TT, ELG, EM[:, :, 0, :], EM[:, :, 1, :], ALU.add)
        vc(TT, ELG, ELG, EM[:, :, 2, :], ALU.add)
        vc(TT, ELG, ELG, EM[:, :, 3, :], ALU.add)
        m1, i1 = first_max(ELG, 8)
        oh1 = one_hot(i1, 8)
        vc(nc.vector.scalar_tensor_tensor, out=ELG, in0=oh1, scalar=NEG, in1=ELG, op0=ALU.mult, op1=ALU.add)
        m2, i2 = first_max(ELG, 8)
        dd, g1, g2 = wk_(8), st("g1", 8), st("g2", 8)
        vc(TT, dd, m2, m1, ALU.subtract)
        t = a_(nc.scalar.activation, dd, dd, ACT.Exp, after=[V.last])
        v(TS, g1, dd, 1.0, None, ALU.add, after=[t])
        vc(nc.vector.reciprocal, g1, g1)
        vc(TT, g1, g1, pg, ALU.mult)
        vc(TT, g2, g1, dd, ALU.mult)
        es, OHS, ranks = [], [], []
        for ii in (i1, i2):
            e_ = wk_(8)
            vc(nc.vector.scalar_tensor_tensor, out=e_, in0=gi, scalar=8.0, in1=ii, op0=ALU.mult, op1=ALU.add)
            es.append(e_)
            OHS.append(one_hot(e_, 32))
        MM = wk_(256)
        M3 = MM.rearrange("p (t n) -> p t n", t=8)
        tm = vc(TT, M3, OHS[0], OHS[1], ALU.add)
        p1 = mm(5, PS[:, 5, 0:256], [(C("su"), MM)], after=[tm])
        p2 = mm(6, PS[:, 6, 0:256], [(C("one"), MM)])
        TOT = PS[:, 6, 0:256].rearrange("p (t n) -> p t n", t=8)
        PRE = wk_(256).rearrange("p (t n) -> p t n", t=8)
        run = wk_(32)
        V.wait(V.last)
        v(nc.vector.memset, run, 0.0)
        for t in range(8):
            vc(TT, PRE[:, t, :], PS[:, 5, 32 * t:32 * t + 32], run, ALU.add, after=[p1, p2])
            vc(TT, run, run, TOT[:, t, :], ALU.add)
        bank_free[5] = bank_free[6] = V.last
        ob, sca, scb, cmpb = wk_(32), wk_(32), wk_(32), wk_(32)
        vc(TS, ob, run, 128.5, None, ALU.is_gt)
        for kk in range(2, 8):
            vc(TS, cmpb, run, 128.0 * kk + 0.5, None, ALU.is_gt)
            vc(TT, ob, ob, cmpb, ALU.add)
        vc(nc.vector.tensor_copy, sca, ob)
        a1, b1 = sca, scb
        for sft in (1, 2, 4, 8, 16):
            vc(nc.vector.tensor_copy, b1[:, 0:sft], a1[:, 0:sft])
            vc(TT, b1[:, sft:32], a1[:, sft:32], a1[:, 0:32 - sft], ALU.add)
            a1, b1 = b1, a1
        os_ = wk_(32)
        vc(TT, os_, a1, ob, ALU.subtract)
        sls, slt = [], []
        for kk in range(2):
            rk, osa, qq, cq, tmp_ = wk_(8), wk_(8), wk_(8), wk_(8), wk_(8)
            prod = em.rearrange("p (t n) -> p t n", t=8)
            vc(TT, prod, OHS[kk], PRE, ALU.mult)
            vc(nc.vector.tensor_reduce, rk, prod, AX, ALU.add)
            vc(TT, prod, OHS[kk], os_.unsqueeze(1).to_broadcast([128, 8, 32]), ALU.mult)
            vc(nc.vector.tensor_reduce, osa, prod, AX, ALU.add)
            vc(TS, qq, rk, 127.5, None, ALU.is_gt)
            for k7 in range(2, 8):
                vc(TS, cq, rk, 128.0 * k7 - 0.5, None, ALU.is_gt)
                vc(TT, qq, qq, cq, ALU.add)
            vc(nc.vector.scalar_tensor_tensor, out=tmp_, in0=osa, scalar=31.0, in1=qq, op0=ALU.add, op1=ALU.add)
            vc(TT, tmp_, tmp_, es[kk], ALU.subtract)
            vc(TS, cq, qq, 1.0, None, ALU.min)
            vc(TT, tmp_, tmp_, cq, ALU.mult)
            vc(TT, tmp_, tmp_, es[kk], ALU.add)
            vc(nc.vector.scalar_tensor_tensor, out=rk, in0=qq, scalar=-128.0, in1=rk, op0=ALU.mult, op1=ALU.add)
            vc(nc.vector.scalar_tensor_tensor, out=qq, in0=tmp_, scalar=128.0, in1=rk, op0=ALU.mult, op1=ALU.add)
            vc(nc.vector.scalar_tensor_tensor, out=tmp_, in0=rk, scalar=float(NBLK), in1=tmp_, op0=ALU.mult,
               op1=ALU.add)
            for lst, val, nm_ in ((sls, qq, "slot"), (slt, tmp_, "tslot")):
                si_ = st(f"{nm_}{kk}", 8).bitcast(I32)
                vc(nc.vector.tensor_copy, si_, val)
                lst.append(si_)
        ov = wk_(NOVF)
        V.wait(V.last)
        for jj in range(NOVF):
            v(TS, cmpb, a1, jj + 0.5, None, ALU.is_lt, after=[V.last])
            vc(nc.vector.tensor_reduce, ov[:, jj:jj + 1], cmpb, AX, ALU.add)
        vc(TS, ov, ov, 31.0, None, ALU.min)
        OVI = st("ovi", NOVF).bitcast(I32)
        vc(nc.vector.tensor_copy, OVI, ov)
        NOV = st("nov", 1).bitcast(I32)
        t_ovi = vc(nc.vector.tensor_copy, NOV, a1[:, 31:32])
        TK = wk_(8 * 16)
        TKI = TK.bitcast(I32).rearrange("p (t w) -> p t w", t=8)
        t_tk = vc(nc.vector.tensor_copy, TKI, C("tok").unsqueeze(2).to_broadcast([128, 8, 16]))
        G.wait(t_tk, t_z)
        sc_t = []
        d_sc = [DmaSem(f"d_sc{i}") for i in range(4)]
        for n in range(16):
            t, kk = n // 2, n % 2
            d = d_sc[n % 4]
            if d.n:
                G.wait((d.sem, 16 * d.n))
            nc.gpsimd.indirect_dma_start(TOKS, bass.IndirectOffsetOnAxis(slt[kk].bitcast(U32)[:, t:t + 1], 0),
                                         TKI[:, t, :], None).then_inc(d.sem, 16)
            d.n += 1
        for d in d_sc:
            G.wait((d.sem, 16 * d.n))
        IDX = st("idx", NBLK).bitcast(I32)
        t_tok = dma(G, "idx", ZI, TOKS.rearrange("(p b) w -> p (b w)", p=128))
        t_idx = v(nc.vector.tensor_copy, IDX, ZI.rearrange("p (b w) -> p b w", w=16)[:, :, 0], after=[t_tok])
        G.wait(t_idx, *t_xz)

        for s in range(2, 11):
            slot_free[s] = [*now(), *t_xz]
        XB = [bc(0), bc(1)]
        XBT = bc(2).rearrange("p (c n) -> p c n", c=8)
        assert CONSTS["ident"][0] == 0 and cst.shape[1] >= 1664
        HID = CT[:, 128:640]
        HIT = CT[:, 640:1152]
        YB = [CT[:, 1152:1664], CSN[:, 0:512]]
        weg, weu, wed = X["w_e_gate_2"][0], X["w_e_up_2"][0], X["w_e_down_2"][0]
        unit = [0]

        def wexp(b):
            if b < 32:
                srcs = [weg[b], weu[b], wed[b]]
            else:
                e_ = nc.sync.value_load(OVI[0:1, b - 32:b - 31], min_val=0, max_val=31)
                srcs = [w_[bass.ds(e_, 1), :, :].rearrange("a k n -> (a k) n") for w_ in (weg, weu, wed)]
            res = []
            for s_ in srcs:
                sl_ = 2 + unit[0] % 9
                unit[0] += 1
                res.append((*wload(sl_, s_), sl_))
            return res

        XBT2 = [XBT, bc(3).rearrange("p (c n) -> p c n", c=8)]

        def experts(blocks):
            xb_free, xbt_free, yb_free = [None, None], [None, None], [None, None]
            hid_free = hit_free = None
            xb_t, xbt_t, hid_t, hit_t = {}, {}, {}, {}

            def gather(b):
                name = branch[0] + f"gat{b % 2}"
                if name not in dsems:
                    dsems[name] = DmaSem("d_" + name)
                d = dsems[name]
                if d.n:
                    G.wait((d.sem, 16 * d.n))
                G.wait(xb_free[b % 2])
                nc.gpsimd.indirect_dma_start(
                    XB[b % 2], None, XZ,
                    bass.IndirectOffsetOnAxis(IDX.bitcast(U32)[:, b:b + 1], 0)).then_inc(d.sem, 16)
                d.n += 1
                xb_t[b] = (d.sem, 16 * d.n)

            def turn(b):
                for hf in range(2):
                    p_ = tr(hf, [(PS[:, hf, 128 * c:128 * c + 128],
                                  XB[b % 2][:, 512 * hf + 128 * c:512 * hf + 128 * c + 128]) for c in range(4)],
                            after=[xb_t[b]])
                    bank_free[hf] = v(nc.vector.tensor_tensor, XBT2[b % 2][:, 4 * hf:4 * hf + 4, :],
                                      h4(PS[:, hf, :]), b4(nf[:, 4 * hf:4 * hf + 4], 128), ALU.mult,
                                      after=[p_, xbt_free[b % 2]])
                xb_free[b % 2] = P.last
                xbt_t[b] = V.last

            first, last = blocks[0], blocks[-1]
            gather(first)
            gather(first + 1)
            we = {first: wexp(first)}
            turn(first)
            for b in [*blocks, last + 1]:
                if b <= last:
                    (wg_, tg_, sg_), (wu_, tu_, su_), _ = we[b]
                    pg_ = mm(2, PS[:, 2, :], [(XBT2[b % 2][:, k, :], wg_[:, k, :]) for k in range(8)],
                             after=[tg_, xbt_t[b]])
                    slot_free[sg_] = pg_
                    pu_ = mm(3, PS[:, 3, :], [(XBT2[b % 2][:, k, :], wu_[:, k, :]) for k in range(8)], after=[tu_])
                    slot_free[su_] = xbt_free[b % 2] = pu_
                    t = bank_free[2] = a_(nc.scalar.activation, HID, PS[:, 2, :], ACT.Silu, after=[pg_, hid_free])
                    hid_t[b] = bank_free[3] = v(nc.vector.tensor_tensor, HID, HID, PS[:, 3, :], ALU.mult,
                                                after=[t, pu_])
                    if b < last:
                        turn(b + 1)
                        if b + 1 < last:
                            gather(b + 2)
                        we[b + 1] = wexp(b + 1)
                if b > first:
                    wd_, td_, sd_ = we[b - 1][2]
                    for hf in range(2):
                        p_ = mm(5 + hf, PS[:, 5 + hf, :],
                                [(HIT[:, 128 * k:128 * k + 128], wd_[:, k, 512 * hf:512 * hf + 512])
                                 for k in range(4)], after=[td_, hit_t[b - 1]])
                        bank_free[5 + hf] = a_(nc.scalar.copy, YB[hf], PS[:, 5 + hf, :], after=[p_, yb_free[hf]])
                        yb_free[hf] = dma(A, f"yo{hf}", YO[128 * (b - 1):128 * b, 512 * hf:512 * hf + 512], YB[hf],
                                          after=[A.last])
                    slot_free[sd_] = hit_free = P.last
                if b <= last:
                    hid_free = tr(4, [(PS[:, 4, 128 * c:128 * c + 128], HID[:, 128 * c:128 * c + 128])
                                      for c in range(4)], after=[hid_t[b]])
                    hit_t[b] = bank_free[4] = a_(nc.scalar.copy, HIT, PS[:, 4, :], after=[hid_free, hit_free])
            return yb_free

        A.wait(*now())
        V.wait(*now())
        G.wait(*now())
        y_out = experts(range(32))
        for q in (P, V, A, G, S):
            q.wait(t_ovi, t_zy, *now(), *y_out)
        n_over = nc.values_load(NOV[0:1, 0:1], min_val=0, max_val=NOVF)
        with branch_of(n_over > 0):
            experts(range(32, NBLK))

        GB = slot(2, 2).rearrange("p (n d) -> p n d", n=8)
        cg = [DmaSem(f"cg{i}") for i in range(8)]
        cg_free = [None] * 8
        odma = []
        for n in range(16):
            t, kk = n // 2, n % 2
            d = cg[n % 8]
            G.wait(cg_free[n % 8])
            if d.n:
                G.wait((d.sem, 16 * d.n))
            nc.gpsimd.indirect_dma_start(GB[:, n % 8, :], None, YO,
                                         bass.IndirectOffsetOnAxis(sls[kk].bitcast(U32)[:, t:t + 1], 0)).then_inc(d.sem, 16)
            d.n += 1
            gt = (g1, g2)[kk]
            r = vc(nc.vector.scalar_tensor_tensor, out=XRES[:, t, :], in0=GB[:, n % 8, :], scalar=gt[:, t:t + 1],
                   in1=XRES[:, t, :], op0=ALU.mult, op1=ALU.add, after=[(d.sem, 16 * d.n)])
            cg_free[n % 8] = r
            if kk:
                odma.append(dma(S, f"o{t}", out[0].rearrange("(t p) d -> p t d", p=128)[:, t, :], XRES[:, t, :],
                                after=[r]))
        S.wait(*odma)


def kernel(**inputs):
    import concourse.bacc as _bacc
    from concourse.bass_utils import run_bass_kernel_spmd as _run

    nc = _bacc.Bacc("TRN2", target_bir_lowering=False, num_devices=1)
    arrays, X = {}, {}
    for name, val in inputs.items():
        a = np.ascontiguousarray(val)
        arrays[f"in_{name}"] = a
        X[name] = nc.dram_tensor(f"in_{name}", a.shape, mybir.dt.from_np(a.dtype), kind="ExternalInput").ap()
    table = const_table()
    arrays["in_table"] = table
    cst = nc.dram_tensor("in_table", table.shape, F32, kind="ExternalInput").ap()
    out = nc.dram_tensor("out_0", (1, 1024, 1024), F32, kind="ExternalOutput").ap()
    scr = (nc.dram_tensor("xz", (1024, 1024), F32).ap(), nc.dram_tensor("toks", (NBLK * 128, 16), I32).ap(),
           nc.dram_tensor("yo", (NBLK * 128, 1024), F32).ap())
    program(nc, X, out, cst, scr)
    r = _run(nc, [arrays], core_ids=[0])
    return r.results[0]["out_0"]
```

```python
import math
from contextlib import ExitStack, contextmanager

import numpy as np

import concourse.bass as bass
from concourse import mybir

F32 = mybir.dt.float32
F32R = mybir.dt.float32r
I32 = mybir.dt.int32
U32 = mybir.dt.uint32
ALU = mybir.AluOpType
ACT = mybir.ActivationFunctionType
AX = mybir.AxisListType.X

NEG = -3.0e38
ALPHA = 2.0 ** 0.25
EPS = 1e-5
EPS2 = 1e-6
NBLK = 47
NOVF = 15
SL = 4096

CONSTS = {}


def const_table():
    p = np.arange(128)
    j, i = p[:, None], p[None, :]
    same = (j // 64) == (i // 64)
    lg = np.log(1.0 - 2.0 ** (-5.0 - np.arange(4)))
    past = (same & (j <= i)).astype(np.float64)
    mid = (i // 64) * 64 + 31
    pmid = (same & (j <= mid)).astype(np.float64)
    parts = {
        "ident": np.eye(128),
        "caus": np.where(i <= j, 0.0, NEG),
        "chm": np.where(i // 64 <= j // 64, 0.0, NEG),
        "dec": np.concatenate([np.where(i >= j, np.exp(g * np.maximum(i - j, 0)), 0.0) * 0.125 for g in lg], 1),
        "zet": np.exp(lg[None, :] * (127 - j)) * 0.125,
        "xi": np.exp(lg[None, :] * (j + 1)),
        "gc": np.tile(np.exp(lg * 128)[None, :], (128, 1)),
        "tri": np.concatenate([past, past - pmid, (same & (j > i)).astype(float)], 1) / 16.0,
        "mp": past,
        "mf": (same & (j > i)).astype(float),
        "inv": np.tile(np.concatenate([10000.0 ** (-np.arange(32) / 32), 10000.0 ** (-np.arange(16) / 16)])[None], (128, 1)),
        "su": (j < i).astype(float),
        "one": np.ones((128, 128)),
        "io": np.tile(np.arange(32.0)[None], (128, 1)),
        "tok": j + 128.0 * np.arange(8)[None],
    }
    at = 0
    for k, v in parts.items():
        CONSTS[k] = (at, v.shape[1])
        at += v.shape[1]
    return np.ascontiguousarray(np.concatenate(list(parts.values()), 1).astype(np.float32))


class Queue:

    def __init__(self, eng, sem):
        self.eng, self.sem, self.n, self.seen = eng, sem, 0, {}

    def wait(self, *tokens):
        for t in tokens:
            if t is None:
                continue
            if isinstance(t, list):
                self.wait(*t)
                continue
            sem, v = t
            if v > self.seen.get(id(sem), 0):
                self.eng.wait_ge(sem, v)
                self.seen[id(sem)] = v

    def mark(self, ins):
        ins.then_inc(self.sem, 1)
        self.n += 1
        return (self.sem, self.n)

    @property
    def last(self):
        return (self.sem, self.n) if self.n else None


def program(nc, X, out, cst, scr):
    ctx = ExitStack()
    with ctx:
        def sem(name):
            return ctx.enter_context(nc.semaphore(name))

        XR = ctx.enter_context(nc.sbuf_tensor("XR", [128, 2 * SL], F32))
        NC_ = cst.shape[1]
        CT = ctx.enter_context(nc.sbuf_tensor("CT", [128, NC_], F32))
        BC = ctx.enter_context(nc.sbuf_tensor("BC", [128, 4 * 1024], F32))
        ST = ctx.enter_context(nc.sbuf_tensor("ST", [128, 1344], F32))
        CSN = ctx.enter_context(nc.sbuf_tensor("CSN", [128, 768], F32))
        PS = ctx.enter_context(nc.psum_tensor("PS", [128, 8, 512], F32))

        P = Queue(nc.tensor, sem("pe"))
        V = Queue(nc.vector, sem("dve"))
        A = Queue(nc.scalar, sem("act"))
        G = Queue(nc.gpsimd, sem("pool"))
        S = Queue(nc.sync, sem("sp"))

        class DmaSem:
            def __init__(self, name):
                self.sem, self.n = sem(name), 0

        dsems = {}

        branch = [""]

        def dma(q, slot, o, i, after=()):
            slot = branch[0] + slot
            if slot not in dsems:
                dsems[slot] = DmaSem("d_" + slot)
            d = dsems[slot]
            if d.n:
                q.wait((d.sem, 16 * d.n))
            q.wait(*after)
            q.eng.dma_start(o, i).then_inc(d.sem, 16)
            d.n += 1
            return (d.sem, 16 * d.n)

        @contextmanager
        def branch_of(cond):
            qs = (P, V, A, G, S)
            kept = [(q.sem, q.n, dict(q.seen)) for q in qs]
            kept_free = (list(bank_free), dict(slot_free))
            branch[0] = "b_"
            with nc.If(cond):
                for q, nm in zip(qs, ("pe_b", "dve_b", "act_b", "pool_b", "sp_b")):
                    q.sem, q.n = sem(nm), 0
                yield
                ends = now() + [(d.sem, 16 * d.n) for nm, d in dsems.items() if nm.startswith("b_")]
                for q in qs:
                    q.wait(*ends)
            for q, (s_, n_, seen) in zip(qs, kept):
                q.sem, q.n, q.seen = s_, n_, seen
            bank_free[:] = kept_free[0]
            slot_free.clear()
            slot_free.update(kept_free[1])
            branch[0] = ""

        def now():
            return [q.last for q in (P, V, A, G)]

        area = [ExitStack(), None]
        ctx.callback(lambda: area[0].close())

        def layout(*parts):
            area[0].close()
            area[0] = ExitStack()
            assert sum(n for _, n, _ in parts) <= 9 * SL
            return [area[0].enter_context(nc.sbuf_tensor(nm, [128, n], ty)) for nm, n, ty in parts]

        area[1], = layout(("BIG", 9 * SL, F32))

        def slot(i, n=1):
            if i < 2:
                return XR[:, i * SL:(i + n) * SL]
            return area[1][:, (i - 2) * SL:(i - 2 + n) * SL]

        def C(name):
            a, n = CONSTS[name]
            return CT[:, a:a + n]

        def v(fn, *a, after=(), **k):
            V.wait(*after)
            return V.mark(fn(*a, **k))

        def a_(fn, *a, after=(), **k):
            A.wait(*after)
            return A.mark(fn(*a, **k))

        def g_(fn, *a, after=(), **k):
            G.wait(*after)
            return G.mark(fn(*a, **k))

        def vc(fn, *a, after=(), **k):
            return v(fn, *a, after=[V.last, *after], **k)

        def ac(fn, *a, after=(), **k):
            return a_(fn, *a, after=[A.last, *after], **k)

        bank_free = [None] * 8

        def mm(bank, o, pairs, after=(), start=True):
            P.wait(bank_free[bank], *after)
            for n, (l, r) in enumerate(pairs):
                ins = nc.tensor.matmul(o, l, r, start=(start and n == 0), stop=(n == len(pairs) - 1),
                                       skip_group_check=True)
            return P.mark(ins)

        def tr(bank, outs_ins, after=()):
            P.wait(bank_free[bank], *after)
            for o, i in outs_ins:
                k = i.shape[0]
                ins = nc.tensor.transpose(o, i, C("ident")[0:k, 0:k])
            return P.mark(ins)

        slot_free = {i: None for i in range(11)}

        def wload(s, src, n=None, off=0, after=()):
            k, n = src.shape[0] // 128, src.shape[1]
            view = slot(s)[:, off:off + k * n].rearrange("p (k n) -> p k n", k=k)
            t = dma(S, f"s{s}_{off}", view, src.rearrange("(k p) n -> p k n", p=128), [slot_free[s], *after])
            return view, t

        st_at = [0]
        st_names = {}

        def st(name, n):
            if name not in st_names:
                st_names[name] = (st_at[0], n)
                st_at[0] += n
                assert st_at[0] <= 1344, st_at
            a, m = st_names[name]
            assert m == n
            return ST[:, a:a + n]

        XRES = slot(0, 2).rearrange("p (t d) -> p t d", t=8)
        XT = slot(2, 2).rearrange("p (c n) -> p c n", c=8)
        U = slot(4, 2).rearrange("p (t d) -> p t d", t=8)

        def bc(i):
            return BC[:, i * 1024:(i + 1) * 1024]

        t_cst = dma(A, "cst", CT[:, :], cst)
        cols, col_at, t_cols = {}, 0, []
        ROWS = slot(10)[:, 3072:3200]
        COLS = st("cols", 83)
        x_in = X["x"][0].rearrange("(t p) d -> p t d", p=128)
        t_x = [dma(A, f"x{t}", XRES[:, t, :], x_in[:, t, :]) for t in range(8)]
        for name, src in (("c", X["c"][0]), ("lng", X["ln_in_g"]), ("lnb", X["ln_in_b"]), ("l1g", X["ln1_g"][0]),
                          ("l1b", X["ln1_b"][0]), ("nmix", X["norm_mix_2"][0]), ("ncr", X["norm_cross_2"][0]),
                          ("nmem", X["norm_mem_2"][0]), ("nffn", X["norm_ffn_2"][0]), ("gq", X["mla_q_norm"][0]),
                          ("gkv", X["mla_kv_norm"][0]), ("cqn", X["cross_q_norm_2"][0]),
                          ("ckn", X["cross_k_norm_2"][0]), ("daon", X["da_out_norm_2"][0]),
                          ("glon", X["gla_out_norm_2"][0])):
            k = src.shape[0] // 128
            t_cols.append(dma(S, "col_" + name, ROWS[col_at:col_at + k, :], src.rearrange("(k p) -> k p", p=128)))
            cols[name] = COLS[:, col_at:col_at + k]
            col_at += k
        for name, src in (("daq", "da_q_norm_2"), ("dak", "da_k_norm_2")):
            for h in range(2):
                t_cols.append(dma(S, f"col_{name}{h}", ROWS[col_at:col_at + 1, 64 * h:64 * h + 64],
                                  X[src][0].rearrange("(k p) -> k p", k=1)))
            cols[name] = COLS[:, col_at:col_at + 1]
            col_at += 1
        POSI = slot(10)[0:8, 3200:3328].bitcast(I32)
        POSR = slot(10)[0:8, 3328:3456]
        t_pos = dma(S, "pos", POSI, X["positions"][0].rearrange("(t p) -> t p", p=128))
        lam4 = BC[:, 2048:2048 + 256].rearrange("p (a n) -> p a n", a=4)
        t_lam = [dma(G, f"lam{n}", lam4[:, n, :], X[s][0].partition_broadcast(128))
                 for n, s in enumerate(("lambda_q1_2", "lambda_k1_2", "lambda_q2_2", "lambda_k2_2"))]
        posf = st("posf", 8)
        P.wait(t_cst, *t_cols)
        nc.tensor.transpose(PS[:, 7, 0:83], ROWS[0:83, :], C("ident")[0:83, 0:83])
        r = v(nc.vector.tensor_copy, POSR, POSI, after=[t_pos])
        p_ = tr(7, [(PS[:, 7, 128:136], POSR)], after=[r])
        v(nc.vector.tensor_copy, COLS, PS[:, 7, 0:83], after=[p_])
        bank_free[7] = v(nc.vector.tensor_copy, posf, PS[:, 7, 128:136])
        V.wait(t_cst, *t_lam, V.last)
        A.wait(t_cst, V.last)

        lamp = BC[:, 3072:3072 + 128].rearrange("p (a n) -> p a n", a=2)
        ls = st("ls", 2)
        v(nc.vector.tensor_tensor, lamp, lam4[:, 0:4:2, :], lam4[:, 1:4:2, :], ALU.mult)
        vc(nc.vector.tensor_reduce, ls, lamp, AX, ALU.add)
        le = st("le", 2)
        a_(nc.scalar.activation, le, ls, ACT.Exp, after=[V.last])
        nlam = st("nlam", 1)
        v(nc.vector.tensor_scalar, nlam, le[:, 1:2], le[:, 0:1], -0.2, ALU.subtract, ALU.add, after=[A.last])

        ce, cs = st("ce", 8), st("cs", 8)
        a_(nc.scalar.activation, ce, cols["c"], ACT.Exp, scale=-1.0)
        v(nc.vector.tensor_scalar, ce, ce, 1.0, None, ALU.add, after=[A.last])
        vc(nc.vector.reciprocal, ce, ce)
        vc(nc.vector.tensor_tensor, cs, ce, cols["c"], ALU.mult)
        CB = slot(10)[:, 0:1024].rearrange("p (k n) -> p k n", k=8)
        t_cb = vc(nc.vector.tensor_copy, CB, cs.unsqueeze(2).to_broadcast([128, 8, 128]))

        RA = slot(9)[:, 0:384].rearrange("p (t n) -> p t n", t=8)
        RK = slot(9)[:, 384:768].rearrange("p (t n) -> p t n", t=8)
        COS = CSN[:, 0:384].rearrange("p (t n) -> p t n", t=8)
        SIN = CSN[:, 384:768].rearrange("p (t n) -> p t n", t=8)
        V.wait(V.last)
        for t in range(8):
            v(nc.vector.tensor_scalar, RA[:, t, :], C("inv"), posf[:, t:t + 1], None, ALU.mult)
        MAGIC = 12582912.0
        vc(nc.vector.tensor_scalar, RK, RA, 1.0 / (2 * math.pi), MAGIC, ALU.mult, ALU.add)
        vc(nc.vector.tensor_scalar, RK, RK, MAGIC, None, ALU.subtract)
        C1 = 6.28125
        C2 = float(np.float32(np.floor((2 * math.pi - C1) * 2 ** 20) / 2 ** 20))
        C3 = float(np.float32(2 * math.pi - C1 - C2))
        for c in (C1, C2, C3):
            vc(nc.vector.scalar_tensor_tensor, out=RA, in0=RK, scalar=-c, in1=RA, op0=ALU.mult, op1=ALU.add)
        PI = float(np.float32(3.1415925))
        vc(nc.vector.tensor_scalar, RA, RA, PI, -PI, ALU.min, ALU.max)
        t_ra = V.last
        a_(nc.scalar.activation, SIN[:, :, :], RA, ACT.Sin, after=[t_ra])
        vc(nc.vector.scalar_tensor_tensor, out=RK, in0=RA, scalar=-1.0, in1=RA, op0=ALU.mult, op1=ALU.max)
        vc(nc.vector.tensor_scalar, RK, RK, -1.0, math.pi / 2, ALU.mult, ALU.add)
        t_cos = a_(nc.scalar.activation, COS[:, :, :], RK, ACT.Sin, after=[V.last])
        COSR, SINR = COS[:, :, 0:32], SIN[:, :, 0:32]
        COSM, SINM = COS[:, :, 32:48], SIN[:, :, 32:48]

        def rsqrt(o, x, scale, eps, after=()):
            t = v(nc.vector.tensor_scalar, o, x, scale, eps, ALU.mult, ALU.add, after=after)
            t = a_(nc.scalar.activation, o, o, ACT.Sqrt, after=[t])
            return v(nc.vector.reciprocal, o, o, after=[t])

        bst = st("bst", 12).rearrange("p (a n) -> p a n", a=2)
        mv = st("mv", 16).rearrange("p (t n) -> p t n", t=8)
        rst = st("rst", 8)

        def layer_norm_z(ready):
            for t in range(8):
                for h in range(2):
                    v(nc.vector.bn_stats, bst[:, h, :], XRES[:, t, 512 * h:512 * h + 512],
                      after=[ready[t], V.last])
                vc(nc.vector.bn_aggr, mv[:, t, :], bst)
            r = rsqrt(rst, mv[:, :, 1], 1.0, EPS, [V.last])
            return [v(nc.vector.tensor_scalar, XRES[:, t, :], XRES[:, t, :], mv[:, t, 0:1], rst[:, t:t + 1],
                      ALU.subtract, ALU.mult, after=[r]) for t in range(8)]

        def to_fm(src, scales, biases, ready, banks=(0, 1, 2, 3)):
            toks, ptoks, n = [], [], 0
            for th in range(2):
                for c in range(8):
                    b = banks[n % len(banks)]
                    t = tr(b, [(PS[:, b, 128 * u:128 * u + 128], src(4 * th + u, c)) for u in range(4)],
                           after=[ready[4 * th + u] for u in range(4)])
                    ptoks.append(t)
                    o = XT[:, c, 512 * th:512 * th + 512]
                    if n % 2 == 0:
                        kw = {"scale": scales(c)}
                        if biases:
                            kw["bias"] = biases(c)
                        r = a_(nc.scalar.activation, o, PS[:, b, :], ACT.Identity, after=[t], **kw)
                    elif biases:
                        r = v(nc.vector.tensor_scalar, o, PS[:, b, :], scales(c), biases(c), ALU.mult, ALU.add,
                              after=[t])
                    else:
                        r = v(nc.vector.tensor_scalar, o, PS[:, b, :], scales(c), None, ALU.mult, after=[t])
                    bank_free[b] = r
                    toks.append(r)
                    n += 1
            return toks, ptoks

        MODT = st("modt", 32)
        GT1, GT2 = bc(0), bc(1)
        w_ada, b_ada = X["w_ada"][0], X["b_ada"][0]
        BADA = slot(10)[:, 1024:1024 + 1024].rearrange("p (b n) -> p b n", b=2)
        MROW = slot(10)[:, 2048:2048 + 1024].rearrange("p (b n) -> p b n", b=2)
        mrow_free = [None, None]
        bada_free = [None, None]
        for n, ch in enumerate([0, 1, 2, 3, 4, 5, 6, 7, 8, 9, 10, 11]):
            sl = 6 + n % 3
            w, tw = wload(sl, w_ada[:, 512 * ch:512 * ch + 512])
            tb = dma(A, f"bada{n % 2}", BADA[:, n % 2, :], b_ada[512 * ch:512 * ch + 512].partition_broadcast(128),
                     after=[bada_free[n % 2]])
            b = 4 + n % 2
            t = mm(b, PS[:, b, :], [(CB[:, k, :], w[:, k, :]) for k in range(8)], after=[tw, t_cb])
            slot_free[sl] = t
            vec, half = ch // 2, ch % 2
            if vec in (2, 5):
                o = (GT1 if vec == 2 else GT2)[:, 512 * half:512 * half + 512]
                r = v(nc.vector.tensor_tensor, o, PS[:, b, :], BADA[:, n % 2, :], ALU.add, after=[t, tb])
                bank_free[b] = bada_free[n % 2] = r
            else:
                o = MROW[:, n % 2, :]
                r = v(nc.vector.tensor_tensor, o, PS[:, b, :], BADA[:, n % 2, :], ALU.add,
                      after=[t, tb, mrow_free[n % 2]])
                bank_free[b] = bada_free[n % 2] = r
                t = tr(6, [(PS[:, 6, 128 * u:128 * u + 128], o[:, 128 * u:128 * u + 128]) for u in range(4)], after=[r])
                mrow_free[n % 2] = t
                at = 8 * {0: 0, 1: 1, 3: 2, 4: 3}[vec] + 4 * half
                bank_free[6] = v(nc.vector.tensor_copy, MODT[:, at:at + 4], PS[:, 6, 0:512:128], after=[t])

        def mod_cols(tag, g, b, sh, sc):
            A1, B1 = st("A" + tag, 8), st("B" + tag, 8)
            one_sc = st("osc" + tag, 8)
            vc(nc.vector.tensor_scalar, one_sc, sc, 1.0, None, ALU.add)
            vc(nc.vector.tensor_tensor, A1, g, one_sc, ALU.mult)
            vc(nc.vector.tensor_tensor, B1, b, one_sc, ALU.mult)
            vc(nc.vector.tensor_tensor, B1, B1, sh, ALU.add)
            return A1, B1

        A1, B1 = mod_cols("1", cols["lng"], cols["lnb"], MODT[:, 0:8], MODT[:, 8:16])
        A2, B2 = mod_cols("2", cols["l1g"], cols["l1b"], MODT[:, 16:24], MODT[:, 24:32])

        z = layer_norm_z(t_x)
        t_bc2 = dma(G, "bc2", bc(2), X["ln_in_g"].partition_broadcast(128), after=now())
        t_bc3 = dma(G, "bc3", bc(3), X["ln_in_b"].partition_broadcast(128), after=now())
        xt1, xt1p = to_fm(lambda t, c: XRES[:, t, 128 * c:128 * c + 128], lambda c: A1[:, c:c + 1],
                          lambda c: B1[:, c:c + 1], z + [])

        def affine_pool(ready, gb, gbt, bb, bbt):
            toks = []
            G.wait(*ready)
            for t in range(8):
                r = g_(nc.gpsimd.tensor_tensor, XRES[:, t, :], XRES[:, t, :], gb, ALU.mult, after=[gbt])
                toks.append(g_(nc.gpsimd.tensor_tensor, XRES[:, t, :], XRES[:, t, :], bb, ALU.add, after=[r, bbt]))
            return toks

        x0 = affine_pool(xt1p, bc(2), t_bc2, bc(3), t_bc3)

        w_in = X["w_in"][0]
        LAT = slot(10)[:, 0:8 * 416].rearrange("p (t n) -> p t n", t=8)
        V.wait(*now())
        A.wait(*now())
        w, tw = wload(6, w_in[:, 0:416])
        lss = st("lss", 16).rearrange("p (t n) -> p t n", t=8)
        TMP = slot(9)[:, 0:2048]
        for t in range(8):
            b = t % 4
            tk = mm(b, PS[:, b, 0:416], [(XT[:, k, 128 * t:128 * t + 128], w[:, k, :]) for k in range(8)],
                    after=[tw, xt1])
            a_(nc.scalar.activation, TMP[:, 0:256], PS[:, b, 0:256], ACT.Square, accum_out=lss[:, t, 0:1],
               after=[tk, A.last])
            r1 = ac(nc.scalar.activation, TMP[:, 0:128], PS[:, b, 256:384], ACT.Square, accum_out=lss[:, t, 1:2])
            r2 = v(nc.vector.tensor_copy, LAT[:, t, :], PS[:, b, 0:416], after=[tk, r1])
            bank_free[b] = r2
        slot_free[6] = P.last
        lr = st("lr", 16).rearrange("p (t n) -> p t n", t=8)
        v(nc.vector.tensor_scalar, lr[:, :, 0], lss[:, :, 0], 1.0 / 256, EPS, ALU.mult, ALU.add, after=[A.last])
        v(nc.vector.tensor_scalar, lr[:, :, 1], lss[:, :, 1], 1.0 / 128, EPS, ALU.mult, ALU.add)
        a_(nc.scalar.activation, lr, lr, ACT.Sqrt, after=[V.last])
        v(nc.vector.reciprocal, lr, lr, after=[A.last])
        V.wait(V.last)
        for t in range(8):
            v(nc.vector.tensor_scalar, LAT[:, t, 0:256], LAT[:, t, 0:256], lr[:, t, 0:1], None, ALU.mult)
            v(nc.vector.tensor_scalar, LAT[:, t, 256:384], LAT[:, t, 256:384], lr[:, t, 1:2], None, ALU.mult)
        t_latn = V.last
        KR = st("kr", 256).rearrange("p (t n) -> p t n", t=8)
        T1 = TMP[:, 256:384].rearrange("p (t n) -> p t n", t=8)
        T2 = TMP[:, 384:512].rearrange("p (t n) -> p t n", t=8)
        V.wait(t_cos)

        def rotate(o1, o2, x1, x2, co, si, t1, t2, after=()):
            v(nc.vector.tensor_tensor, t1, x1, co, ALU.mult, after=[V.last, *after])
            v(nc.vector.tensor_tensor, t2, x2, si, ALU.mult)
            vc(nc.vector.tensor_tensor, o1, t1, t2, ALU.subtract)
            v(nc.vector.tensor_tensor, t1, x2, co, ALU.mult, after=[V.last])
            v(nc.vector.tensor_tensor, t2, x1, si, ALU.mult)
            return vc(nc.vector.tensor_tensor, o2, t1, t2, ALU.add)

        t_kr = rotate(KR[:, :, 0:16], KR[:, :, 16:32], LAT[:, :, 384:400], LAT[:, :, 400:416], COSM, SINM, T1, T2)

        wqk, tqk = wload(7, w_in[:, 416:928])
        wv, twv = wload(8, w_in[:, 928:1440])
        wg, twg = wload(6, w_in[:, 1440:1952])
        SG = slot(4).rearrange("p (t n) -> p t n", t=8)
        RO = slot(5).rearrange("p (t n) -> p t n", t=8)
        R = slot(9)
        QK, RQK = R[:, 0:512], R[:, 512:1024]
        TA, TB = R[:, 1024:1280], R[:, 1280:1536]
        QKT = R[0:64, 1536:2560]
        SC = R[:, 2560:3072]
        KZ = R[:, 3072:3328]
        STA = R[0:64, 3328:3840]
        VT = slot(10)[:, 3328:3840]
        V.wait(V.last)
        v(nc.vector.memset, STA, 0.0)
        mvr = st("mvr", 64).rearrange("p (t n) -> p t n", t=8)
        bs4 = st("bs4", 24).rearrange("p (h n) -> p h n", h=4)
        st_free = [None]

        def b4(ap, n, parts=128):
            return ap.unsqueeze(2).to_broadcast([parts, ap.shape[1], n])

        def silu_into(o, ps, after):
            t = a_(nc.scalar.activation, o, ps, ACT.Exp, scale=-1.0, after=after)
            t = v(nc.vector.tensor_scalar, o, o, 1.0, None, ALU.add, after=[t])
            t = v(nc.vector.reciprocal, o, o, after=[t])
            return v(nc.vector.tensor_tensor, o, o, ps, ALU.mult, after=[t])

        t_inner = t_kvm = None
        for t in range(8):
            xt = [XT[:, k, 128 * t:128 * t + 128] for k in range(8)]
            p0 = mm(0, PS[:, 0, :], [(xt[k], wqk[:, k, :]) for k in range(8)], after=[tqk])
            p1 = mm(1, PS[:, 1, :], [(xt[k], wv[:, k, :]) for k in range(8)], after=[twv])
            p2 = mm(2, PS[:, 2, :], [(xt[k], wg[:, k, :]) for k in range(8)], after=[twg])
            bank_free[0] = a_(nc.scalar.copy, QK, PS[:, 0, :], after=[p0, V.last])
            tqk_ = bank_free[0]
            tv = bank_free[1] = a_(nc.scalar.copy, VT, PS[:, 1, :], after=[p1, t_inner, t_kvm])
            q3 = QK.rearrange("p (h n) -> p h n", h=8)
            r3 = RQK.rearrange("p (h n) -> p h n", h=8)
            co = COSR[:, t, :].unsqueeze(1).to_broadcast([128, 8, 32])
            si = SINR[:, t, :].unsqueeze(1).to_broadcast([128, 8, 32])
            ta = TA.rearrange("p (h n) -> p h n", h=8)
            tb = TB.rearrange("p (h n) -> p h n", h=8)
            tr_ = rotate(r3[:, :, 0:32], r3[:, :, 32:64], q3[:, :, 0:32], q3[:, :, 32:64], co, si, ta, tb,
                         after=[tqk_, P.last])
            pq = tr(3, [(PS[0:64, 3, 128 * h:128 * h + 128], RQK[:, 64 * h:64 * h + 64]) for h in range(4)], [tr_])
            pk = tr(4, [(PS[0:64, 4, 128 * h:128 * h + 128], RQK[:, 256 + 64 * h:320 + 64 * h]) for h in range(4)])
            bank_free[3] = eq = a_(nc.scalar.copy, QKT[:, 0:512], PS[0:64, 3, :], after=[pq])
            bank_free[4] = ek = a_(nc.scalar.copy, QKT[:, 512:1024], PS[0:64, 4, :], after=[pk])
            tkz = v(nc.vector.tensor_tensor, KZ.rearrange("p (h n) -> p h n", h=4),
                    RQK[:, 256:512].rearrange("p (h n) -> p h n", h=4), b4(C("zet"), 64), ALU.mult, after=[t_kvm, tr_])
            for h in range(4):
                ps_ = mm(5, PS[:, 5, 128 * h:128 * h + 128],
                         [(QKT[:, 512 + 128 * h:640 + 128 * h], QKT[:, 128 * h:128 * h + 128])], after=[eq, ek])
            for h in range(4):
                pc = mm(6, PS[:, 6, 128 * h:128 * h + 128],
                        [(QKT[:, 128 * h:128 * h + 128], STA[:, 128 * h:128 * h + 128])], after=[st_free[0], V.last])
            tsc = bank_free[5] = v(nc.vector.tensor_tensor, SC, PS[:, 5, :], C("dec"), ALU.mult, after=[ps_])
            for h in range(4):
                t_kvm = mm(3, PS[0:64, 3, 128 * h:128 * h + 128],
                           [(KZ[:, 64 * h:64 * h + 64], VT[:, 128 * h:128 * h + 128])], after=[tkz, tv])
            for h in range(4):
                t_inner = mm(7, PS[:, 7, 128 * h:128 * h + 128],
                             [(SC[:, 128 * h:128 * h + 128], VT[:, 128 * h:128 * h + 128])], after=[tsc])
            s4 = STA.rearrange("p (h n) -> p h n", h=4)
            v(nc.vector.tensor_tensor, s4, s4, b4(C("gc")[0:64, :], 128, 64), ALU.mult, after=[pc, V.last])
            st_free[0] = bank_free[3] = vc(nc.vector.tensor_tensor, STA, STA, PS[0:64, 3, :], ALU.add, after=[t_kvm])
            o3 = RO[:, t, :].rearrange("p (h n) -> p h n", h=4)
            bank_free[6] = v(nc.vector.tensor_tensor, o3, PS[:, 6, :].rearrange("p (h n) -> p h n", h=4),
                             b4(C("xi"), 128), ALU.mult, after=[pc])
            bank_free[7] = vc(nc.vector.tensor_tensor, RO[:, t, :], RO[:, t, :], PS[:, 7, :], ALU.add,
                              after=[t_inner])
            V.wait(V.last)
            for h in range(4):
                v(nc.vector.bn_stats, bs4[:, h, :], o3[:, h, :])
            V.wait(V.last)
            for h in range(4):
                v(nc.vector.bn_aggr, mvr[:, t, 2 * h:2 * h + 2], bs4[:, h, :])
            bank_free[2] = silu_into(SG[:, t, :], PS[:, 2, :], [p2])
        slot_free[6] = slot_free[7] = slot_free[8] = P.last
        t_xt_free = P.last
        rsr = st("rsr", 32)
        mvr2 = mvr.rearrange("p t (h n) -> p (t h) n", n=2)
        tr_ = rsqrt(rsr, mvr2[:, :, 1], 1.0, EPS, [V.last])
        G.wait(*x0)
        t_gn = [dma(G, "bc2", bc(2)[:, 0:512], X["ret_gn_g"][0].partition_broadcast(128), after=x0),
                dma(G, "gnb", bc(2)[:, 512:1024], X["ret_gn_b"][0].partition_broadcast(128), after=x0)]
        for t in range(8):
            o3 = RO[:, t, :].rearrange("p (h n) -> p h n", h=4)
            m = mvr2[:, 4 * t:4 * t + 4, 0]
            vc(nc.vector.tensor_tensor, o3, o3, b4(m, 128), ALU.subtract)
            vc(nc.vector.tensor_tensor, o3, o3, b4(rsr[:, 4 * t:4 * t + 4], 128), ALU.mult)
            vc(nc.vector.tensor_tensor, RO[:, t, :], RO[:, t, :], bc(2)[:, 0:512], ALU.mult, after=t_gn)
            vc(nc.vector.tensor_tensor, RO[:, t, :], RO[:, t, :], bc(2)[:, 512:1024], ALU.add)
            vc(nc.vector.tensor_tensor, RO[:, t, :], RO[:, t, :], SG[:, t, :], ALU.mult)
        t_ro = V.last

        QNT = slot(9)[:, 0:2048].rearrange("p (c n) -> p c n", c=2)
        VA = slot(9)[:, 2048:4096].rearrange("p (t n) -> p t n", t=8)
        KVT = bc(3)
        QT = slot(2).rearrange("p (h n) -> p h n", h=4)
        KT = slot(3).rearrange("p (h n) -> p h n", h=4)
        A.wait(*now())
        V.wait(*now())
        n = 0
        lat_t = []
        for c in range(3):
            for th in range(2):
                b = n % 2
                t = tr(b, [(PS[:, b, 128 * u:128 * u + 128], LAT[:, 4 * th + u, 128 * c:128 * c + 128])
                           for u in range(4)], after=[t_latn])
                o = (QNT[:, c, :] if c < 2 else KVT)[:, 512 * th:512 * th + 512]
                sc = cols["gq"][:, c:c + 1] if c < 2 else cols["gkv"][:, 0:1]
                bank_free[b] = a_(nc.scalar.activation, o, PS[:, b, :], ACT.Copy, scale=sc, after=[t])
                lat_t.append(A.last)
                n += 1
        wu = slot(6)[:, 0:1536].rearrange("p (k n) -> p k n", k=2)
        twu = dma(S, "s6_0", wu, X["w_uq"][0].rearrange("(k p) n -> p k n", p=128), [slot_free[6]])
        wk = slot(6)[:, 1536:2560]
        twk = dma(S, "s6_b", wk, X["w_ukv"][0], [slot_free[6]])
        QTM = slot(10)[:, 0:384].rearrange("p (h n) -> p h n", h=4)
        KTM = slot(10)[:, 384:768].rearrange("p (h n) -> p h n", h=4)
        MT1 = slot(10)[:, 768:832].rearrange("p (h n) -> p h n", h=4)
        MT2 = slot(10)[:, 832:896].rearrange("p (h n) -> p h n", h=4)
        PB = [slot(10)[:, 0:1024], slot(10)[:, 1024:2048]]
        PTB = [slot(10)[:, 2048:3072], slot(10)[:, 3072:4096]]
        AO = slot(4).rearrange("p (t n) -> p t n", t=8)

        sm = st("sm", 32)

        def attention(items, qk, mask, scale, PBUF, PTBUF, vsrc, ov, out_fn, nmap=1, combine=None):
            p_free = [[None] * nmap, [None] * nmap]
            pt_free = [None, None]
            S_t, P_t, T_t = {}, {}, {}
            sm_n = [0]
            for n in range(len(items) + 2):
                if n < len(items):
                    h, i = items[n]
                    nk = 128 * (i + 1)
                    P_t[n] = []
                    for m in range(nmap):
                        sb = 2 * (n % 2) if nmap == 1 else 2 * m
                        tq = None
                        for c0 in range(0, nk, 512):
                            c1 = min(nk, c0 + 512)
                            b = sb + c0 // 512
                            tq = mm(b, PS[:, b, 0:c1 - c0], [qk(h, i, m, c0, c1)])
                        flat = PS[:, sb:sb + 2, :].rearrange("p b n -> p (b n)")
                        d = flat[:, nk - 128:nk]
                        t = v(nc.vector.tensor_tensor, d, d, mask, ALU.add, after=[tq])
                        k = 4 * (sm_n[0] % 8)
                        sm_n[0] += 1
                        mx, bi, rs, ri = (sm[:, k + z:k + z + 1] for z in range(4))
                        vc(nc.vector.tensor_reduce, mx, flat[:, 0:nk], AX, ALU.max)
                        t = vc(nc.vector.tensor_scalar, bi, mx, -scale, None, ALU.mult)
                        pb = PBUF[n % 2][m]
                        t = a_(nc.scalar.activation, pb[:, 0:nk], flat[:, 0:nk], ACT.Exp, bias=bi, scale=scale,
                               accum_out=rs, after=[t, p_free[n % 2][m]])
                        bank_free[sb] = bank_free[sb + 1] = t
                        t = v(nc.vector.reciprocal, ri, rs, after=[t])
                        P_t[n].append((t, ri))
                    if combine:
                        src, t = combine(n, nk, P_t[n])
                    else:
                        src, t = PBUF[n % 2][0], P_t[n][0][0]
                    S_t[n] = (src, t)
                if 1 <= n <= len(items):
                    k = n - 1
                    h, i = items[k]
                    src, ts = S_t[k]
                    T_t[k] = []
                    for g0 in range(0, i + 1, 4):
                        g1 = min(i + 1, g0 + 4)
                        b = 4 + (g0 // 4)
                        t = tr(b, [(PS[:, b, 128 * (j - g0):128 * (j - g0) + 128], src[:, 128 * j:128 * j + 128])
                                   for j in range(g0, g1)], after=[ts])
                        o = PTBUF[k % 2][:, 128 * g0:128 * g1]
                        w_ = 128 * (g1 - g0)
                        if g0 == 0:
                            r = a_(nc.scalar.copy, o, PS[:, b, 0:w_], after=[t, pt_free[k % 2]])
                        else:
                            r = v(nc.vector.tensor_copy, o, PS[:, b, 0:w_], after=[t, pt_free[k % 2]])
                        bank_free[b] = r
                        T_t[k].append(r)
                    for m in range(nmap):
                        p_free[k % 2][m] = P.last
                    if combine:
                        combine.free[k % 2] = P.last
                if n >= 2:
                    k = n - 2
                    h, i = items[k]
                    b = 6 + k % 2
                    t = mm(b, PS[:, b, 0:ov], [(PTBUF[k % 2][:, 128 * j:128 * j + 128], vsrc(h, j))
                                               for j in range(i + 1)], after=[T_t[k]])
                    pt_free[k % 2] = t
                    bank_free[b] = out_fn(h, i, PS[:, b, 0:ov], t, P_t[k])

        for g in range(2):
            A.wait(*now())
            V.wait(*now())
            tm_free = None
            for t in range(8):
                pq = mm(0, PS[:, 0, 0:384], [(QNT[:, k, 128 * t:128 * t + 128], wu[:, k, 384 * g:384 * g + 384])
                                            for k in range(2)], after=[twu, lat_t])
                pk = mm(1, PS[:, 1, :], [(KVT[:, 128 * t:128 * t + 128], wk[:, 512 * g:512 * g + 512])], after=[twk])
                q3 = PS[:, 0, 0:384].rearrange("p (h n) -> p h n", h=4)
                k3 = PS[:, 1, :].rearrange("p (h n) -> p h n", h=4)
                a_(nc.scalar.copy, QTM[:, :, 0:64], q3[:, :, 0:64], after=[pq, tm_free])
                a_(nc.scalar.copy, KTM[:, :, 0:64], k3[:, :, 0:64], after=[pk])
                a_(nc.scalar.copy, KTM[:, :, 64:96], KR[:, t, :].unsqueeze(1).to_broadcast([128, 4, 32]), after=[t_kr])
                bank_free[1] = a_(nc.scalar.copy, VA[:, t, :].rearrange("p (h n) -> p h n", h=4),
                                        k3[:, :, 64:128])
                co = COSM[:, t, :].unsqueeze(1).to_broadcast([128, 4, 16])
                si = SINM[:, t, :].unsqueeze(1).to_broadcast([128, 4, 16])
                r = rotate(QTM[:, :, 64:80], QTM[:, :, 80:96], q3[:, :, 64:80], q3[:, :, 80:96], co, si, MT1, MT2,
                           after=[pq, A.last, tm_free])
                bank_free[0] = r
                p1 = tr(2, [(PS[0:96, 2, 128 * h:128 * h + 128], QTM[:, h, :]) for h in range(4)], after=[r, A.last])
                p2 = tr(3, [(PS[0:96, 3, 128 * h:128 * h + 128], KTM[:, h, :]) for h in range(4)])
                tm_free = p2
                bank_free[2] = a_(nc.scalar.copy, QT[0:96, :, 128 * t:128 * t + 128],
                                  PS[0:96, 2, :].rearrange("p (h n) -> p h n", h=4), after=[p1])
                bank_free[3] = v(nc.vector.tensor_copy, KT[0:96, :, 128 * t:128 * t + 128],
                                 PS[0:96, 3, :].rearrange("p (h n) -> p h n", h=4), after=[p2])
            A.wait(*now())
            V.wait(*now())
            P.wait(*now())

            def mla_qk(h, i, m, c0, c1):
                return (QT[0:96, h, 128 * i:128 * i + 128], KT[0:96, h, c0:c1])

            def mla_out(h, i, o, t, pt):
                o = o[:, 64 * (h % 2):64 * (h % 2) + 64]
                return v(nc.vector.tensor_scalar, AO[:, i, 256 * g + 64 * h:256 * g + 64 * h + 64], o, pt[0][1], None,
                         ALU.mult, after=[t, pt[0][0]])

            attention([(h, i) for h in range(4) for i in range(8)], mla_qk, C("caus"), 96.0 ** -0.5,
                      [[PB[0]], [PB[1]]], PTB, lambda h, j: VA[:, j, 128 * (h // 2):128 * (h // 2) + 128], 128, mla_out)
        slot_free[6] = P.last

        def project(wd, src_t, evac, ready, slots=(6, 7, 8), banks=(4, 5, 6, 7)):
            n_ = 0
            last = {}
            for n in range(wd.shape[1] // 512):
                s = slots[n % len(slots)]
                w, tw = wload(s, wd[:, 512 * n:512 * n + 512])
                for t in range(8):
                    b = banks[n_ % len(banks)]
                    n_ += 1
                    tk = mm(b, PS[:, b, :], [(src_t(k, t), w[:, k, :]) for k in range(8)], after=[tw, ready])
                    last[t] = bank_free[b] = evac(t, n, PS[:, b, :], tk)
                slot_free[s] = P.last
            return [last[t] for t in range(8)]

        A.wait(*now())
        V.wait(*now())
        MIX = [slot(4).rearrange("p (t n) -> p t n", t=8), slot(5).rearrange("p (t n) -> p t n", t=8)]
        one1 = C("one")[:, 0:1]
        mt, _ = to_fm(lambda t, c: MIX[c // 4][:, t, 128 * (c % 4):128 * (c % 4) + 128], lambda c: one1, None,
                      [now()] * 8)
        PT_ = [slot(10)[:, 512 * i:512 * i + 512] for i in range(4)]

        def residual(gt, alpha, ready, tmp):
            k = [0]

            def f(t, n, ps, tk):
                x = XRES[:, t, 512 * n:512 * n + 512]
                o = tmp[k[0] % len(tmp)]
                k[0] += 1
                r = v(nc.vector.tensor_tensor, o, ps, gt[:, 512 * n:512 * n + 512], ALU.mult, after=[tk, ready])
                if alpha is None:
                    vc(nc.vector.tensor_tensor, x, x, o, ALU.add)
                else:
                    vc(nc.vector.scalar_tensor_tensor, out=x, in0=x, scalar=alpha, in1=o, op0=ALU.mult, op1=ALU.add)
                return V.last
            return f

        xr = project(X["w_out"][0], lambda k, t: XT[:, k, 128 * t:128 * t + 128], residual(GT1, ALPHA, x0, PT_), mt)
        z = layer_norm_z(xr)
        t_bc2 = dma(G, "bc2", bc(2), X["ln1_g"][0].partition_broadcast(128), after=now())
        t_bc3 = dma(G, "bc3", bc(3), X["ln1_b"][0].partition_broadcast(128), after=now())
        A.wait(P.last)
        V.wait(P.last)
        FXH, FXL, FHH, FHL, FWR, FWH, FWL = layout(
            ("FXH", 2 * SL, F32R), ("FXL", 2 * SL, F32R), ("FHH", SL, F32R), ("FHL", SL, F32R),
            ("FWR", SL, F32), ("FWH", SL, F32R), ("FWL", SL, F32R))

        def split(hi, lo, x, after=(), hi_after=(), lo_after=()):
            t = a_(nc.scalar.copy, hi, x, after=[*after, *hi_after])
            return v(nc.vector.tensor_tensor, lo, x, hi.bitcast(F32), ALU.subtract, after=[t, *after, *lo_after])

        def mm3(bank, o, quads, after=(), start=True):
            pairs = []
            for lh, ll, rh, rl in quads:
                pairs += [(lh, rh), (ll, rh), (lh, rl)]
            return mm(bank, o, pairs, after=after, start=start)

        XHH = FXH[:, :].rearrange("p (c n) -> p c n", c=8)
        XLL = FXL[:, :].rearrange("p (c n) -> p c n", c=8)
        QB = [CSN[:, 0:512], C("dec")]
        qb_free = [None, None]
        qn = [0]
        xt2, xt2p = [], []
        pre = now()
        wr_free, wh_free = [pre] * 2, [pre] * 2
        w1, w2 = X["w_ff1"][0], X["w_ff2"][0]
        chunks = []
        for g in range(8):
            for cc in range(2):
                chunks.append(w1[:, 512 * g + 256 * cc:512 * g + 256 * cc + 256])
            for n in range(2):
                chunks.append(w2[512 * g:512 * g + 512, 512 * n:512 * n + 512])
        raw_t, cut_t = {}, {}

        def chunk(t_, i, k):
            return t_[:, 2048 * (i % 2):2048 * (i % 2) + 2048].rearrange("p (k n) -> p k n", k=k)

        def fetch(i):
            if i < len(chunks):
                k = 8 if i % 4 < 2 else 4
                raw_t[i] = dma(S, f"fw{i % 2}", chunk(FWR, i, k), chunks[i].rearrange("(k p) n -> p k n", p=128),
                               after=[wr_free[i % 2]])

        def cut(i):
            if i < len(chunks):
                o = (slice(None), slice(2048 * (i % 2), 2048 * (i % 2) + 2048))
                wr_free[i % 2] = cut_t[i] = split(FWH[o], FWL[o], FWR[o], after=[raw_t[i], wh_free[i % 2]])

        fetch(0)
        fetch(1)
        A.wait(pre)
        V.wait(pre)
        for th in range(2):
            for c in range(8):
                b = qn[0] % 4
                i_ = qn[0] % 2
                qn[0] += 1
                t = tr(b, [(PS[:, b, 128 * u:128 * u + 128], XRES[:, 4 * th + u, 128 * c:128 * c + 128])
                           for u in range(4)], after=[z[4 * th + u] for u in range(4)])
                xt2p.append(t)
                bank_free[b] = t = v(nc.vector.tensor_scalar, QB[i_], PS[:, b, :], A2[:, c:c + 1], B2[:, c:c + 1],
                                     ALU.mult, ALU.add, after=[t, qb_free[i_]])
                o = (slice(None), c, slice(512 * th, 512 * th + 512))
                qb_free[i_] = t = split(XHH[o], XLL[o], QB[i_], after=[t])
                xt2.append(t)
        x1 = affine_pool(xt2p, bc(2), t_bc2, bc(3), t_bc3)

        ZT = bc(2)
        g_(nc.gpsimd.memset, ZT, 0.0, after=x1)
        t_zy = dma(G, "zy", scr[2][32 * 128:, :].rearrange("(b p) d -> p b d", p=128),
                   ZT.unsqueeze(1).to_broadcast([128, NOVF, 1024]), after=[G.last])
        PT_ = [bc(0)[:, 0:512], bc(0)[:, 512:1024]]
        cut(0)
        HHH = FHH[:, :].rearrange("p (c n) -> p c n", c=4)
        HLL = FHL[:, :].rearrange("p (c n) -> p c n", c=4)
        ci = 0
        hq = None
        h_free = None

        def finish(item):
            o, i_, t = item
            qb_free[i_] = r = split(HHH[o], HLL[o], QB[i_], after=[t], hi_after=[h_free])
            return r

        for g in range(8):
            h_t = []
            for cc in range(2):
                wh, wl = chunk(FWH, ci, 8), chunk(FWL, ci, 8)
                for fb in range(2):
                    for th in range(2):
                        b = (fb * 2 + th) % 4
                        tk = mm3(b, PS[:, b, :], [(wh[:, k, 128 * fb:128 * fb + 128], wl[:, k, 128 * fb:128 * fb + 128],
                                                   XHH[:, k, 512 * th:512 * th + 512], XLL[:, k, 512 * th:512 * th + 512])
                                                  for k in range(8)], after=[cut_t[ci], xt2])
                        i_ = qn[0] % 2
                        qn[0] += 1
                        r = a_(nc.scalar.activation, QB[i_], PS[:, b, :], ACT.Relu, after=[tk, qb_free[i_]])
                        bank_free[b] = r
                        r = g_(nc.gpsimd.tensor_tensor, QB[i_], QB[i_], QB[i_], ALU.mult, after=[r])
                        h_t.append(finish(((slice(None), 2 * cc + fb, slice(512 * th, 512 * th + 512)), i_, r)))
                        if fb == 0 and th == 0:
                            fetch(ci + 2)
                            cut(ci + 1)
                wh_free[ci % 2] = P.last
                ci += 1
            for n in range(2):
                wh, wl = chunk(FWH, ci, 4), chunk(FWL, ci, 4)
                ev = residual(GT2, ALPHA if g == 0 else None, x1, PT_)
                for t in range(8):
                    b = 4 + t % 4
                    tk = mm3(b, PS[:, b, :], [(HHH[:, k, 128 * t:128 * t + 128], HLL[:, k, 128 * t:128 * t + 128],
                                               wh[:, k, :], wl[:, k, :]) for k in range(4)],
                             after=[cut_t[ci], h_t])
                    bank_free[b] = ev(t, n, PS[:, b, :], tk)
                    if t == 0:
                        fetch(ci + 2)
                        cut(ci + 1)
                wh_free[ci % 2] = P.last
                ci += 1
            h_free = P.last
        area[1], = layout(("BIG2", 9 * SL, F32))
        XT = slot(2, 2).rearrange("p (c n) -> p c n", c=8)
        U = slot(4, 2).rearrange("p (t d) -> p t d", t=8)
        for s_ in slot_free:
            slot_free[s_] = P.last
        z = layer_norm_z([V.last] * 8)
        t_bc2 = dma(G, "bc2", bc(2), X["ln2_g"][0].partition_broadcast(128), after=now())
        t_bc3 = dma(G, "bc3", bc(3), X["ln2_b"][0].partition_broadcast(128), after=now())
        x2 = []
        for t in range(8):
            v(nc.vector.tensor_tensor, XRES[:, t, :], XRES[:, t, :], bc(2), ALU.mult, after=[z[t], t_bc2])
            x2.append(vc(nc.vector.tensor_tensor, XRES[:, t, :], XRES[:, t, :], bc(3), ALU.add, after=[t_bc3]))

        ss8 = st("ss8", 8)

        def rms_u(ready, eps):
            A.wait(*now())
            V.wait(*now())
            for t in range(8):
                a_(nc.scalar.activation, U[:, t, :], XRES[:, t, :], ACT.Square, accum_out=ss8[:, t:t + 1],
                   after=[ready[t], A.last])
            r = rsqrt(ss8, ss8, 1.0 / 1024, eps, [A.last])
            return [v(nc.vector.tensor_scalar, U[:, t, :], XRES[:, t, :], ss8[:, t:t + 1], None, ALU.mult, after=[r])
                    for t in range(8)]

        V.wait(t_zy)
        u = rms_u(x2, EPS2)
        nm = cols["nmix"]
        xt3, _ = to_fm(lambda t, c: U[:, t, 128 * c:128 * c + 128], lambda c: nm[:, c:c + 1], None, u)

        wi2 = X["w_in_2"][0]
        wqk, tqk = wload(6, wi2[:, 1536:2048])
        wv, twv = wload(7, wi2[:, 2048:2560])
        wg, twg = wload(8, wi2[:, 2560:3072])
        WGR = st("wgr", 128).rearrange("p (k n) -> p k n", k=8)
        twr = dma(G, "wgr", WGR, wi2[:, 3072:3088].rearrange("(k p) n -> p k n", p=128))
        GW = bc(1)[0:17, 512:768]
        tgw = [dma(G, "gw", GW[0:16, :], X["gla_gate_w_2"][0], after=now()),
               dma(G, "gwb", GW[16:17, :], X["gla_gate_b_2"][0].rearrange("(a n) -> a n", a=1))]
        A.wait(*now())
        V.wait(*now())
        GQ = slot(9)[0:64, :].rearrange("p (h n) -> p h n", h=4)
        GK = slot(10)[0:64, :].rearrange("p (h n) -> p h n", h=4)
        for fb in range(4):
            dst = GQ if fb < 2 else GK
            scl = 0.125 if fb < 2 else 1.0
            for th in range(2):
                b = 4 + (2 * fb + th) % 4
                tk = mm(b, PS[:, b, :], [(wqk[:, k, 128 * fb:128 * fb + 128], XT[:, k, 512 * th:512 * th + 512])
                                        for k in range(8)], after=[tqk, xt3])
                h0 = 2 * (fb % 2)
                a_(nc.scalar.activation, dst[:, h0, 512 * th:512 * th + 512], PS[0:64, b, :], ACT.Copy, scale=scl,
                   after=[tk])
                bank_free[b] = v(nc.vector.tensor_scalar, dst[:, h0 + 1, 512 * th:512 * th + 512], PS[64:128, b, :],
                                 scl, None, ALU.mult, after=[tk, A.last])
        GR = bc(0)[0:17, :]
        v(nc.vector.memset, GR, 1.0)
        for th in range(2):
            tk = mm(4 + th, PS[0:16, 4 + th, :], [(WGR[:, k, :], XT[:, k, 512 * th:512 * th + 512]) for k in range(8)],
                    after=[twr])
            bank_free[4 + th] = v(nc.vector.tensor_copy, GR[0:16, 512 * th:512 * th + 512], PS[0:16, 4 + th, :],
                                  after=[tk, V.last])
        R6 = slot(6)
        EL, EP, EN, EE = (R6[0:64, 512 * i:512 * i + 512] for i in range(4))
        K2, K3, SS0, SS1 = (R6[0:64, 512 * i:512 * i + 512] for i in range(4, 8))
        Q1, Q2, Q3, K4 = EL, EP, EN, EE
        ELD = st("eld", 8)[0:64, :].rearrange("p (h c) -> p h c", h=4)
        LA, KE = bc(2)[:, 0:256], bc(2)[:, 256:512]
        LB = bc(2)[:, 512:768]
        AT = bc(3)[:, 0:512]
        SQ = bc(3)[:, 512:1024]
        SS = [SS0, SS1]
        VG = bc(1)[:, 0:512]
        A.wait(*now())
        V.wait(*now())
        v(nc.vector.memset, AT, 0.0)
        v(nc.vector.memset, SS[0], 0.0)
        MPI = C("mp").bitcast(I32).unsqueeze(1).to_broadcast([128, 4, 128])
        MFI = C("mf").bitcast(I32).unsqueeze(1).to_broadcast([128, 4, 128])
        gss = st("gss", 32)
        SG = slot(4).rearrange("p (t n) -> p t n", t=8)
        GO = slot(5).rearrange("p (t n) -> p t n", t=8)
        V.wait(V.last)

        def h4(ap):
            return ap.rearrange("p (h n) -> p h n", h=4)

        def gate_logs(t):
            pz = mm(2, PS[:, 2, 0:256], [(GR[:, 128 * t:128 * t + 128], GW)], after=[tgw, t_gr])
            a_(nc.scalar.activation, LB, PS[:, 2, 0:256], ACT.Abs, after=[pz, t_la[0]])
            ac(nc.scalar.activation, LB, LB, ACT.Exp, scale=-1.0)
            r = ac(nc.scalar.activation, LB, LB, ACT.Ln, bias=1.0)
            t_la[0] = bank_free[2] = v(nc.vector.scalar_tensor_tensor, out=LA, in0=PS[:, 2, 0:256], scalar=0.0,
                                       in1=LB, op0=ALU.min, op1=ALU.subtract, after=[r, la_free[0]])

        t_gr = V.last
        t_la, la_free = [None], [None]
        pke = pu1 = po = pf = pp = None
        gate_logs(0)
        for t in range(8):
            xt = [XT[:, k, 128 * t:128 * t + 128] for k in range(8)]
            pl = []
            for k3 in range(3):
                for h in range(4):
                    x_ = mm(3 + k3, PS[0:64, 3 + k3, 128 * h:128 * h + 128],
                            [(LA[:, 64 * h:64 * h + 64], C("tri")[:, 128 * k3:128 * k3 + 128])], after=[t_la[0]])
                pl.append(x_)
            la_free[0] = pl[2]
            p0 = mm(0, PS[:, 0, :], [(xt[k], wv[:, k, :]) for k in range(8)], after=[twv])
            t_ee = a_(nc.scalar.activation, EE, PS[0:64, 5, :], ACT.Exp, after=[pl[2], pke])
            bank_free[5] = t_ee
            t_ep = a_(nc.scalar.activation, EP, PS[0:64, 4, :], ACT.Exp, after=[pl[1], pp, V.last])
            t_en = a_(nc.scalar.activation, EN, PS[0:64, 4, :], ACT.Exp, scale=-1.0, after=[pf])
            bank_free[4] = t_en
            t_el = a_(nc.scalar.activation, EL, PS[0:64, 3, :], ACT.Exp, after=[pl[0], po])
            bank_free[3] = t_el
            tv = bank_free[0] = a_(nc.scalar.copy, VG, PS[:, 0, :], after=[p0, pu1, po])
            gq = GQ[:, :, 128 * t:128 * t + 128]
            gk = GK[:, :, 128 * t:128 * t + 128]
            tk4 = v(nc.vector.tensor_tensor, h4(K4), gk, h4(EE), ALU.mult, after=[t_ee])
            v(nc.vector.tensor_tensor, h4(K3), gk, h4(EP), ALU.mult, after=[t_ep, pf])
            v(nc.vector.tensor_tensor, h4(K2), gk, h4(EN), ALU.mult, after=[t_en, pp])
            V.wait(V.last)
            tpast = v(nc.vector.tensor_tensor, h4(Q2), gq, h4(EP), ALU.mult)
            tfut = v(nc.vector.tensor_tensor, h4(Q3), gq, h4(EN), ALU.mult)
            v(nc.vector.tensor_copy, ELD, h4(EL)[:, :, 63:128:64], after=[t_el, V.last])
            tq1 = vc(nc.vector.tensor_tensor, h4(Q1), gq, h4(EL), ALU.mult)
            pke = tr(2, [(PS[:, 2, 64 * h:64 * h + 64], K4[:, 128 * h:128 * h + 128]) for h in range(4)], after=[tk4])
            for h in range(4):
                pp = mm(6, PS[:, 6, 128 * h:128 * h + 128],
                        [(K2[:, 128 * h:128 * h + 128], Q2[:, 128 * h:128 * h + 128])], after=[tpast])
            for h in range(4):
                pf = mm(7, PS[:, 7, 128 * h:128 * h + 128],
                        [(K3[:, 128 * h:128 * h + 128], Q3[:, 128 * h:128 * h + 128])], after=[tfut])
            tke = bank_free[2] = a_(nc.scalar.copy, KE, PS[:, 2, 0:256], after=[pke, pu1])
            v(nc.vector.copy_predicated, h4(AT), MPI, h4(PS[:, 6, :]), after=[pp, po])
            bank_free[6] = V.last
            tat = bank_free[7] = vc(nc.vector.copy_predicated, h4(AT), MFI, h4(PS[:, 7, :]), after=[pf])
            for h in range(4):
                pu0 = mm(4, PS[0:64, 4, 128 * h:128 * h + 128],
                         [(KE[0:64, 64 * h:64 * h + 64], VG[0:64, 128 * h:128 * h + 128])], after=[tke, tv])
            for h in range(4):
                pu1 = mm(5, PS[0:64, 5, 128 * h:128 * h + 128],
                         [(KE[64:128, 64 * h:64 * h + 64], VG[64:128, 128 * h:128 * h + 128])])
            if t < 7:
                gate_logs(t + 1)
            p1 = mm(1, PS[:, 1, :], [(xt[k], wg[:, k, :]) for k in range(8)], after=[twg])
            v(nc.vector.tensor_tensor, h4(SS[1]), h4(SS[0]), ELD[:, :, 0:1].to_broadcast([64, 4, 128]), ALU.mult,
              after=[V.last, po])
            ts1 = bank_free[4] = vc(nc.vector.tensor_tensor, SS[1], SS[1], PS[0:64, 4, :], ALU.add, after=[pu0])
            for h in range(4):
                o = PS[:, 6, 128 * h:128 * h + 128]
                mm(6, o, [(AT[:, 128 * h:128 * h + 128], VG[:, 128 * h:128 * h + 128])], after=[tat])
                mm(6, PS[0:64, 6, 128 * h:128 * h + 128],
                   [(Q1[:, 128 * h:128 * h + 64], SS[0][:, 128 * h:128 * h + 128])], after=[tq1], start=False)
                po = mm(6, PS[64:128, 6, 128 * h:128 * h + 128],
                        [(Q1[:, 128 * h + 64:128 * h + 128], SS[1][:, 128 * h:128 * h + 128])], after=[ts1],
                        start=False)
            x_ = a_(nc.scalar.activation, SQ, PS[:, 6, :], ACT.Square, after=[po, V.last])
            v(nc.vector.tensor_tensor, h4(SS[0]), h4(SS[1]), ELD[:, :, 1:2].to_broadcast([64, 4, 128]), ALU.mult,
              after=[po])
            bank_free[5] = vc(nc.vector.tensor_tensor, SS[0], SS[0], PS[0:64, 5, :], ALU.add, after=[pu1])
            bank_free[6] = v(nc.vector.tensor_copy, GO[:, t, :], PS[:, 6, :], after=[x_])
            v(nc.vector.tensor_reduce, gss[:, 4 * t:4 * t + 4], h4(SQ), AX, ALU.add, after=[x_])
            bank_free[1] = silu_into(SG[:, t, :], PS[:, 1, :], [p1])
        slot_free[6] = slot_free[7] = slot_free[8] = now()
        r = rsqrt(gss, gss, 1.0 / 128, EPS2, [V.last])
        for t in range(8):
            o3 = h4(GO[:, t, :])
            vc(nc.vector.tensor_tensor, o3, o3, b4(gss[:, 4 * t:4 * t + 4], 128), ALU.mult)
            vc(nc.vector.tensor_tensor, GO[:, t, :], GO[:, t, :], SG[:, t, :], ALU.mult)

        ws = [wload(6 + n, wi2[:, 512 * n:512 * n + 512]) for n in range(3)]
        DQ = slot(9).rearrange("p (h n) -> p h n", h=4)
        DK = slot(10).rearrange("p (h n) -> p h n", h=4)
        DV = slot(4).rearrange("p (t n) -> p t n", t=8)
        DQT = [bc(0)[:, 0:512], bc(0)[:, 512:1024]]
        A.wait(*now())
        V.wait(*now())
        dss = st("dss", 16)
        tm_free, dq_t = [None, None], [None, None]

        def turn_qk(t, n):
            b, o = 3 + n, DQT[n]
            tm_free[n] = p_ = tr(b, [(PS[:, b, 128 * h:128 * h + 128], o[:, 128 * h:128 * h + 128])
                                     for h in range(4)], after=[dq_t[n]])
            dst = (DQ, DK)[n][:, :, 128 * t:128 * t + 128]
            bank_free[b] = a_(nc.scalar.activation, dst, h4(PS[:, b, :]), ACT.Copy,
                              scale=cols[("daq", "dak")[n]], after=[p_])

        for t in range(8):
            xt = [XT[:, k, 128 * t:128 * t + 128] for k in range(8)]
            for n in range(3):
                pr = mm(n, PS[:, n, :], [(xt[k], ws[n][0][:, k, :]) for k in range(8)], after=[ws[n][1]])
                if n < 2 and t:
                    turn_qk(t - 1, n)
                if n == 2:
                    bank_free[2] = a_(nc.scalar.copy, DV[:, t, :], PS[:, 2, :], after=[pr])
                    continue
                sq = bc(1)[:, 512 * n:512 * n + 512]
                d8 = dss[:, 8 * n:8 * n + 8]
                x_ = a_(nc.scalar.activation, sq, PS[:, n, :], ACT.Square, after=[pr, V.last])
                v(nc.vector.tensor_reduce, d8, sq.rearrange("p (h n) -> p h n", h=8), AX, ALU.add, after=[x_])
                r = rsqrt(d8, d8, 1.0 / 64, EPS2, [V.last])
                o = DQT[n]
                bank_free[n] = r = v(nc.vector.tensor_tensor, o.rearrange("p (h n) -> p h n", h=8),
                                     PS[:, n, :].rearrange("p (h n) -> p h n", h=8), b4(d8, 64), ALU.mult,
                                     after=[r, tm_free[n]])
                dq_t[n] = r
        for n in range(2):
            turn_qk(7, n)
        A.wait(*now())
        V.wait(*now())
        P.wait(*now())
        slot_free[7] = slot_free[8] = now()
        DO = slot(6).rearrange("p (t n) -> p t n", t=8)
        s23 = slot(2, 2)
        PB1 = [[s23[:, 0:1024], s23[:, 1024:2048]], [s23[:, 2048:3072], s23[:, 3072:4096]]]
        PC = [s23[:, 4096:5120], s23[:, 5120:6144]]
        PT2 = [s23[:, 6144:7168], s23[:, 7168:8192]]

        def da_qk(h, i, m, c0, c1):
            return (DQ[64 * m:64 * m + 64, h, 128 * i:128 * i + 128], DK[64 * m:64 * m + 64, h, c0:c1])

        class Combine:
            free = [None, None]

            def __call__(self, n, nk, pt):
                (t1, r1), (t2, r2) = pt
                c2 = st(f"c2{n % 2}", 1)
                v(nc.vector.tensor_tensor, c2, r2, nlam, ALU.mult, after=[t1, t2])
                pc = PC[n % 2][:, 0:nk]
                vc(nc.vector.tensor_scalar, pc, PB1[n % 2][1][:, 0:nk], c2, None, ALU.mult, after=[self.free[n % 2]])
                t = vc(nc.vector.scalar_tensor_tensor, out=pc, in0=PB1[n % 2][0][:, 0:nk], scalar=r1, in1=pc,
                       op0=ALU.mult, op1=ALU.add)
                return PC[n % 2], t

        dos = st("dos", 32).rearrange("p (t h) -> p t h", t=8)
        SQD = bc(1)[:, 0:128]

        def da_out(h, i, o, t, pt):
            x_ = a_(nc.scalar.activation, SQD, o, ACT.Square, accum_out=dos[:, i, h:h + 1], after=[t, A.last])
            return v(nc.vector.tensor_copy, DO[:, i, 128 * h:128 * h + 128], o, after=[x_])

        attention([(h, i) for h in range(4) for i in range(8)], da_qk, C("chm"), 64.0 ** -0.5, PB1, PT2,
                  lambda h, j: DV[:, j, 128 * h:128 * h + 128], 128, da_out, nmap=2, combine=Combine())
        dosf = dos.rearrange("p t h -> p (t h)")
        rsqrt(dosf, dosf, 1.0 / 128, EPS2, now())
        for t in range(8):
            vc(nc.vector.tensor_tensor, h4(DO[:, t, :]), h4(DO[:, t, :]), b4(dos[:, t, :], 128), ALU.mult)
        dag = st("dag", 1)
        vc(nc.vector.tensor_scalar, dag, cols["daon"], 0.8, None, ALU.mult)

        MIX2 = [DO, GO]
        A.wait(*now())
        V.wait(*now())
        mt, _ = to_fm(lambda t, c: MIX2[c // 4][:, t, 128 * (c % 4):128 * (c % 4) + 128],
                      lambda c: dag if c < 4 else cols["glon"], None, [now()] * 8)

        def add_res(t, n, ps, tk):
            x = XRES[:, t, 512 * n:512 * n + 512]
            return v(nc.vector.tensor_tensor, x, x, ps, ALU.add, after=[tk])

        xr = project(X["w_o_2"][0], lambda k, t: XT[:, k, 128 * t:128 * t + 128], add_res, mt, slots=(7, 8))
        slot_free[6] = now()

        MEM = slot(9)[:, 0:2048].rearrange("p (t d) -> p t d", t=2)
        MEMT = slot(9)[:, 2048:4096].rearrange("p (c n) -> p c n", c=8)
        CK = slot(10)[:, 0:2048].rearrange("p (c n) -> p c n", c=8)
        CV = slot(10)[:, 2048:4096].rearrange("p (t d) -> p t d", t=2)
        tmem = dma(G, "mem", MEM, X["mem_2"][0].rearrange("(t p) d -> p t d", p=128), after=now())
        mss = st("mss", 2)
        SQC = bc(0)
        for t in range(2):
            a_(nc.scalar.activation, SQC, MEM[:, t, :], ACT.Square, accum_out=mss[:, t:t + 1],
               after=[tmem, V.last, A.last])
        r = rsqrt(mss, mss, 1.0 / 1024, EPS2, [A.last])
        for t in range(2):
            v(nc.vector.tensor_scalar, MEM[:, t, :], MEM[:, t, :], mss[:, t:t + 1], None, ALU.mult, after=[r])
        tm = V.last
        tmt = []
        for c in range(8):
            b = c % 4
            p_ = tr(b, [(PS[:, b, 128 * t:128 * t + 128], MEM[:, t, 128 * c:128 * c + 128]) for t in range(2)],
                    after=[tm])
            bank_free[b] = a_(nc.scalar.activation, MEMT[:, c, :], PS[:, b, 0:256], ACT.Copy,
                              scale=cols["nmem"][:, c:c + 1], after=[p_])
            tmt.append(bank_free[b])
        wkv = X["w_ckv_2"][0]
        css = st("css", 4)
        KTM2 = bc(1)[:, 0:512]
        ktm_free = None
        A.wait(*now())
        V.wait(*now())
        for n in range(4):
            s = 6 + n % 3
            w, tw = wload(s, wkv[:, 512 * n:512 * n + 512])
            for t in range(2):
                b = 4 + t
                p_ = mm(b, PS[:, b, :], [(MEMT[:, k, 128 * t:128 * t + 128], w[:, k, :]) for k in range(8)],
                        after=[tw, tmt])
                if n >= 2:
                    bank_free[b] = a_(nc.scalar.copy, CV[:, t, 512 * (n - 2):512 * (n - 2) + 512], PS[:, b, :],
                                      after=[p_])
                    continue
                for hh in range(2):
                    a_(nc.scalar.activation, SQC[:, 0:256], PS[:, b, 256 * hh:256 * hh + 256], ACT.Square,
                       accum_out=css[:, hh:hh + 1], after=[p_, A.last, V.last])
                r = rsqrt(css[:, 0:2], css[:, 0:2], 1.0 / 256, EPS2, [A.last])
                bank_free[b] = r = v(nc.vector.tensor_tensor, KTM2.rearrange("p (h n) -> p h n", h=2),
                                     PS[:, b, :].rearrange("p (h n) -> p h n", h=2), b4(css[:, 0:2], 256), ALU.mult,
                                     after=[r, ktm_free])
                ktm_free = p_ = tr(6, [(PS[:, 6, 128 * c:128 * c + 128], KTM2[:, 128 * c:128 * c + 128])
                                       for c in range(4)], after=[r])
                for dc in range(2):
                    o = CK[:, 4 * dc + 2 * n:4 * dc + 2 * n + 2, 128 * t:128 * t + 128]
                    i_ = PS[:, 6, :].rearrange("p (h d n) -> p h d n", h=2, d=2)[:, :, dc, :]
                    bank_free[6] = a_(nc.scalar.activation, o, i_, ACT.Copy, scale=cols["ckn"][:, dc:dc + 1],
                                      after=[p_])
            slot_free[s] = P.last
        u = rms_u(xr, EPS2)
        nc_ = cols["ncr"]
        V.wait(P.last)
        A.wait(P.last)
        xt4, _ = to_fm(lambda t, c: U[:, t, 128 * c:128 * c + 128], lambda c: nc_[:, c:c + 1], None, u)
        wq_, twq_ = zip(*[wload(6 + n, X["w_cq_2"][0][:, 512 * n:512 * n + 512]) for n in range(2)])
        A.wait(*now())
        V.wait(*now())
        G.wait(*now())
        CQ = bc(0)
        CQT = bc(1).rearrange("p (d h n) -> p d h n", d=2, h=4)
        CP = bc(2).rearrange("p (h n) -> p h n", h=4)
        CPT = bc(3).rearrange("p (m h n) -> p m h n", m=2, h=4)
        cm, cr = st("cm", 4), st("cr", 4)
        s4_ = PS[:, 4:6, :].rearrange("p b n -> p (b n)").rearrange("p (h n) -> p h n", h=4)
        JUNK = slot(8)[:, 0:256]
        css_ = [st("cssa", 4), st("cssb", 4)]
        cr_ = [st("cra", 4), st("crb", 4)]
        tq_t, cq_t, cpt_t = {}, {}, {}
        pav = pcq = psc = cp_free = None

        def q_part(t, n):
            pq = mm(n, PS[:, n, :], [(XT[:, k, 128 * t:128 * t + 128], wq_[n][:, k, :]) for k in range(8)],
                    after=[twq_[n], xt4])
            for h in range(2 * n, 2 * n + 2):
                ac(nc.scalar.activation, JUNK, PS[:, n, 256 * (h % 2):256 * (h % 2) + 256], ACT.Square,
                   accum_out=css_[t % 2][:, h:h + 1], after=[pq, V.last])

        def q_norm(t):
            c_ = css_[t % 2]
            r = rsqrt(c_, c_, 1.0 / 256, EPS2, [A.last])
            bank_free[0] = bank_free[1] = cq_t[t] = v(
                nc.vector.tensor_tensor, CQ.rearrange("p (h n) -> p h n", h=4),
                PS[:, 0:2, :].rearrange("p b n -> p (b n)").rearrange("p (h n) -> p h n", h=4), b4(c_, 256), ALU.mult,
                after=[r, pcq])

        def values(t):
            for h in range(4):
                b = 6 + h // 2
                po = mm(b, PS[:, b, 256 * (h % 2):256 * (h % 2) + 256],
                        [(CPT[:, m, h, :], CV[:, m, 256 * h:256 * h + 256]) for m in range(2)], after=[cpt_t[t]])
            bank_free[6] = bank_free[7] = v(
                nc.vector.tensor_tensor, U[:, t, :].rearrange("p (h n) -> p h n", h=4),
                PS[:, 6:8, :].rearrange("p b n -> p (b n)").rearrange("p (h n) -> p h n", h=4), b4(cr_[t % 2], 256),
                ALU.mult, after=[po])
            return po

        q_part(0, 0)
        q_part(0, 1)
        q_norm(0)
        for t in range(8):
            if t:
                pav = values(t - 1)
            for dc in range(2):
                p_ = tr(2 + dc, [(PS[:, 2 + dc, 128 * h:128 * h + 128], CQ[:, 256 * h + 128 * dc:256 * h + 128 * dc + 128])
                                 for h in range(4)], after=[cq_t[t]])
                bank_free[2 + dc] = a_(nc.scalar.activation, CQT[:, dc, :, :], h4(PS[:, 2 + dc, :]), ACT.Copy,
                                       scale=cols["cqn"][:, dc:dc + 1], after=[p_, psc])
            pcq, tq = P.last, A.last
            if t < 7:
                q_part(t + 1, 0)
            for h in range(4):
                b = 4 + h // 2
                psc = mm(b, PS[:, b, 256 * (h % 2):256 * (h % 2) + 256],
                         [(CQT[:, dc, h, :], CK[:, 4 * dc + h, :]) for dc in range(2)], after=[tq])
            v(nc.vector.tensor_reduce, cm, s4_, AX, ALU.max, after=[psc, A.last])
            r = vc(nc.vector.tensor_scalar, cm, cm, -1.0 / 16, None, ALU.mult)
            for h in range(4):
                a_(nc.scalar.activation, CP[:, h, :], s4_[:, h, :], ACT.Exp, bias=cm[:, h:h + 1], scale=1.0 / 16,
                   accum_out=cr_[t % 2][:, h:h + 1], after=[r, cp_free])
            te = bank_free[4] = bank_free[5] = A.last
            r = v(nc.vector.reciprocal, cr_[t % 2], cr_[t % 2], after=[te])
            if t < 7:
                q_part(t + 1, 1)
            for m in range(2):
                p_ = tr(6 + m, [(PS[:, 6 + m, 128 * h:128 * h + 128], CP[:, h, 128 * m:128 * m + 128])
                                for h in range(4)], after=[te])
                bank_free[6 + m] = v(nc.vector.tensor_copy, CPT[:, m, :, :], h4(PS[:, 6 + m, :]), after=[p_, pav])
            cp_free, cpt_t[t] = P.last, V.last
            if t < 7:
                q_norm(t + 1)
        values(7)
        slot_free[8] = now()
        slot_free[6] = slot_free[7] = P.last
        A.wait(*now())
        V.wait(*now())
        mt, _ = to_fm(lambda t, c: U[:, t, 128 * c:128 * c + 128], lambda c: one1, None, [now()] * 8)
        xr = project(X["w_co_2"][0], lambda k, t: XT[:, k, 128 * t:128 * t + 128], add_res, mt, slots=(8, 6, 7))

        XZ, TOKS, YO = scr
        u = rms_u(xr, EPS2)
        A.wait(P.last)
        V.wait(P.last)
        t_nf = dma(G, "bc0", bc(0), X["norm_ffn_2"][0].partition_broadcast(128), after=now())
        u = [v(nc.vector.tensor_tensor, U[:, t, :], U[:, t, :], bc(0), ALU.mult, after=[u[t], t_nf]) for t in range(8)]
        t_xz = [dma(A, f"x{t}", XZ.rearrange("(t p) d -> p t d", p=128)[:, t, :], U[:, t, :], after=[u[t]])
                for t in range(8)]
        WRT = slot(9)[:, 0:1024].rearrange("p (k n) -> p k n", k=8)
        v(nc.vector.memset, WRT, 0.0, after=now())
        twr = [dma(G, "wr0", WRT[:, :, 0:4], X["w_group_2"][0].rearrange("(k p) n -> p k n", p=128), after=now()),
               dma(G, "wr1", WRT[:, :, 4:36], X["w_expert_2"][0].rearrange("(k p) n -> p k n", p=128))]
        BR = slot(9)[:, 1024:1060]
        tbr = [dma(G, "br0", BR[:, 0:4], X["b_group_2"][0].partition_broadcast(128)),
               dma(G, "br1", BR[:, 4:36], X["b_expert_2"][0].partition_broadcast(128))]
        ZI = slot(9)[:, 1152:1152 + 752].bitcast(I32)
        v(nc.vector.memset, ZI, 0, after=now())
        t_z = dma(G, "tz", TOKS.rearrange("(p b) w -> p (b w)", p=128), ZI, after=[V.last])
        xt5, _ = to_fm(lambda t, c: U[:, t, 128 * c:128 * c + 128], lambda c: one1, None, u)
        for t in range(8):
            pr = mm(4 + t // 4, PS[:, 4 + t // 4, 128 * (t % 4):128 * (t % 4) + 128],
                    [(XT[:, k, 128 * t:128 * t + 128], WRT[:, k, :]) for k in range(8)], after=[twr, xt5])
        W9 = slot(10)
        wat = [0]

        def wk_(n):
            a = wat[0]
            wat[0] += n
            assert wat[0] <= 4096
            return W9[:, a:a + n]

        V.wait(*now())
        TT = nc.vector.tensor_tensor
        TS = nc.vector.tensor_scalar
        LG = wk_(288).rearrange("p (t n) -> p t n", t=8)
        bank_free[4] = bank_free[5] = vc(TT, LG, PS[:, 4:6, :].rearrange("p b (t n) -> p (b t) n", t=4)[:, :, 0:36],
                          BR.unsqueeze(1).to_broadcast([128, 8, 36]), ALU.add, after=[pr, *tbr])
        io = C("io")

        def bt(ap, n):
            return ap.unsqueeze(2).to_broadcast([128, 8, n])

        def first_max(x, n):
            m_, i_ = wk_(8), wk_(8)
            eq = wk_(8 * n).rearrange("p (t n) -> p t n", t=8)
            vc(nc.vector.tensor_reduce, m_, x, AX, ALU.max)
            vc(TT, eq, x, bt(m_, n), ALU.is_equal)
            vc(TS, eq, eq, -100.0, 100.0, ALU.mult, ALU.add)
            vc(TT, eq, eq, io[:, 0:n].unsqueeze(1).to_broadcast([128, 8, n]), ALU.add)
            vc(nc.vector.tensor_reduce, i_, eq, AX, ALU.min)
            return m_, i_

        def one_hot(i_, n):
            o = wk_(8 * n).rearrange("p (t n) -> p t n", t=8)
            vc(TT, o, io[:, 0:n].unsqueeze(1).to_broadcast([128, 8, n]), bt(i_, n), ALU.is_equal)
            return o

        gm, gi = first_max(LG[:, :, 0:4], 4)
        ge = wk_(32).rearrange("p (t n) -> p t n", t=8)
        vc(TT, ge, LG[:, :, 0:4], bt(gm, 4), ALU.subtract)
        t = a_(nc.scalar.activation, ge, ge, ACT.Exp, after=[V.last])
        pg = wk_(8)
        v(nc.vector.tensor_reduce, pg, ge, AX, ALU.add, after=[t])
        vc(nc.vector.reciprocal, pg, pg)
        o4 = one_hot(gi, 4)
        em = wk_(256)
        EM = em.rearrange("p (t g e) -> p t g e", t=8, g=4)
        for gg in range(4):
            vc(TT, EM[:, :, gg, :], LG[:, :, 4 + 8 * gg:12 + 8 * gg], o4[:, :, gg:gg + 1].to_broadcast([128, 8, 8]),
               ALU.mult)
        ELG = wk_(64).rearrange("p (t n) -> p t n", t=8)
        vc(TT, ELG, EM[:, :, 0, :], EM[:, :, 1, :], ALU.add)
        vc(TT, ELG, ELG, EM[:, :, 2, :], ALU.add)
        vc(TT, ELG, ELG, EM[:, :, 3, :], ALU.add)
        m1, i1 = first_max(ELG, 8)
        oh1 = one_hot(i1, 8)
        vc(nc.vector.scalar_tensor_tensor, out=ELG, in0=oh1, scalar=NEG, in1=ELG, op0=ALU.mult, op1=ALU.add)
        m2, i2 = first_max(ELG, 8)
        dd, g1, g2 = wk_(8), st("g1", 8), st("g2", 8)
        vc(TT, dd, m2, m1, ALU.subtract)
        t = a_(nc.scalar.activation, dd, dd, ACT.Exp, after=[V.last])
        v(TS, g1, dd, 1.0, None, ALU.add, after=[t])
        vc(nc.vector.reciprocal, g1, g1)
        vc(TT, g1, g1, pg, ALU.mult)
        vc(TT, g2, g1, dd, ALU.mult)
        es, OHS, ranks = [], [], []
        for ii in (i1, i2):
            e_ = wk_(8)
            vc(nc.vector.scalar_tensor_tensor, out=e_, in0=gi, scalar=8.0, in1=ii, op0=ALU.mult, op1=ALU.add)
            es.append(e_)
            OHS.append(one_hot(e_, 32))
        MM = wk_(256)
        M3 = MM.rearrange("p (t n) -> p t n", t=8)
        tm = vc(TT, M3, OHS[0], OHS[1], ALU.add)
        p1 = mm(5, PS[:, 5, 0:256], [(C("su"), MM)], after=[tm])
        p2 = mm(6, PS[:, 6, 0:256], [(C("one"), MM)])
        TOT = PS[:, 6, 0:256].rearrange("p (t n) -> p t n", t=8)
        PRE = wk_(256).rearrange("p (t n) -> p t n", t=8)
        run = wk_(32)
        V.wait(V.last)
        v(nc.vector.memset, run, 0.0)
        for t in range(8):
            vc(TT, PRE[:, t, :], PS[:, 5, 32 * t:32 * t + 32], run, ALU.add, after=[p1, p2])
            vc(TT, run, run, TOT[:, t, :], ALU.add)
        bank_free[5] = bank_free[6] = V.last
        ob, sca, scb, cmpb = wk_(32), wk_(32), wk_(32), wk_(32)
        vc(TS, ob, run, 128.5, None, ALU.is_gt)
        for kk in range(2, 8):
            vc(TS, cmpb, run, 128.0 * kk + 0.5, None, ALU.is_gt)
            vc(TT, ob, ob, cmpb, ALU.add)
        vc(nc.vector.tensor_copy, sca, ob)
        a1, b1 = sca, scb
        for sft in (1, 2, 4, 8, 16):
            vc(nc.vector.tensor_copy, b1[:, 0:sft], a1[:, 0:sft])
            vc(TT, b1[:, sft:32], a1[:, sft:32], a1[:, 0:32 - sft], ALU.add)
            a1, b1 = b1, a1
        os_ = wk_(32)
        vc(TT, os_, a1, ob, ALU.subtract)
        sls, slt = [], []
        for kk in range(2):
            rk, osa, qq, cq, tmp_ = wk_(8), wk_(8), wk_(8), wk_(8), wk_(8)
            prod = em.rearrange("p (t n) -> p t n", t=8)
            vc(TT, prod, OHS[kk], PRE, ALU.mult)
            vc(nc.vector.tensor_reduce, rk, prod, AX, ALU.add)
            vc(TT, prod, OHS[kk], os_.unsqueeze(1).to_broadcast([128, 8, 32]), ALU.mult)
            vc(nc.vector.tensor_reduce, osa, prod, AX, ALU.add)
            vc(TS, qq, rk, 127.5, None, ALU.is_gt)
            for k7 in range(2, 8):
                vc(TS, cq, rk, 128.0 * k7 - 0.5, None, ALU.is_gt)
                vc(TT, qq, qq, cq, ALU.add)
            vc(nc.vector.scalar_tensor_tensor, out=tmp_, in0=osa, scalar=31.0, in1=qq, op0=ALU.add, op1=ALU.add)
            vc(TT, tmp_, tmp_, es[kk], ALU.subtract)
            vc(TS, cq, qq, 1.0, None, ALU.min)
            vc(TT, tmp_, tmp_, cq, ALU.mult)
            vc(TT, tmp_, tmp_, es[kk], ALU.add)
            vc(nc.vector.scalar_tensor_tensor, out=rk, in0=qq, scalar=-128.0, in1=rk, op0=ALU.mult, op1=ALU.add)
            vc(nc.vector.scalar_tensor_tensor, out=qq, in0=tmp_, scalar=128.0, in1=rk, op0=ALU.mult, op1=ALU.add)
            vc(nc.vector.scalar_tensor_tensor, out=tmp_, in0=rk, scalar=float(NBLK), in1=tmp_, op0=ALU.mult,
               op1=ALU.add)
            for lst, val, nm_ in ((sls, qq, "slot"), (slt, tmp_, "tslot")):
                si_ = st(f"{nm_}{kk}", 8).bitcast(I32)
                vc(nc.vector.tensor_copy, si_, val)
                lst.append(si_)
        ov = wk_(NOVF)
        V.wait(V.last)
        for jj in range(NOVF):
            v(TS, cmpb, a1, jj + 0.5, None, ALU.is_lt, after=[V.last])
            vc(nc.vector.tensor_reduce, ov[:, jj:jj + 1], cmpb, AX, ALU.add)
        vc(TS, ov, ov, 31.0, None, ALU.min)
        OVI = st("ovi", NOVF).bitcast(I32)
        vc(nc.vector.tensor_copy, OVI, ov)
        NOV = st("nov", 1).bitcast(I32)
        t_ovi = vc(nc.vector.tensor_copy, NOV, a1[:, 31:32])
        TK = wk_(8 * 16)
        TKI = TK.bitcast(I32).rearrange("p (t w) -> p t w", t=8)
        t_tk = vc(nc.vector.tensor_copy, TKI, C("tok").unsqueeze(2).to_broadcast([128, 8, 16]))
        G.wait(t_tk, t_z)
        sc_t = []
        d_sc = [DmaSem(f"d_sc{i}") for i in range(4)]
        for n in range(16):
            t, kk = n // 2, n % 2
            d = d_sc[n % 4]
            if d.n:
                G.wait((d.sem, 16 * d.n))
            nc.gpsimd.indirect_dma_start(TOKS, bass.IndirectOffsetOnAxis(slt[kk].bitcast(U32)[:, t:t + 1], 0),
                                         TKI[:, t, :], None).then_inc(d.sem, 16)
            d.n += 1
        for d in d_sc:
            G.wait((d.sem, 16 * d.n))
        IDX = st("idx", NBLK).bitcast(I32)
        t_tok = dma(G, "idx", ZI, TOKS.rearrange("(p b) w -> p (b w)", p=128))
        t_idx = v(nc.vector.tensor_copy, IDX, ZI.rearrange("p (b w) -> p b w", w=16)[:, :, 0], after=[t_tok])
        G.wait(t_idx, t_xz)

        MH, ML, MR, MX, MTH, MTL = layout(("MH", 2 * SL, F32R), ("ML", 2 * SL, F32R), ("MR", 3 * SL, F32),
                                          ("MX", SL, F32R), ("MTH", 512, F32R), ("MTL", 512, F32R))
        MTH, MTL = MTH[:, :], MTL[:, :]

        def hi4(ap, c):
            return ap[:, 128 * c:128 * c + 128]

        XB = [bc(0), bc(1)]
        assert CONSTS["ident"][0] == 0 and cst.shape[1] >= 1664
        HID = CT[:, 128:640]
        YB = [CT[:, 1152:1664], CSN[:, 0:512]]
        weg, weu, wed = X["w_e_gate_2"][0], X["w_e_up_2"][0], X["w_e_down_2"][0]
        MXH = [MX[:, 2048 * i:2048 * i + 1024].rearrange("p (c n) -> p c n", c=8) for i in range(2)]
        MXL = [MX[:, 2048 * i + 1024:2048 * i + 2048].rearrange("p (c n) -> p c n", c=8) for i in range(2)]

        def experts(blocks, free):
            xb_free, xbt_free, yb_free = [None, None], [None, None], [None, None]
            hid_free = hit_free = None
            xb_t, xbt_t, hid_t, hit_t = {}, {}, {}, {}
            first, last = blocks[0], blocks[-1]
            order = []
            for b in [*blocks, last + 1]:
                if b <= last:
                    order += [(0, b, 0), (0, b, 1), (1, b, 0), (1, b, 1)]
                if b > first:
                    order += [(2, b - 1, 0), (2, b - 1, 1)]
            NR, NH = 6, 4
            raw_t, cut_t, used = {}, {}, {}

            def fetch(i):
                if i >= len(order):
                    return
                w_, b, hf = order[i]
                src = (weg, weu, wed)[w_]
                if b < 32:
                    src = src[b]
                else:
                    e_ = nc.sync.value_load(OVI[0:1, b - 32:b - 31], min_val=0, max_val=31)
                    src = src[bass.ds(e_, 1), :, :].rearrange("a k n -> (a k) n")
                k = src.shape[0] // 2
                o = MR[:, 2048 * (i % NR):2048 * (i % NR) + 2048].rearrange("p (k n) -> p k n", k=k // 128)
                raw_t[i] = dma(S, f"mw{i % NR}", o, src[k * hf:k * hf + k, :].rearrange("(k p) n -> p k n", p=128),
                               after=[cut_t[i - NR]] if i >= NR else [free])

            def cut(i):
                if i < len(order):
                    x = MR[:, 2048 * (i % NR):2048 * (i % NR) + 2048]
                    o = (slice(None), slice(2048 * (i % NH), 2048 * (i % NH) + 2048))
                    t = a_(nc.scalar.copy, MH[o], x, after=[raw_t[i], used[i - NH] if i >= NH else free])
                    if i % 3 == 2:
                        t = g_(nc.gpsimd.tensor_tensor, ML[o], x, MH[o].bitcast(F32), ALU.subtract,
                               after=[t, used[i - NH] if i >= NH else free])
                    else:
                        t = v(nc.vector.tensor_tensor, ML[o], x, MH[o].bitcast(F32), ALU.subtract,
                              after=[t, used[i - NH] if i >= NH else free])
                    cut_t[i] = t

            def gather(b):
                name = branch[0] + f"gat{b % 2}"
                if name not in dsems:
                    dsems[name] = DmaSem("d_" + name)
                d = dsems[name]
                if d.n:
                    G.wait((d.sem, 16 * d.n))
                G.wait(xb_free[b % 2])
                nc.gpsimd.indirect_dma_start(
                    XB[b % 2], None, XZ,
                    bass.IndirectOffsetOnAxis(IDX.bitcast(U32)[:, b:b + 1], 0)).then_inc(d.sem, 16)
                d.n += 1
                xb_t[b] = (d.sem, 16 * d.n)

            def turn(b):
                for hf in range(2):
                    p_ = tr(hf, [(PS[:, hf, 128 * c:128 * c + 128],
                                  XB[b % 2][:, 512 * hf + 128 * c:512 * hf + 128 * c + 128]) for c in range(4)],
                            after=[xb_t[b]])
                    bank_free[hf] = split(MXH[b % 2][:, 4 * hf:4 * hf + 4, :], MXL[b % 2][:, 4 * hf:4 * hf + 4, :],
                                          h4(PS[:, hf, :]), after=[p_, xbt_free[b % 2]])
                xb_free[b % 2] = P.last
                xbt_t[b] = V.last

            at = [0]

            def use(k, products):
                i = at[0]
                at[0] += 1
                o = (slice(None), slice(2048 * (i % NH), 2048 * (i % NH) + 2048))
                P.wait(cut_t[i])
                used[i] = products(MH[o].rearrange("p (k n) -> p k n", k=k), ML[o].rearrange("p (k n) -> p k n", k=k))
                cut(i + 3)
                fetch(i + 3 + NR)
                return used[i]

            for i in range(NR):
                fetch(i)
            gather(first)
            gather(first + 1)
            for i in range(3):
                cut(i)
                fetch(i + NR)
            turn(first)
            for b in [*blocks, last + 1]:
                if b <= last:
                    xh, xl = MXH[b % 2], MXL[b % 2]
                    done = []
                    for bank in (2, 3):
                        for hf in range(2):
                            def gu(wh, wl):
                                return mm(bank, PS[:, bank, :],
                                          [pr_ for k in range(4) for pr_ in
                                           ((xh[:, 4 * hf + k, :], wh[:, k, :]), (xl[:, 4 * hf + k, :], wh[:, k, :]),
                                            (xh[:, 4 * hf + k, :], wl[:, k, :]))],
                                          after=[xbt_t[b]], start=(hf == 0))
                            done.append(use(4, gu))
                        if bank == 2:
                            t_silu = bank_free[2] = a_(nc.scalar.activation, HID, PS[:, 2, :], ACT.Silu,
                                                       after=[done[1], hid_free])
                    xbt_free[b % 2] = done[3]
                    hid_t[b] = bank_free[3] = v(nc.vector.tensor_tensor, HID, HID, PS[:, 3, :], ALU.mult,
                                                after=[t_silu, done[3]])
                    if b < last:
                        turn(b + 1)
                        if b + 1 < last:
                            gather(b + 2)
                if b > first:
                    for hf in range(2):
                        def dn(wh, wl):
                            for n in range(2):
                                r = mm(5 + n, PS[:, 5 + n, :],
                                       [pr_ for k in range(2) for pr_ in
                                        ((hi4(MTH, 2 * hf + k), wh[:, k, 512 * n:512 * n + 512]),
                                         (hi4(MTL, 2 * hf + k), wh[:, k, 512 * n:512 * n + 512]),
                                         (hi4(MTH, 2 * hf + k), wl[:, k, 512 * n:512 * n + 512]))],
                                       after=[hit_t[b - 1]], start=(hf == 0))
                            return r
                        use(2, dn)
                    hit_free = P.last
                    for n in range(2):
                        bank_free[5 + n] = a_(nc.scalar.copy, YB[n], PS[:, 5 + n, :], after=[hit_free, yb_free[n]])
                        yb_free[n] = dma(A, f"yo{n}", YO[128 * (b - 1):128 * b, 512 * n:512 * n + 512], YB[n],
                                         after=[A.last])
                if b <= last:
                    hid_free = tr(4, [(PS[:, 4, 128 * c:128 * c + 128], HID[:, 128 * c:128 * c + 128])
                                      for c in range(4)], after=[hid_t[b]])
                    hit_t[b] = bank_free[4] = split(MTH, MTL, PS[:, 4, :], after=[hid_free, hit_free])
            return yb_free

        A.wait(*now())
        V.wait(*now())
        G.wait(*now())
        y_out = experts(range(32), [now(), t_xz])
        for q in (P, V, A, G, S):
            q.wait(t_ovi, t_zy, *now(), *y_out)
        n_over = nc.values_load(NOV[0:1, 0:1], min_val=0, max_val=NOVF)
        with branch_of(n_over > 0):
            experts(range(32, NBLK), None)

        GB = MR[:, 0:8192].rearrange("p (n d) -> p n d", n=8)
        cg = [DmaSem(f"cg{i}") for i in range(8)]
        cg_free = [None] * 8
        odma = []
        for n in range(16):
            t, kk = n // 2, n % 2
            d = cg[n % 8]
            G.wait(cg_free[n % 8])
            if d.n:
                G.wait((d.sem, 16 * d.n))
            nc.gpsimd.indirect_dma_start(GB[:, n % 8, :], None, YO,
                                         bass.IndirectOffsetOnAxis(sls[kk].bitcast(U32)[:, t:t + 1], 0)).then_inc(d.sem, 16)
            d.n += 1
            gt = (g1, g2)[kk]
            r = vc(nc.vector.scalar_tensor_tensor, out=XRES[:, t, :], in0=GB[:, n % 8, :], scalar=gt[:, t:t + 1],
                   in1=XRES[:, t, :], op0=ALU.mult, op1=ALU.add, after=[(d.sem, 16 * d.n)])
            cg_free[n % 8] = r
            if kk:
                odma.append(dma(S, f"o{t}", out[0].rearrange("(t p) d -> p t d", p=128)[:, t, :], XRES[:, t, :],
                                after=[r]))
        S.wait(*odma)


def kernel(**inputs):
    import concourse.bacc as _bacc
    from concourse.bass_utils import run_bass_kernel_spmd as _run

    nc = _bacc.Bacc("TRN2", target_bir_lowering=False, num_devices=1)
    arrays, X = {}, {}
    for name, val in inputs.items():
        a = np.ascontiguousarray(val)
        arrays[f"in_{name}"] = a
        X[name] = nc.dram_tensor(f"in_{name}", a.shape, mybir.dt.from_np(a.dtype), kind="ExternalInput").ap()
    table = const_table()
    arrays["in_table"] = table
    cst = nc.dram_tensor("in_table", table.shape, F32, kind="ExternalInput").ap()
    out = nc.dram_tensor("out_0", (1, 1024, 1024), F32, kind="ExternalOutput").ap()
    scr = (nc.dram_tensor("xz", (1024, 1024), F32).ap(), nc.dram_tensor("toks", (NBLK * 128, 16), I32).ap(),
           nc.dram_tensor("yo", (NBLK * 128, 1024), F32).ap())
    program(nc, X, out, cst, scr)
    r = _run(nc, [arrays], core_ids=[0])
    return r.results[0]["out_0"]
```

```python
import math
from contextlib import ExitStack, contextmanager

import numpy as np

import concourse.bass as bass
from concourse import mybir

F32 = mybir.dt.float32
F32R = mybir.dt.float32r
I32 = mybir.dt.int32
U32 = mybir.dt.uint32
ALU = mybir.AluOpType
ACT = mybir.ActivationFunctionType
AX = mybir.AxisListType.X

NEG = -3.0e38
ALPHA = 2.0 ** 0.25
EPS = 1e-5
EPS2 = 1e-6
NBLK = 47
NOVF = 15
SL = 4096

CONSTS = {}


def const_table():
    p = np.arange(128)
    j, i = p[:, None], p[None, :]
    same = (j // 64) == (i // 64)
    lg = np.log(1.0 - 2.0 ** (-5.0 - np.arange(4)))
    past = (same & (j <= i)).astype(np.float64)
    mid = (i // 64) * 64 + 31
    pmid = (same & (j <= mid)).astype(np.float64)
    parts = {
        "ident": np.eye(128),
        "caus": np.where(i <= j, 0.0, NEG),
        "chm": np.where(i // 64 <= j // 64, 0.0, NEG),
        "dec": np.concatenate([np.where(i >= j, np.exp(g * np.maximum(i - j, 0)), 0.0) * 0.125 for g in lg], 1),
        "zet": np.exp(lg[None, :] * (127 - j)) * 0.125,
        "xi": np.exp(lg[None, :] * (j + 1)),
        "gc": np.tile(np.exp(lg * 128)[None, :], (128, 1)),
        "tri": np.concatenate([past, past - pmid, (same & (j > i)).astype(float)], 1) / 16.0,
        "mp": past,
        "mf": (same & (j > i)).astype(float),
        "inv": np.tile(np.concatenate([10000.0 ** (-np.arange(32) / 32), 10000.0 ** (-np.arange(16) / 16)])[None], (128, 1)),
        "su": (j < i).astype(float),
        "one": np.ones((128, 128)),
        "io": np.tile(np.arange(128.0)[None], (128, 1)),
        "thr": np.tile(128.0 * np.arange(1, 8)[None] - 0.5, (128, 1)),
        "tok": j + 128.0 * np.arange(8)[None],
    }
    at = 0
    for k, v in parts.items():
        CONSTS[k] = (at, v.shape[1])
        at += v.shape[1]
    return np.ascontiguousarray(np.concatenate(list(parts.values()), 1).astype(np.float32))


class Queue:

    def __init__(self, eng, sem):
        self.eng, self.sem, self.n, self.seen = eng, sem, 0, {}

    def wait(self, *tokens):
        for t in tokens:
            if t is None:
                continue
            if isinstance(t, list):
                self.wait(*t)
                continue
            sem, v = t
            if v > self.seen.get(id(sem), 0):
                self.eng.wait_ge(sem, v)
                self.seen[id(sem)] = v

    def mark(self, ins):
        ins.then_inc(self.sem, 1)
        self.n += 1
        return (self.sem, self.n)

    @property
    def last(self):
        return (self.sem, self.n) if self.n else None


def program(nc, X, out, cst, scr):
    ctx = ExitStack()
    with ctx:
        def sem(name):
            return ctx.enter_context(nc.semaphore(name))

        XR = ctx.enter_context(nc.sbuf_tensor("XR", [128, 2 * SL], F32))
        NC_ = cst.shape[1]
        CT = ctx.enter_context(nc.sbuf_tensor("CT", [128, NC_], F32))
        BC = ctx.enter_context(nc.sbuf_tensor("BC", [128, 4 * 1024], F32))
        ST = ctx.enter_context(nc.sbuf_tensor("ST", [128, 1280], F32))
        CSN = ctx.enter_context(nc.sbuf_tensor("CSN", [128, 768], F32))
        PS = ctx.enter_context(nc.psum_tensor("PS", [128, 8, 512], F32))

        P = Queue(nc.tensor, sem("pe"))
        V = Queue(nc.vector, sem("dve"))
        A = Queue(nc.scalar, sem("act"))
        G = Queue(nc.gpsimd, sem("pool"))
        S = Queue(nc.sync, sem("sp"))

        class DmaSem:
            def __init__(self, name):
                self.sem, self.n = sem(name), 0

        dsems = {}

        branch = [""]

        def dma(q, slot, o, i, after=()):
            slot = branch[0] + slot
            if slot not in dsems:
                dsems[slot] = DmaSem("d_" + slot)
            d = dsems[slot]
            if d.n:
                q.wait((d.sem, 16 * d.n))
            q.wait(*after)
            q.eng.dma_start(o, i).then_inc(d.sem, 16)
            d.n += 1
            return (d.sem, 16 * d.n)

        @contextmanager
        def branch_of(cond):
            qs = (P, V, A, G, S)
            kept = [(q.sem, q.n, dict(q.seen)) for q in qs]
            kept_free = (list(bank_free), dict(slot_free))
            branch[0] = "b_"
            with nc.If(cond):
                for q, nm in zip(qs, ("pe_b", "dve_b", "act_b", "pool_b", "sp_b")):
                    q.sem, q.n = sem(nm), 0
                yield
                ends = now() + [(d.sem, 16 * d.n) for nm, d in dsems.items() if nm.startswith("b_")]
                for q in qs:
                    q.wait(*ends)
            for q, (s_, n_, seen) in zip(qs, kept):
                q.sem, q.n, q.seen = s_, n_, seen
            bank_free[:] = kept_free[0]
            slot_free.clear()
            slot_free.update(kept_free[1])
            branch[0] = ""

        def now():
            return [q.last for q in (P, V, A, G)]

        area = [ExitStack(), None]
        ctx.callback(lambda: area[0].close())

        def layout(*parts):
            area[0].close()
            area[0] = ExitStack()
            assert sum(n for _, n, _ in parts) <= 9 * SL
            return [area[0].enter_context(nc.sbuf_tensor(nm, [128, n], ty)) for nm, n, ty in parts]

        area[1], = layout(("BIG", 9 * SL, F32))

        def slot(i, n=1):
            if i < 2:
                return XR[:, i * SL:(i + n) * SL]
            return area[1][:, (i - 2) * SL:(i - 2 + n) * SL]

        def C(name):
            a, n = CONSTS[name]
            return CT[:, a:a + n]

        def v(fn, *a, after=(), **k):
            V.wait(*after)
            return V.mark(fn(*a, **k))

        def a_(fn, *a, after=(), **k):
            A.wait(*after)
            return A.mark(fn(*a, **k))

        def g_(fn, *a, after=(), **k):
            G.wait(*after)
            return G.mark(fn(*a, **k))

        def vc(fn, *a, after=(), **k):
            return v(fn, *a, after=[V.last, *after], **k)

        def ac(fn, *a, after=(), **k):
            return a_(fn, *a, after=[A.last, *after], **k)

        bank_free = [None] * 8

        def mm(bank, o, pairs, after=(), start=True):
            P.wait(bank_free[bank], *after)
            for n, (l, r) in enumerate(pairs):
                ins = nc.tensor.matmul(o, l, r, start=(start and n == 0), stop=(n == len(pairs) - 1),
                                       skip_group_check=True)
            return P.mark(ins)

        def tr(bank, outs_ins, after=()):
            P.wait(bank_free[bank], *after)
            for o, i in outs_ins:
                k = i.shape[0]
                ins = nc.tensor.transpose(o, i, C("ident")[0:k, 0:k])
            return P.mark(ins)

        slot_free = {i: None for i in range(11)}

        def wload(s, src, n=None, off=0, after=()):
            k, n = src.shape[0] // 128, src.shape[1]
            view = slot(s)[:, off:off + k * n].rearrange("p (k n) -> p k n", k=k)
            t = dma(S, f"s{s}_{off}", view, src.rearrange("(k p) n -> p k n", p=128), [slot_free[s], *after])
            return view, t

        st_at = [0]
        st_names = {}

        def st(name, n):
            if name not in st_names:
                st_names[name] = (st_at[0], n)
                st_at[0] += n
                assert st_at[0] <= 1280, st_at
            a, m = st_names[name]
            assert m == n
            return ST[:, a:a + n]

        XRES = slot(0, 2).rearrange("p (t d) -> p t d", t=8)
        XT = slot(2, 2).rearrange("p (c n) -> p c n", c=8)
        U = slot(4, 2).rearrange("p (t d) -> p t d", t=8)

        def bc(i):
            return BC[:, i * 1024:(i + 1) * 1024]

        t_cst = dma(A, "cst", CT[:, :], cst)
        cols, col_at, t_cols = {}, 0, []
        ROWS = slot(10)[:, 3072:3200]
        COLS = st("cols", 83)
        x_in = X["x"][0].rearrange("(t p) d -> p t d", p=128)
        t_x = [dma(A, f"x{t}", XRES[:, t, :], x_in[:, t, :]) for t in range(8)]
        for name, src in (("c", X["c"][0]), ("lng", X["ln_in_g"]), ("lnb", X["ln_in_b"]), ("l1g", X["ln1_g"][0]),
                          ("l1b", X["ln1_b"][0]), ("nmix", X["norm_mix_2"][0]), ("ncr", X["norm_cross_2"][0]),
                          ("nmem", X["norm_mem_2"][0]), ("nffn", X["norm_ffn_2"][0]), ("gq", X["mla_q_norm"][0]),
                          ("gkv", X["mla_kv_norm"][0]), ("cqn", X["cross_q_norm_2"][0]),
                          ("ckn", X["cross_k_norm_2"][0]), ("daon", X["da_out_norm_2"][0]),
                          ("glon", X["gla_out_norm_2"][0])):
            k = src.shape[0] // 128
            t_cols.append(dma(S, "col_" + name, ROWS[col_at:col_at + k, :], src.rearrange("(k p) -> k p", p=128)))
            cols[name] = COLS[:, col_at:col_at + k]
            col_at += k
        for name, src in (("daq", "da_q_norm_2"), ("dak", "da_k_norm_2")):
            for h in range(2):
                t_cols.append(dma(S, f"col_{name}{h}", ROWS[col_at:col_at + 1, 64 * h:64 * h + 64],
                                  X[src][0].rearrange("(k p) -> k p", k=1)))
            cols[name] = COLS[:, col_at:col_at + 1]
            col_at += 1
        POSI = slot(10)[0:8, 3200:3328].bitcast(I32)
        POSR = slot(10)[0:8, 3328:3456]
        t_pos = dma(S, "pos", POSI, X["positions"][0].rearrange("(t p) -> t p", p=128))
        lam4 = BC[:, 2048:2048 + 256].rearrange("p (a n) -> p a n", a=4)
        t_lam = [dma(G, f"lam{n}", lam4[:, n, :], X[s][0].partition_broadcast(128))
                 for n, s in enumerate(("lambda_q1_2", "lambda_k1_2", "lambda_q2_2", "lambda_k2_2"))]
        posf = st("posf", 8)
        P.wait(t_cst, *t_cols)
        nc.tensor.transpose(PS[:, 7, 0:83], ROWS[0:83, :], C("ident")[0:83, 0:83])
        r = v(nc.vector.tensor_copy, POSR, POSI, after=[t_pos])
        p_ = tr(7, [(PS[:, 7, 128:136], POSR)], after=[r])
        v(nc.vector.tensor_copy, COLS, PS[:, 7, 0:83], after=[p_])
        bank_free[7] = v(nc.vector.tensor_copy, posf, PS[:, 7, 128:136])
        V.wait(t_cst, *t_lam, V.last)
        A.wait(t_cst, V.last)

        lamp = BC[:, 3072:3072 + 128].rearrange("p (a n) -> p a n", a=2)
        ls = st("ls", 2)
        v(nc.vector.tensor_tensor, lamp, lam4[:, 0:4:2, :], lam4[:, 1:4:2, :], ALU.mult)
        vc(nc.vector.tensor_reduce, ls, lamp, AX, ALU.add)
        le = st("le", 2)
        a_(nc.scalar.activation, le, ls, ACT.Exp, after=[V.last])
        nlam = st("nlam", 1)
        v(nc.vector.tensor_scalar, nlam, le[:, 1:2], le[:, 0:1], -0.2, ALU.subtract, ALU.add, after=[A.last])

        ce, cs = st("ce", 8), st("cs", 8)
        a_(nc.scalar.activation, ce, cols["c"], ACT.Exp, scale=-1.0)
        v(nc.vector.tensor_scalar, ce, ce, 1.0, None, ALU.add, after=[A.last])
        vc(nc.vector.reciprocal, ce, ce)
        vc(nc.vector.tensor_tensor, cs, ce, cols["c"], ALU.mult)
        CB = slot(10)[:, 0:1024].rearrange("p (k n) -> p k n", k=8)
        t_cb = vc(nc.vector.tensor_copy, CB, cs.unsqueeze(2).to_broadcast([128, 8, 128]))

        RA = slot(9)[:, 0:384].rearrange("p (t n) -> p t n", t=8)
        RK = slot(9)[:, 384:768].rearrange("p (t n) -> p t n", t=8)
        COS = CSN[:, 0:384].rearrange("p (t n) -> p t n", t=8)
        SIN = CSN[:, 384:768].rearrange("p (t n) -> p t n", t=8)
        V.wait(V.last)
        for t in range(8):
            v(nc.vector.tensor_scalar, RA[:, t, :], C("inv"), posf[:, t:t + 1], None, ALU.mult)
        MAGIC = 12582912.0
        vc(nc.vector.tensor_scalar, RK, RA, 1.0 / (2 * math.pi), MAGIC, ALU.mult, ALU.add)
        vc(nc.vector.tensor_scalar, RK, RK, MAGIC, None, ALU.subtract)
        C1 = 6.28125
        C2 = float(np.float32(np.floor((2 * math.pi - C1) * 2 ** 20) / 2 ** 20))
        C3 = float(np.float32(2 * math.pi - C1 - C2))
        for c in (C1, C2, C3):
            vc(nc.vector.scalar_tensor_tensor, out=RA, in0=RK, scalar=-c, in1=RA, op0=ALU.mult, op1=ALU.add)
        PI = float(np.float32(3.1415925))
        vc(nc.vector.tensor_scalar, RA, RA, PI, -PI, ALU.min, ALU.max)
        t_ra = V.last
        a_(nc.scalar.activation, SIN[:, :, :], RA, ACT.Sin, after=[t_ra])
        vc(nc.vector.scalar_tensor_tensor, out=RK, in0=RA, scalar=-1.0, in1=RA, op0=ALU.mult, op1=ALU.max)
        vc(nc.vector.tensor_scalar, RK, RK, -1.0, math.pi / 2, ALU.mult, ALU.add)
        t_cos = a_(nc.scalar.activation, COS[:, :, :], RK, ACT.Sin, after=[V.last])
        COSR, SINR = COS[:, :, 0:32], SIN[:, :, 0:32]
        COSM, SINM = COS[:, :, 32:48], SIN[:, :, 32:48]

        def rsqrt(o, x, scale, eps, after=()):
            t = v(nc.vector.tensor_scalar, o, x, scale, eps, ALU.mult, ALU.add, after=after)
            t = a_(nc.scalar.activation, o, o, ACT.Sqrt, after=[t])
            return v(nc.vector.reciprocal, o, o, after=[t])

        bst = st("bst", 12).rearrange("p (a n) -> p a n", a=2)
        mv = st("mv", 16).rearrange("p (t n) -> p t n", t=8)
        rst = st("rst", 8)

        def ln_tile(t, ready):
            for h in range(2):
                v(nc.vector.bn_stats, bst[:, h, :], XRES[:, t, 512 * h:512 * h + 512], after=[ready, V.last])
            vc(nc.vector.bn_aggr, mv[:, t, :], bst)
            r = rsqrt(rst[:, t:t + 1], mv[:, t, 1:2], 1.0, EPS, [V.last])
            return v(nc.vector.tensor_scalar, XRES[:, t, :], XRES[:, t, :], mv[:, t, 0:1], rst[:, t:t + 1],
                     ALU.subtract, ALU.mult, after=[r])

        def rms_tile(t, ready, u_free):
            s_ = ss8[:, t:t + 1]
            x_ = a_(nc.scalar.activation, U[:, t, :], XRES[:, t, :], ACT.Square, accum_out=s_, after=[ready, u_free])
            r = rsqrt(s_, s_, 1.0 / 1024, EPS2, [x_])
            return v(nc.vector.tensor_scalar, U[:, t, :], XRES[:, t, :], s_, None, ALU.mult, after=[r])

        ss8 = st("ss8", 8)

        def to_fm(src, scales, biases, ready, banks=(0, 1, 2, 3)):
            toks, ptoks, n = [], [], 0
            for th in range(2):
                for c in range(8):
                    b = banks[n % len(banks)]
                    t = tr(b, [(PS[:, b, 128 * u:128 * u + 128], src(4 * th + u, c)) for u in range(4)],
                           after=[ready[4 * th + u] for u in range(4)])
                    ptoks.append(t)
                    o = XT[:, c, 512 * th:512 * th + 512]
                    if n % 2 == 0:
                        kw = {"scale": scales(c)}
                        if biases:
                            kw["bias"] = biases(c)
                        r = a_(nc.scalar.activation, o, PS[:, b, :], ACT.Identity, after=[t], **kw)
                    elif biases:
                        r = v(nc.vector.tensor_scalar, o, PS[:, b, :], scales(c), biases(c), ALU.mult, ALU.add,
                              after=[t])
                    else:
                        r = v(nc.vector.tensor_scalar, o, PS[:, b, :], scales(c), None, ALU.mult, after=[t])
                    bank_free[b] = r
                    toks.append(r)
                    n += 1
            return toks, ptoks

        def fm_half(th, scales, ready, banks=(0, 1, 2, 3), both=True):
            toks = []
            for c in range(8):
                b = banks[c % len(banks)]
                t = tr(b, [(PS[:, b, 128 * u_:128 * u_ + 128], U[:, 4 * th + u_, 128 * c:128 * c + 128])
                           for u_ in range(4)], after=ready)
                o = XT[:, c, 512 * th:512 * th + 512]
                if both and c % 2:
                    r = v(nc.vector.tensor_scalar, o, PS[:, b, :], scales(c), None, ALU.mult, after=[t])
                else:
                    r = a_(nc.scalar.activation, o, PS[:, b, :], ACT.Copy, scale=scales(c), after=[t])
                bank_free[b] = r
                toks.append(r)
            return toks

        MODT = st("modt", 32)
        GT1, GT2 = bc(0), bc(1)
        w_ada, b_ada = X["w_ada"][0], X["b_ada"][0]
        BADA = slot(10)[:, 1024:1024 + 1024].rearrange("p (b n) -> p b n", b=2)
        MROW = slot(10)[:, 2048:2048 + 1024].rearrange("p (b n) -> p b n", b=2)
        mrow_free = [None, None]
        bada_free = [None, None]
        def modulation(n):
            ch = n
            sl = 6 + n % 3
            w, tw = wload(sl, w_ada[:, 512 * ch:512 * ch + 512])
            tb = dma(A, f"bada{n % 2}", BADA[:, n % 2, :], b_ada[512 * ch:512 * ch + 512].partition_broadcast(128),
                     after=[bada_free[n % 2]])
            b = 4 + n % 2
            t = mm(b, PS[:, b, :], [(CB[:, k, :], w[:, k, :]) for k in range(8)], after=[tw, t_cb])
            slot_free[sl] = t
            vec, half = ch // 2, ch % 2
            if vec in (2, 5):
                o = (GT1 if vec == 2 else GT2)[:, 512 * half:512 * half + 512]
                r = v(nc.vector.tensor_tensor, o, PS[:, b, :], BADA[:, n % 2, :], ALU.add, after=[t, tb])
                bank_free[b] = bada_free[n % 2] = r
            else:
                o = MROW[:, n % 2, :]
                r = v(nc.vector.tensor_tensor, o, PS[:, b, :], BADA[:, n % 2, :], ALU.add,
                      after=[t, tb, mrow_free[n % 2]])
                bank_free[b] = bada_free[n % 2] = r
                t = tr(6, [(PS[:, 6, 128 * u:128 * u + 128], o[:, 128 * u:128 * u + 128]) for u in range(4)], after=[r])
                mrow_free[n % 2] = t
                at = 8 * {0: 0, 1: 1, 3: 2, 4: 3}[vec] + 4 * half
                bank_free[6] = v(nc.vector.tensor_copy, MODT[:, at:at + 4], PS[:, 6, 0:512:128], after=[t])

        z = []
        for n in range(4):
            modulation(n)
            for t in (2 * n, 2 * n + 1):
                z.append(ln_tile(t, t_x[t]))

        def mod_cols(tag, g, b, sh, sc):
            A1, B1 = st("A" + tag, 8), st("B" + tag, 8)
            one_sc = st("osc" + tag, 8)
            vc(nc.vector.tensor_scalar, one_sc, sc, 1.0, None, ALU.add)
            vc(nc.vector.tensor_tensor, A1, g, one_sc, ALU.mult)
            vc(nc.vector.tensor_tensor, B1, b, one_sc, ALU.mult)
            vc(nc.vector.tensor_tensor, B1, B1, sh, ALU.add)
            return A1, B1

        A1, B1 = mod_cols("1", cols["lng"], cols["lnb"], MODT[:, 0:8], MODT[:, 8:16])

        V.wait(V.last)
        A.wait(V.last)
        t_bc2 = dma(G, "bc2", bc(2), X["ln_in_g"].partition_broadcast(128), after=now())
        t_bc3 = dma(G, "bc3", bc(3), X["ln_in_b"].partition_broadcast(128), after=now())
        xt1, xt1p = to_fm(lambda t, c: XRES[:, t, 128 * c:128 * c + 128], lambda c: A1[:, c:c + 1],
                          lambda c: B1[:, c:c + 1], z + [])

        def affine_pool(ready, gb, gbt, bb, bbt):
            toks = []
            G.wait(*ready)
            for t in range(8):
                r = g_(nc.gpsimd.tensor_tensor, XRES[:, t, :], XRES[:, t, :], gb, ALU.mult, after=[gbt])
                toks.append(g_(nc.gpsimd.tensor_tensor, XRES[:, t, :], XRES[:, t, :], bb, ALU.add, after=[r, bbt]))
            return toks

        x0 = affine_pool(xt1p, bc(2), t_bc2, bc(3), t_bc3)
        for n in range(4, 12):
            modulation(n)
        A2, B2 = mod_cols("2", cols["l1g"], cols["l1b"], MODT[:, 16:24], MODT[:, 24:32])

        w_in = X["w_in"][0]
        LAT = slot(10)[:, 0:8 * 416].rearrange("p (t n) -> p t n", t=8)
        V.wait(*now())
        A.wait(*now())
        w, tw = wload(6, w_in[:, 0:416])
        lss = st("lss", 16).rearrange("p (t n) -> p t n", t=8)
        TMP = slot(9)[:, 0:2048]
        for t in range(8):
            b = t % 4
            tk = mm(b, PS[:, b, 0:416], [(XT[:, k, 128 * t:128 * t + 128], w[:, k, :]) for k in range(8)],
                    after=[tw, xt1])
            a_(nc.scalar.activation, TMP[:, 0:256], PS[:, b, 0:256], ACT.Square, accum_out=lss[:, t, 0:1],
               after=[tk, A.last])
            r1 = ac(nc.scalar.activation, TMP[:, 0:128], PS[:, b, 256:384], ACT.Square, accum_out=lss[:, t, 1:2])
            r2 = v(nc.vector.tensor_copy, LAT[:, t, :], PS[:, b, 0:416], after=[tk, r1])
            bank_free[b] = r2
        slot_free[6] = P.last
        lr = st("lr", 16).rearrange("p (t n) -> p t n", t=8)
        v(nc.vector.tensor_scalar, lr[:, :, 0], lss[:, :, 0], 1.0 / 256, EPS, ALU.mult, ALU.add, after=[A.last])
        v(nc.vector.tensor_scalar, lr[:, :, 1], lss[:, :, 1], 1.0 / 128, EPS, ALU.mult, ALU.add)
        a_(nc.scalar.activation, lr, lr, ACT.Sqrt, after=[V.last])
        v(nc.vector.reciprocal, lr, lr, after=[A.last])
        V.wait(V.last)
        for t in range(8):
            v(nc.vector.tensor_scalar, LAT[:, t, 0:256], LAT[:, t, 0:256], lr[:, t, 0:1], None, ALU.mult)
            v(nc.vector.tensor_scalar, LAT[:, t, 256:384], LAT[:, t, 256:384], lr[:, t, 1:2], None, ALU.mult)
        t_latn = V.last
        KR = st("kr", 256).rearrange("p (t n) -> p t n", t=8)
        T1 = TMP[:, 256:384].rearrange("p (t n) -> p t n", t=8)
        T2 = TMP[:, 384:512].rearrange("p (t n) -> p t n", t=8)
        V.wait(t_cos)

        def rotate(o1, o2, x1, x2, co, si, t1, t2, after=()):
            v(nc.vector.tensor_tensor, t1, x1, co, ALU.mult, after=[V.last, *after])
            v(nc.vector.tensor_tensor, t2, x2, si, ALU.mult)
            vc(nc.vector.tensor_tensor, o1, t1, t2, ALU.subtract)
            v(nc.vector.tensor_tensor, t1, x2, co, ALU.mult, after=[V.last])
            v(nc.vector.tensor_tensor, t2, x1, si, ALU.mult)
            return vc(nc.vector.tensor_tensor, o2, t1, t2, ALU.add)

        t_kr = rotate(KR[:, :, 0:16], KR[:, :, 16:32], LAT[:, :, 384:400], LAT[:, :, 400:416], COSM, SINM, T1, T2)

        wqk, tqk = wload(7, w_in[:, 416:928])
        wv, twv = wload(8, w_in[:, 928:1440])
        wg, twg = wload(6, w_in[:, 1440:1952])
        SG = slot(4).rearrange("p (t n) -> p t n", t=8)
        RO = slot(5).rearrange("p (t n) -> p t n", t=8)
        R = slot(9)
        QK, RQK = R[:, 0:512], R[:, 512:1024]
        TA, TB = R[:, 1024:1280], R[:, 1280:1536]
        QKT = R[0:64, 1536:2560]
        SC = R[:, 2560:3072]
        KZ = R[:, 3072:3328]
        STA = R[0:64, 3328:3840]
        VT = slot(10)[:, 3328:3840]
        V.wait(V.last)
        v(nc.vector.memset, STA, 0.0)
        mvr = st("mvr", 64).rearrange("p (t n) -> p t n", t=8)
        bs4 = st("bs4", 24).rearrange("p (h n) -> p h n", h=4)
        st_free = [None]

        def b4(ap, n, parts=128):
            return ap.unsqueeze(2).to_broadcast([parts, ap.shape[1], n])

        def silu_into(o, ps, after):
            t = a_(nc.scalar.activation, o, ps, ACT.Exp, scale=-1.0, after=after)
            t = v(nc.vector.tensor_scalar, o, o, 1.0, None, ALU.add, after=[t])
            t = v(nc.vector.reciprocal, o, o, after=[t])
            return v(nc.vector.tensor_tensor, o, o, ps, ALU.mult, after=[t])

        t_inner = t_kvm = None
        for t in range(8):
            xt = [XT[:, k, 128 * t:128 * t + 128] for k in range(8)]
            p0 = mm(0, PS[:, 0, :], [(xt[k], wqk[:, k, :]) for k in range(8)], after=[tqk])
            p1 = mm(1, PS[:, 1, :], [(xt[k], wv[:, k, :]) for k in range(8)], after=[twv])
            p2 = mm(2, PS[:, 2, :], [(xt[k], wg[:, k, :]) for k in range(8)], after=[twg])
            bank_free[0] = a_(nc.scalar.copy, QK, PS[:, 0, :], after=[p0, V.last])
            tqk_ = bank_free[0]
            tv = bank_free[1] = a_(nc.scalar.copy, VT, PS[:, 1, :], after=[p1, t_inner, t_kvm])
            q3 = QK.rearrange("p (h n) -> p h n", h=8)
            r3 = RQK.rearrange("p (h n) -> p h n", h=8)
            co = COSR[:, t, :].unsqueeze(1).to_broadcast([128, 8, 32])
            si = SINR[:, t, :].unsqueeze(1).to_broadcast([128, 8, 32])
            ta = TA.rearrange("p (h n) -> p h n", h=8)
            tb = TB.rearrange("p (h n) -> p h n", h=8)
            tr_ = rotate(r3[:, :, 0:32], r3[:, :, 32:64], q3[:, :, 0:32], q3[:, :, 32:64], co, si, ta, tb,
                         after=[tqk_, P.last])
            pq = tr(3, [(PS[0:64, 3, 128 * h:128 * h + 128], RQK[:, 64 * h:64 * h + 64]) for h in range(4)], [tr_])
            pk = tr(4, [(PS[0:64, 4, 128 * h:128 * h + 128], RQK[:, 256 + 64 * h:320 + 64 * h]) for h in range(4)])
            bank_free[3] = eq = a_(nc.scalar.copy, QKT[:, 0:512], PS[0:64, 3, :], after=[pq])
            bank_free[4] = ek = a_(nc.scalar.copy, QKT[:, 512:1024], PS[0:64, 4, :], after=[pk])
            tkz = v(nc.vector.tensor_tensor, KZ.rearrange("p (h n) -> p h n", h=4),
                    RQK[:, 256:512].rearrange("p (h n) -> p h n", h=4), b4(C("zet"), 64), ALU.mult, after=[t_kvm, tr_])
            for h in range(4):
                ps_ = mm(5, PS[:, 5, 128 * h:128 * h + 128],
                         [(QKT[:, 512 + 128 * h:640 + 128 * h], QKT[:, 128 * h:128 * h + 128])], after=[eq, ek])
            for h in range(4):
                pc = mm(6, PS[:, 6, 128 * h:128 * h + 128],
                        [(QKT[:, 128 * h:128 * h + 128], STA[:, 128 * h:128 * h + 128])], after=[st_free[0], V.last])
            tsc = bank_free[5] = v(nc.vector.tensor_tensor, SC, PS[:, 5, :], C("dec"), ALU.mult, after=[ps_])
            for h in range(4):
                t_kvm = mm(3, PS[0:64, 3, 128 * h:128 * h + 128],
                           [(KZ[:, 64 * h:64 * h + 64], VT[:, 128 * h:128 * h + 128])], after=[tkz, tv])
            for h in range(4):
                t_inner = mm(7, PS[:, 7, 128 * h:128 * h + 128],
                             [(SC[:, 128 * h:128 * h + 128], VT[:, 128 * h:128 * h + 128])], after=[tsc])
            s4 = STA.rearrange("p (h n) -> p h n", h=4)
            v(nc.vector.tensor_tensor, s4, s4, b4(C("gc")[0:64, :], 128, 64), ALU.mult, after=[pc, V.last])
            st_free[0] = bank_free[3] = vc(nc.vector.tensor_tensor, STA, STA, PS[0:64, 3, :], ALU.add, after=[t_kvm])
            o3 = RO[:, t, :].rearrange("p (h n) -> p h n", h=4)
            bank_free[6] = v(nc.vector.tensor_tensor, o3, PS[:, 6, :].rearrange("p (h n) -> p h n", h=4),
                             b4(C("xi"), 128), ALU.mult, after=[pc])
            bank_free[7] = vc(nc.vector.tensor_tensor, RO[:, t, :], RO[:, t, :], PS[:, 7, :], ALU.add,
                              after=[t_inner])
            V.wait(V.last)
            for h in range(4):
                v(nc.vector.bn_stats, bs4[:, h, :], o3[:, h, :])
            V.wait(V.last)
            for h in range(4):
                v(nc.vector.bn_aggr, mvr[:, t, 2 * h:2 * h + 2], bs4[:, h, :])
            bank_free[2] = silu_into(SG[:, t, :], PS[:, 2, :], [p2])
        slot_free[6] = slot_free[7] = slot_free[8] = P.last
        t_xt_free = P.last
        rsr = st("rsr", 32)
        mvr2 = mvr.rearrange("p t (h n) -> p (t h) n", n=2)
        tr_ = rsqrt(rsr, mvr2[:, :, 1], 1.0, EPS, [V.last])
        G.wait(*x0)
        t_gn = [dma(G, "bc2", bc(2)[:, 0:512], X["ret_gn_g"][0].partition_broadcast(128), after=x0),
                dma(G, "gnb", bc(2)[:, 512:1024], X["ret_gn_b"][0].partition_broadcast(128), after=x0)]

        def finish_retention(t):
            o3 = RO[:, t, :].rearrange("p (h n) -> p h n", h=4)
            m = mvr2[:, 4 * t:4 * t + 4, 0]
            vc(nc.vector.tensor_tensor, o3, o3, b4(m, 128), ALU.subtract)
            r = vc(nc.vector.tensor_tensor, o3, o3, b4(rsr[:, 4 * t:4 * t + 4], 128), ALU.mult)
            r = g_(nc.gpsimd.tensor_tensor, RO[:, t, :], RO[:, t, :], bc(2)[:, 0:512], ALU.mult, after=[r, *t_gn])
            r = g_(nc.gpsimd.tensor_tensor, RO[:, t, :], RO[:, t, :], bc(2)[:, 512:1024], ALU.add, after=[r])
            return g_(nc.gpsimd.tensor_tensor, RO[:, t, :], RO[:, t, :], SG[:, t, :], ALU.mult, after=[r])


        QNT = slot(9)[:, 0:2048].rearrange("p (c n) -> p c n", c=2)
        VA = slot(9)[:, 2048:4096].rearrange("p (t n) -> p t n", t=8)
        KVT = bc(3)
        QT = slot(2).rearrange("p (h n) -> p h n", h=4)
        KT = slot(3).rearrange("p (h n) -> p h n", h=4)
        A.wait(*now())
        V.wait(*now())
        n = 0
        lat_t = []
        for c in range(3):
            for th in range(2):
                b = n % 2
                t = tr(b, [(PS[:, b, 128 * u:128 * u + 128], LAT[:, 4 * th + u, 128 * c:128 * c + 128])
                           for u in range(4)], after=[t_latn])
                o = (QNT[:, c, :] if c < 2 else KVT)[:, 512 * th:512 * th + 512]
                sc = cols["gq"][:, c:c + 1] if c < 2 else cols["gkv"][:, 0:1]
                bank_free[b] = a_(nc.scalar.activation, o, PS[:, b, :], ACT.Copy, scale=sc, after=[t])
                lat_t.append(A.last)
                n += 1
        wu = slot(6)[:, 0:1536].rearrange("p (k n) -> p k n", k=2)
        twu = dma(S, "s6_0", wu, X["w_uq"][0].rearrange("(k p) n -> p k n", p=128), [slot_free[6]])
        wk = slot(6)[:, 1536:2560]
        twk = dma(S, "s6_b", wk, X["w_ukv"][0], [slot_free[6]])
        TM = [(slot(10)[:, a:a + 384].rearrange("p (h n) -> p h n", h=4),
               slot(10)[:, a + 384:a + 768].rearrange("p (h n) -> p h n", h=4)) for a in (0, 1024)]
        MT1 = slot(10)[:, 768:832].rearrange("p (h n) -> p h n", h=4)
        MT2 = slot(10)[:, 832:896].rearrange("p (h n) -> p h n", h=4)
        PB = [slot(10)[:, 0:1024], slot(10)[:, 1024:2048]]
        PTB = [slot(10)[:, 2048:3072], slot(10)[:, 3072:4096]]
        AO = slot(4).rearrange("p (t n) -> p t n", t=8)

        sm = st("sm", 32)

        def attention(items, qk, mask, scale, PBUF, PTBUF, vsrc, ov, out_fn, nmap=1, combine=None):
            p_free = [[None] * nmap, [None] * nmap]
            pt_free = [None, None]
            S_t, P_t, T_t = {}, {}, {}
            sm_n = [0]
            for n in range(len(items) + 2):
                if n < len(items):
                    h, i = items[n]
                    nk = 128 * (i + 1)
                    P_t[n] = []
                    for m in range(nmap):
                        sb = 2 * (n % 2) if nmap == 1 else 2 * m + (n % 2 if nk <= 512 else 0)
                        nb = 1 if nk <= 512 else 2
                        tq = None
                        for c0 in range(0, nk, 512):
                            c1 = min(nk, c0 + 512)
                            b = sb + c0 // 512
                            tq = mm(b, PS[:, b, 0:c1 - c0], [qk(h, i, m, c0, c1)])
                        flat = PS[:, sb:sb + nb, :].rearrange("p b n -> p (b n)")
                        d = flat[:, nk - 128:nk]
                        t = v(nc.vector.tensor_tensor, d, d, mask, ALU.add, after=[tq])
                        k = 4 * (sm_n[0] % 8)
                        sm_n[0] += 1
                        mx, bi, rs, ri = (sm[:, k + z:k + z + 1] for z in range(4))
                        vc(nc.vector.tensor_reduce, mx, flat[:, 0:nk], AX, ALU.max)
                        t = vc(nc.vector.tensor_scalar, bi, mx, -scale, None, ALU.mult)
                        pb = PBUF[n % 2][m]
                        t = a_(nc.scalar.activation, pb[:, 0:nk], flat[:, 0:nk], ACT.Exp, bias=bi, scale=scale,
                               accum_out=rs, after=[t, p_free[n % 2][m]])
                        for b in range(sb, sb + nb):
                            bank_free[b] = t
                        P_t[n].append([t, ri, rs])
                if 1 <= n <= len(items):
                    k = n - 1
                    h, i = items[k]
                    src, ts = S_t[k]
                    T_t[k] = []
                    for g0 in range(0, i + 1, 4):
                        g1 = min(i + 1, g0 + 4)
                        b = 4 + (g0 // 4)
                        t = tr(b, [(PS[:, b, 128 * (j - g0):128 * (j - g0) + 128], src[:, 128 * j:128 * j + 128])
                                   for j in range(g0, g1)], after=[ts])
                        o = PTBUF[k % 2][:, 128 * g0:128 * g1]
                        w_ = 128 * (g1 - g0)
                        if g0 == 0:
                            r = a_(nc.scalar.copy, o, PS[:, b, 0:w_], after=[t, pt_free[k % 2]])
                        else:
                            r = v(nc.vector.tensor_copy, o, PS[:, b, 0:w_], after=[t, pt_free[k % 2]])
                        bank_free[b] = r
                        T_t[k].append(r)
                    for m in range(nmap):
                        p_free[k % 2][m] = P.last
                    if combine:
                        combine.free[k % 2] = P.last
                if n >= 2:
                    k = n - 2
                    h, i = items[k]
                    b = 6 + k % 2
                    t = mm(b, PS[:, b, 0:ov], [(PTBUF[k % 2][:, 128 * j:128 * j + 128], vsrc(h, j))
                                               for j in range(i + 1)], after=[T_t[k]])
                    pt_free[k % 2] = t
                    bank_free[b] = out_fn(h, i, PS[:, b, 0:ov], t, P_t[k])
                if n < len(items):
                    S_t[n] = (PBUF[n % 2][0], P_t[n][0][0])
                    for e in P_t[n]:
                        e[0] = v(nc.vector.reciprocal, e[1], e[2], after=[e[0]])
                    if combine:
                        S_t[n] = combine(n, 128 * (items[n][1] + 1), P_t[n])

        for g in range(2):
            A.wait(*now())
            V.wait(*now())
            if g:
                G.wait(*now())
            tm_free = [None, None]
            tm_t = {}

            def turn_heads(t):
                QTM, KTM = TM[t % 2]
                p1 = tr(2, [(PS[0:96, 2, 128 * h:128 * h + 128], QTM[:, h, :]) for h in range(4)], after=[tm_t[t]])
                p2 = tr(3, [(PS[0:96, 3, 128 * h:128 * h + 128], KTM[:, h, :]) for h in range(4)])
                tm_free[t % 2] = p2
                bank_free[2] = a_(nc.scalar.copy, QT[0:96, :, 128 * t:128 * t + 128],
                                  PS[0:96, 2, :].rearrange("p (h n) -> p h n", h=4), after=[p1])
                bank_free[3] = v(nc.vector.tensor_copy, KT[0:96, :, 128 * t:128 * t + 128],
                                 PS[0:96, 3, :].rearrange("p (h n) -> p h n", h=4), after=[p2])

            for t in range(8):
                QTM, KTM = TM[t % 2]
                b0 = 4 * (t % 2)
                pq = mm(b0, PS[:, b0, 0:384], [(QNT[:, k, 128 * t:128 * t + 128], wu[:, k, 384 * g:384 * g + 384])
                                            for k in range(2)], after=[twu, lat_t])
                pk = mm(b0 + 1, PS[:, b0 + 1, :], [(KVT[:, 128 * t:128 * t + 128], wk[:, 512 * g:512 * g + 512])], after=[twk])
                q3 = PS[:, b0, 0:384].rearrange("p (h n) -> p h n", h=4)
                k3 = PS[:, b0 + 1, :].rearrange("p (h n) -> p h n", h=4)
                a_(nc.scalar.copy, QTM[:, :, 0:64], q3[:, :, 0:64], after=[pq, tm_free[t % 2]])
                a_(nc.scalar.copy, KTM[:, :, 0:64], k3[:, :, 0:64], after=[pk])
                a_(nc.scalar.copy, KTM[:, :, 64:96], KR[:, t, :].unsqueeze(1).to_broadcast([128, 4, 32]), after=[t_kr])
                bank_free[b0 + 1] = a_(nc.scalar.copy, VA[:, t, :].rearrange("p (h n) -> p h n", h=4),
                                        k3[:, :, 64:128])
                co = COSM[:, t, :].unsqueeze(1).to_broadcast([128, 4, 16])
                si = SINM[:, t, :].unsqueeze(1).to_broadcast([128, 4, 16])
                r = rotate(QTM[:, :, 64:80], QTM[:, :, 80:96], q3[:, :, 64:80], q3[:, :, 80:96], co, si, MT1, MT2,
                           after=[pq, A.last, tm_free[t % 2]])
                bank_free[b0] = r
                tm_t[t] = [r, A.last]
                if t:
                    turn_heads(t - 1)
                if g == 0:
                    t_ro = finish_retention(t)
            turn_heads(7)
            A.wait(*now())
            V.wait(*now())
            P.wait(*now())

            def mla_qk(h, i, m, c0, c1):
                return (QT[0:96, h, 128 * i:128 * i + 128], KT[0:96, h, c0:c1])

            def mla_out(h, i, o, t, pt):
                o = o[:, 64 * (h % 2):64 * (h % 2) + 64]
                return v(nc.vector.tensor_scalar, AO[:, i, 256 * g + 64 * h:256 * g + 64 * h + 64], o, pt[0][1], None,
                         ALU.mult, after=[t, pt[0][0]])

            attention([(h, i) for i in range(8) for h in range(4)], mla_qk, C("caus"), 96.0 ** -0.5,
                      [[PB[0]], [PB[1]]], PTB, lambda h, j: VA[:, j, 128 * (h // 2):128 * (h // 2) + 128], 128, mla_out)
        slot_free[6] = P.last

        def split(hi, lo, x, after=(), hi_after=(), lo_after=()):
            t = a_(nc.scalar.copy, hi, x, after=[*after, *hi_after])
            return v(nc.vector.tensor_tensor, lo, x, hi.bitcast(F32), ALU.subtract, after=[t, *after, *lo_after])

        def mm3(bank, o, quads, after=(), start=True):
            pairs = []
            for lh, ll, rh, rl in quads:
                pairs += [(lh, rh), (ll, rh), (lh, rl)]
            return mm(bank, o, pairs, after=after, start=start)

        def project(wd, src, scales, evac, ready, fetch_ready, xh, xl, wr, wh, wl, lo_free, after_tile):
            xh3, xl3 = (x.rearrange("p (c n) -> p c n", c=8) for x in (xh, xl))
            free = [None, None]
            raw_t, cut_t = {}, {}

            def half(x, i):
                return x[:, 2048 * (i % 2):2048 * (i % 2) + 2048]

            def fetch(i):
                raw_t[i] = dma(S, f"fw{i % 2}", half(wr, i).rearrange("p (k n) -> p k n", k=8),
                               wd[:, 256 * i:256 * i + 256].rearrange("(k p) n -> p k n", p=128),
                               after=[cut_t[i - 2]] if i >= 2 else [fetch_ready])

            def cut(i):
                cut_t[i] = split(half(wh, i), half(wl, i), half(wr, i), after=[raw_t[i], free[i % 2]],
                                 lo_after=[lo_free[0]])

            fetch(0)
            fetch(1)
            toks = []
            for th in range(2):
                for c in range(8):
                    b = c % 4
                    t = tr(b, [(PS[:, b, 128 * u:128 * u + 128], src(4 * th + u, c)) for u in range(4)], after=ready[4 * th:4 * th + 4])
                    o = (slice(None), c, slice(512 * th, 512 * th + 512))
                    r = a_(nc.scalar.activation, xh3[o], PS[:, b, :], ACT.Copy, scale=scales(c), after=[t])
                    bank_free[b] = r = v(nc.vector.scalar_tensor_tensor, out=xl3[o], in0=PS[:, b, :], scalar=scales(c),
                                         in1=xh3[o].bitcast(F32), op0=ALU.mult, op1=ALU.subtract, after=[r])
                    toks.append(r)
            lo_free[0] = t_src = P.last
            cut(0)
            cut(1)
            steps = [(n, t) for n in range(2) for t in range(8)] + [(n, t) for t in range(8) for n in (2, 3)]
            last = []
            for k_, (n, t) in enumerate(steps):
                b = 4 + k_ % 4
                h_, l_ = (half(x, n).rearrange("p (k n) -> p k n", k=8) for x in (wh, wl))
                tk = mm3(b, PS[:, b, 0:256], [(xh3[:, k, 128 * t:128 * t + 128], xl3[:, k, 128 * t:128 * t + 128],
                                               h_[:, k, :], l_[:, k, :]) for k in range(8)],
                         after=[cut_t[n], toks[8 * (t // 4):8 * (t // 4) + 8]])
                bank_free[b] = r = evac(t, n, PS[:, b, 0:256], tk)
                if n == 3:
                    last.append(after_tile(t, r, t_src))
                if t == 0 and n < 2:
                    fetch(n + 2)
                if t == 7 and n < 2:
                    free[n] = tk
                    cut(n + 2)
            return last

        def residual(gt, alpha, ready, tmp):
            k = [0]

            def f(t, n, ps, tk):
                w_ = ps.shape[1]
                x = XRES[:, t, w_ * n:w_ * n + w_]
                o = tmp[k[0] % len(tmp)][:, 0:w_]
                k[0] += 1
                v(nc.vector.tensor_tensor, o, ps, gt[:, w_ * n:w_ * n + w_], ALU.mult, after=[tk, ready])
                if alpha is None:
                    vc(nc.vector.tensor_tensor, x, x, o, ALU.add)
                else:
                    vc(nc.vector.scalar_tensor_tensor, out=x, in0=x, scalar=alpha, in1=o, op0=ALU.mult, op1=ALU.add)
                return V.last
            return f

        A.wait(*now())
        V.wait(*now())
        MIX = [slot(4).rearrange("p (t n) -> p t n", t=8), slot(5).rearrange("p (t n) -> p t n", t=8)]
        one1 = C("one")[:, 0:1]
        OXH, OXL, OWR, OWH, OWL = (x[:, :] for x in layout(
            ("OXH", 2 * SL, F32R), ("OPAD", 2 * SL, F32), ("OXL", 2 * SL, F32R), ("OWR", SL, F32),
            ("OWH", SL, F32R), ("OWL", SL, F32R)) if "PAD" not in x.name)
        PT_ = [bc(2)[:, 0:512], bc(2)[:, 512:1024]]
        xr = project(X["w_out"][0], lambda t, c: MIX[c // 4][:, t, 128 * (c % 4):128 * (c % 4) + 128], lambda c: one1,
                     residual(GT1, ALPHA, x0, PT_), [now()] * 8, [t_xt_free, x0], OXH, OXL, OWR, OWH, OWL, [None],
                     lambda t, r, _: ln_tile(t, r))
        z = xr
        t_bc2 = dma(G, "bc2", bc(2), X["ln1_g"][0].partition_broadcast(128), after=now())
        t_bc3 = dma(G, "bc3", bc(3), X["ln1_b"][0].partition_broadcast(128), after=now())
        A.wait(P.last)
        V.wait(P.last)
        FXH, FXL, FHH, FHL, FWR, FWH, FWL = layout(
            ("FXH", 2 * SL, F32R), ("FXL", 2 * SL, F32R), ("FHH", SL, F32R), ("FHL", SL, F32R),
            ("FWR", SL, F32), ("FWH", SL, F32R), ("FWL", SL, F32R))

        XHH = FXH[:, :].rearrange("p (c n) -> p c n", c=8)
        XLL = FXL[:, :].rearrange("p (c n) -> p c n", c=8)
        QB = [CSN[:, 0:512], C("dec")]
        qb_free = [None, None]
        qn = [0]
        xt2, xt2p = [], []
        pre = now()
        wr_free, wh_free = [pre] * 2, [pre] * 2
        w1, w2 = X["w_ff1"][0], X["w_ff2"][0]
        chunks = []
        for g in range(8):
            for cc in range(2):
                chunks.append(w1[:, 512 * g + 256 * cc:512 * g + 256 * cc + 256])
            for n in range(2):
                chunks.append(w2[512 * g:512 * g + 512, 512 * n:512 * n + 512])
        raw_t, cut_t = {}, {}

        def chunk(t_, i, k):
            return t_[:, 2048 * (i % 2):2048 * (i % 2) + 2048].rearrange("p (k n) -> p k n", k=k)

        def fetch(i):
            if i < len(chunks):
                k = 8 if i % 4 < 2 else 4
                raw_t[i] = dma(S, f"fw{i % 2}", chunk(FWR, i, k), chunks[i].rearrange("(k p) n -> p k n", p=128),
                               after=[wr_free[i % 2]])

        def cut(i):
            if i < len(chunks):
                o = (slice(None), slice(2048 * (i % 2), 2048 * (i % 2) + 2048))
                wr_free[i % 2] = cut_t[i] = split(FWH[o], FWL[o], FWR[o], after=[raw_t[i], wh_free[i % 2]])

        fetch(0)
        fetch(1)
        A.wait(pre)
        V.wait(pre)
        for th in range(2):
            for c in range(8):
                b = qn[0] % 4
                i_ = qn[0] % 2
                qn[0] += 1
                t = tr(b, [(PS[:, b, 128 * u:128 * u + 128], XRES[:, 4 * th + u, 128 * c:128 * c + 128])
                           for u in range(4)], after=[z[4 * th + u] for u in range(4)])
                xt2p.append(t)
                o = (slice(None), c, slice(512 * th, 512 * th + 512))
                r = a_(nc.scalar.activation, XHH[o], PS[:, b, :], ACT.Identity, scale=A2[:, c:c + 1],
                       bias=B2[:, c:c + 1], after=[t])
                bank_free[b] = v(nc.vector.tensor_scalar, QB[i_], PS[:, b, :], A2[:, c:c + 1], B2[:, c:c + 1],
                                 ALU.mult, ALU.add, after=[t, r, V.last])
                qb_free[i_] = t = vc(nc.vector.tensor_tensor, XLL[o], QB[i_], XHH[o].bitcast(F32), ALU.subtract)
                xt2.append(t)
        PT_ = [bc(0)[:, 0:512], bc(0)[:, 512:1024]]
        cut(0)
        x1 = []
        g2b = [None, None]
        HHH = FHH[:, :].rearrange("p (c n) -> p c n", c=4)
        HLL = FHL[:, :].rearrange("p (c n) -> p c n", c=4)
        ci = 0
        hq = None
        h_free = None

        area[1], = layout(("BIG2", 9 * SL, F32))
        XT = slot(2, 2).rearrange("p (c n) -> p c n", c=8)
        U = slot(4, 2).rearrange("p (t d) -> p t d", t=8)
        x2, u, xt3 = [], [], []
        nm = cols["nmix"]

        def finish_tile(t, tok):
            r = ln_tile(t, tok)
            x = XRES[:, t, :]
            r = (g_, v)[t % 2](((nc.gpsimd, nc.vector)[t % 2]).tensor_tensor, x, x, bc(2), ALU.mult, after=[r, t_bc2])
            x2.append(g_(nc.gpsimd.tensor_tensor, x, x, bc(3), ALU.add, after=[r, t_bc3]))
            if t:
                u.append(rms_tile(t - 1, x2[t - 1], x_free))
            if t == 5:
                A.wait(x_free)
                xt3.append(fm_half(0, lambda c: nm[:, c:c + 1], u[0:4], both=False))

        def finish(item):
            o, i_, t = item
            qb_free[i_] = r = split(HHH[o], HLL[o], QB[i_], after=[t], hi_after=[h_free])
            return r

        for g in range(8):
            h_t = []
            for cc in range(2):
                wh, wl = chunk(FWH, ci, 8), chunk(FWL, ci, 8)
                for fb in range(2):
                    for th in range(2):
                        b = (fb * 2 + th) % 4
                        tk = mm3(b, PS[:, b, :], [(wh[:, k, 128 * fb:128 * fb + 128], wl[:, k, 128 * fb:128 * fb + 128],
                                                   XHH[:, k, 512 * th:512 * th + 512], XLL[:, k, 512 * th:512 * th + 512])
                                                  for k in range(8)], after=[cut_t[ci], xt2[8 * th:8 * th + 8]])
                        i_ = qn[0] % 2
                        qn[0] += 1
                        r = a_(nc.scalar.activation, QB[i_], PS[:, b, :], ACT.Relu, after=[tk, qb_free[i_]])
                        bank_free[b] = r
                        r = g_(nc.gpsimd.tensor_tensor, QB[i_], QB[i_], QB[i_], ALU.mult, after=[r])
                        if g == 0:
                            x_ = XRES[:, len(x1), :]
                            t = g_(nc.gpsimd.tensor_tensor, x_, x_, bc(2), ALU.mult, after=[t_bc2, *xt2p])
                            x1.append(g_(nc.gpsimd.tensor_tensor, x_, x_, bc(3), ALU.add, after=[t, t_bc3]))
                        h_t.append(finish(((slice(None), 2 * cc + fb, slice(512 * th, 512 * th + 512)), i_, r)))
                        if fb == 0 and th == 0:
                            fetch(ci + 2)
                            cut(ci + 1)
                wh_free[ci % 2] = P.last
                ci += 1
            if g == 0:
                ZT = bc(2)
                g_(nc.gpsimd.memset, ZT, 0.0, after=x1)
                t_zy = dma(G, "zy", scr[1][32 * 128:, :].rearrange("(b p) d -> p b d", p=128),
                           ZT.unsqueeze(1).to_broadcast([128, NOVF, 1024]), after=[G.last])
                t_bc2 = dma(G, "bc2", bc(2), X["ln2_g"][0].partition_broadcast(128), after=[t_zy])
                t_bc3 = dma(G, "bc3", bc(3), X["ln2_b"][0].partition_broadcast(128), after=x1)
            x_free = P.last
            ev = residual(GT2, ALPHA if g == 0 else None, x1, PT_)
            steps = [(n, t) for t in range(8) for n in range(2)] if g == 7 else \
                    [(n, t) for n in range(2) for t in range(8)]
            if g == 7:
                cut(ci + 1)
            for k_, (n, t) in enumerate(steps):
                wh, wl = chunk(FWH, ci + n, 4), chunk(FWL, ci + n, 4)
                b = 4 + k_ % 4
                tk = mm3(b, PS[:, b, :], [(HHH[:, k, 128 * t:128 * t + 128], HLL[:, k, 128 * t:128 * t + 128],
                                           wh[:, k, :], wl[:, k, :]) for k in range(4)],
                         after=[cut_t[ci + n], h_t])
                bank_free[b] = ev(t, n, PS[:, b, :], tk)
                if g == 7:
                    if n == 1:
                        finish_tile(t, bank_free[b])
                    continue
                if t == 0:
                    fetch(ci + n + 2)
                    cut(ci + n + 1)
                if t == 7:
                    wh_free[(ci + n) % 2] = P.last
            ci += 2
            h_free = P.last
        for s_ in slot_free:
            slot_free[s_] = P.last
        slot_free[8] = cut_t[31]

        u.append(rms_tile(7, x2[7], x_free))
        A.wait(x_free)
        V.wait(x_free)

        wi2 = X["w_in_2"][0]
        wqk, tqk = wload(8, wi2[:, 1536:2048])
        wv, twv = wload(7, wi2[:, 2048:2560])
        wg, twg = wload(6, wi2[:, 2560:3072])
        x_rows = scr[0].rearrange("(t p) d -> p t d", p=128)
        t_sp = [dma(S, f"sp{t}", x_rows[:, t, :], XRES[:, t, :], after=[x2[t]]) for t in range(8)]
        WGR = st("wgr", 128).rearrange("p (k n) -> p k n", k=8)
        twr = dma(G, "wgr", WGR, wi2[:, 3072:3088].rearrange("(k p) n -> p k n", p=128))
        GW = bc(1)[0:17, 512:768]
        tgw = [dma(G, "gw", GW[0:16, :], X["gla_gate_w_2"][0], after=now()),
               dma(G, "gwb", GW[16:17, :], X["gla_gate_b_2"][0].rearrange("(a n) -> a n", a=1))]
        A.wait(P.last)
        V.wait(P.last)
        GQ = slot(9)[0:64, :].rearrange("p (h n) -> p h n", h=4)
        GK = slot(10)[0:64, :].rearrange("p (h n) -> p h n", h=4)
        for th in range(2):
            if th:
                xt3.append(fm_half(1, lambda c: nm[:, c:c + 1], u[4:8]))
            for fb in range(4):
                dst = GQ if fb < 2 else GK
                scl = 0.125 if fb < 2 else 1.0
                b = 4 + fb
                tk = mm(b, PS[:, b, :], [(wqk[:, k, 128 * fb:128 * fb + 128], XT[:, k, 512 * th:512 * th + 512])
                                        for k in range(8)], after=[tqk, xt3[th]])
                h0 = 2 * (fb % 2)
                a_(nc.scalar.activation, dst[:, h0, 512 * th:512 * th + 512], PS[0:64, b, :], ACT.Copy, scale=scl,
                   after=[tk])
                bank_free[b] = v(nc.vector.tensor_scalar, dst[:, h0 + 1, 512 * th:512 * th + 512], PS[64:128, b, :],
                                 scl, None, ALU.mult, after=[tk, A.last])
        GR = bc(0)[0:17, :]
        v(nc.vector.memset, GR, 1.0)
        for th in range(2):
            tk = mm(4 + th, PS[0:16, 4 + th, :], [(WGR[:, k, :], XT[:, k, 512 * th:512 * th + 512]) for k in range(8)],
                    after=[twr])
            bank_free[4 + th] = v(nc.vector.tensor_copy, GR[0:16, 512 * th:512 * th + 512], PS[0:16, 4 + th, :],
                                  after=[tk, V.last])
        R6 = slot(8)
        EL, EP, EN, EE = (R6[0:64, 512 * i:512 * i + 512] for i in range(4))
        K2, K3, SS0, SS1 = (R6[0:64, 512 * i:512 * i + 512] for i in range(4, 8))
        Q1, Q2, Q3, K4 = EL, EP, EN, EE
        ELD = st("eld", 8)[0:64, :].rearrange("p (h c) -> p h c", h=4)
        LA, KE = bc(2)[:, 0:256], bc(2)[:, 256:512]
        LB = bc(2)[:, 512:768]
        AT = bc(3)[:, 0:512]
        SQ = bc(3)[:, 512:1024]
        SS = [SS0, SS1]
        VG = bc(1)[:, 0:512]
        A.wait(*now())
        V.wait(*now())
        v(nc.vector.memset, AT, 0.0)
        v(nc.vector.memset, SS[0], 0.0)
        MPI = C("mp").bitcast(I32).unsqueeze(1).to_broadcast([128, 4, 128])
        MFI = C("mf").bitcast(I32).unsqueeze(1).to_broadcast([128, 4, 128])
        gss = st("gss", 32)
        SG = slot(4)[:, 3584:4096]
        GO = slot(5).rearrange("p (t n) -> p t n", t=8)
        V.wait(V.last)

        def h4(ap):
            return ap.rearrange("p (h n) -> p h n", h=4)

        def gate_logs(t):
            pz = mm(2, PS[:, 2, 0:256], [(GR[:, 128 * t:128 * t + 128], GW)], after=[tgw, t_gr])
            a_(nc.scalar.activation, LB, PS[:, 2, 0:256], ACT.Abs, after=[pz, t_la[0]])
            ac(nc.scalar.activation, LB, LB, ACT.Exp, scale=-1.0)
            r = ac(nc.scalar.activation, LB, LB, ACT.Ln, bias=1.0)
            t_la[0] = bank_free[2] = v(nc.vector.scalar_tensor_tensor, out=LA, in0=PS[:, 2, 0:256], scalar=0.0,
                                       in1=LB, op0=ALU.min, op1=ALU.subtract, after=[r, la_free[0]])

        t_gr = V.last
        DWL, DXH, DXL, DWH = (x[:, :] for x in layout(
            ("DPAD0", 2 * SL, F32), ("DWL", SL, F32R), ("DPAD1", SL, F32), ("DXH", 2 * SL, F32R),
            ("DXL", 2 * SL, F32R), ("DWH", SL, F32R)) if "PAD" not in x.name)
        DWR = slot(0)
        DQ = slot(2).rearrange("p (h n) -> p h n", h=4)
        DK = slot(3).rearrange("p (h n) -> p h n", h=4)
        DV = slot(1).rearrange("p (t n) -> p t n", t=8)
        DQT = [bc(0)[:, 256 * i:256 * i + 256] for i in range(4)]
        dw_free, draw_t, dcut_t = [None, None], {}, {}

        def dhalf(x, i):
            return x[:, 2048 * (i % 2):2048 * (i % 2) + 2048]

        def dfetch(i):
            if i < 6:
                draw_t[i] = dma(S, f"dw{i % 2}", dhalf(DWR, i).rearrange("p (k n) -> p k n", k=8),
                                wi2[:, 256 * i:256 * i + 256].rearrange("(k p) n -> p k n", p=128),
                                after=[dcut_t[i - 2]] if i >= 2 else [t_sp, u])

        def dcut(i):
            if i < 6:
                dcut_t[i] = split(dhalf(DWH, i), dhalf(DWL, i), dhalf(DWR, i), after=[draw_t[i], dw_free[i % 2]])

        DX3H, DX3L = (x.rearrange("p (c n) -> p c n", c=8) for x in (DXH, DXL))
        dx_t = []

        def dsplit(th, c, after):
            o = (slice(None), c, slice(512 * th, 512 * th + 512))
            dx_t.append(split(DX3H[o], DX3L[o], XT[o], after=after))

        dfetch(0)
        dfetch(1)
        t_la, la_free = [None], [None]
        pke = pu1 = po = pf = pp = None
        gate_logs(0)
        for t in range(8):
            xt = [XT[:, k, 128 * t:128 * t + 128] for k in range(8)]
            pl = []
            for k3 in range(3):
                for h in range(4):
                    x_ = mm(3 + k3, PS[0:64, 3 + k3, 128 * h:128 * h + 128],
                            [(LA[:, 64 * h:64 * h + 64], C("tri")[:, 128 * k3:128 * k3 + 128])], after=[t_la[0]])
                pl.append(x_)
            la_free[0] = pl[2]
            p0 = mm(0, PS[:, 0, :], [(xt[k], wv[:, k, :]) for k in range(8)], after=[twv])
            t_ee = a_(nc.scalar.activation, EE, PS[0:64, 5, :], ACT.Exp, after=[pl[2], pke])
            bank_free[5] = t_ee
            t_ep = a_(nc.scalar.activation, EP, PS[0:64, 4, :], ACT.Exp, after=[pl[1], pp, V.last])
            t_en = a_(nc.scalar.activation, EN, PS[0:64, 4, :], ACT.Exp, scale=-1.0, after=[pf])
            bank_free[4] = t_en
            t_el = a_(nc.scalar.activation, EL, PS[0:64, 3, :], ACT.Exp, after=[pl[0], po])
            bank_free[3] = t_el
            tv = bank_free[0] = a_(nc.scalar.copy, VG, PS[:, 0, :], after=[p0, pu1, po])
            gq = GQ[:, :, 128 * t:128 * t + 128]
            gk = GK[:, :, 128 * t:128 * t + 128]
            tk4 = v(nc.vector.tensor_tensor, h4(K4), gk, h4(EE), ALU.mult, after=[t_ee])
            v(nc.vector.tensor_tensor, h4(K3), gk, h4(EP), ALU.mult, after=[t_ep, pf])
            v(nc.vector.tensor_tensor, h4(K2), gk, h4(EN), ALU.mult, after=[t_en, pp])
            V.wait(V.last)
            tpast = v(nc.vector.tensor_tensor, h4(Q2), gq, h4(EP), ALU.mult)
            tfut = v(nc.vector.tensor_tensor, h4(Q3), gq, h4(EN), ALU.mult)
            v(nc.vector.tensor_copy, ELD, h4(EL)[:, :, 63:128:64], after=[t_el, V.last])
            tq1 = vc(nc.vector.tensor_tensor, h4(Q1), gq, h4(EL), ALU.mult)
            pke = tr(2, [(PS[:, 2, 64 * h:64 * h + 64], K4[:, 128 * h:128 * h + 128]) for h in range(4)], after=[tk4])
            for h in range(4):
                pp = mm(6, PS[:, 6, 128 * h:128 * h + 128],
                        [(K2[:, 128 * h:128 * h + 128], Q2[:, 128 * h:128 * h + 128])], after=[tpast])
            for h in range(4):
                pf = mm(7, PS[:, 7, 128 * h:128 * h + 128],
                        [(K3[:, 128 * h:128 * h + 128], Q3[:, 128 * h:128 * h + 128])], after=[tfut])
            tke = bank_free[2] = a_(nc.scalar.copy, KE, PS[:, 2, 0:256], after=[pke, pu1])
            v(nc.vector.copy_predicated, h4(AT), MPI, h4(PS[:, 6, :]), after=[pp, po])
            bank_free[6] = V.last
            tat = bank_free[7] = vc(nc.vector.copy_predicated, h4(AT), MFI, h4(PS[:, 7, :]), after=[pf])
            for h in range(4):
                pu0 = mm(4, PS[0:64, 4, 128 * h:128 * h + 128],
                         [(KE[0:64, 64 * h:64 * h + 64], VG[0:64, 128 * h:128 * h + 128])], after=[tke, tv])
            for h in range(4):
                pu1 = mm(5, PS[0:64, 5, 128 * h:128 * h + 128],
                         [(KE[64:128, 64 * h:64 * h + 64], VG[64:128, 128 * h:128 * h + 128])])
            if t < 7:
                gate_logs(t + 1)
            p1 = mm(1, PS[:, 1, :], [(xt[k], wg[:, k, :]) for k in range(8)], after=[twg])
            v(nc.vector.tensor_tensor, h4(SS[1]), h4(SS[0]), ELD[:, :, 0:1].to_broadcast([64, 4, 128]), ALU.mult,
              after=[V.last, po])
            ts1 = bank_free[4] = vc(nc.vector.tensor_tensor, SS[1], SS[1], PS[0:64, 4, :], ALU.add, after=[pu0])
            for h in range(4):
                o = PS[:, 6, 128 * h:128 * h + 128]
                mm(6, o, [(AT[:, 128 * h:128 * h + 128], VG[:, 128 * h:128 * h + 128])], after=[tat])
                mm(6, PS[0:64, 6, 128 * h:128 * h + 128],
                   [(Q1[:, 128 * h:128 * h + 64], SS[0][:, 128 * h:128 * h + 128])], after=[tq1], start=False)
                po = mm(6, PS[64:128, 6, 128 * h:128 * h + 128],
                        [(Q1[:, 128 * h + 64:128 * h + 128], SS[1][:, 128 * h:128 * h + 128])], after=[ts1],
                        start=False)
            if t == 7:
                dw_free[0] = V.last
                dcut(0)
                for c in range(4, 8):
                    dsplit(0, c, [p0, tfut])
            x_ = a_(nc.scalar.activation, SQ, PS[:, 6, :], ACT.Square, after=[po, V.last])
            v(nc.vector.tensor_tensor, h4(SS[0]), h4(SS[1]), ELD[:, :, 1:2].to_broadcast([64, 4, 128]), ALU.mult,
              after=[po])
            bank_free[5] = vc(nc.vector.tensor_tensor, SS[0], SS[0], PS[0:64, 5, :], ALU.add, after=[pu1])
            if t == 7:
                for c in range(4):
                    dsplit(0, c, [po, p1, V.last])
                for c in range(8):
                    dsplit(1, c, [])
            v(nc.vector.tensor_reduce, gss[:, 4 * t:4 * t + 4], h4(SQ), AX, ALU.add, after=[x_])
            bank_free[1] = silu_into(SG, PS[:, 1, :], [p1, V.last])
            bank_free[6] = vc(nc.vector.tensor_tensor, GO[:, t, :], SG, PS[:, 6, :], ALU.mult)
        slot_free[6], slot_free[7], slot_free[8] = p1, p0, now()

        go_done = V.last
        dw_free[1] = go_done
        dcut(1)
        dss = st("dss", 16)
        tm_free = [None] * 4
        pend = []

        def turn_qk():
            i, t, k_, r = pend.pop(0)
            b, o = 4 + k_ % 2, DQT[k_ % 4]
            tm_free[k_ % 4] = p_ = tr(b, [(PS[:, b, 128 * h:128 * h + 128], o[:, 128 * h:128 * h + 128])
                                          for h in range(2)], after=[r])
            h0 = 2 * (i % 2)
            dst = (DQ, DK)[i // 2][:, h0:h0 + 2, 128 * t:128 * t + 128]
            bank_free[b] = a_(nc.scalar.activation, dst, PS[:, b, 0:256].rearrange("p (h n) -> p h n", h=2), ACT.Copy,
                              scale=cols[("daq", "dak")[i // 2]], after=[p_, dx_t])

        for i in range(6):
            hh, ll = (dhalf(x, i).rearrange("p (k n) -> p k n", k=8) for x in (DWH, DWL))
            for t in range(8):
                k_ = 8 * i + t
                b = k_ % 4
                pr = mm3(b, PS[:, b, 0:256], [(DX3H[:, k, 128 * t:128 * t + 128], DX3L[:, k, 128 * t:128 * t + 128],
                                               hh[:, k, :], ll[:, k, :]) for k in range(8)],
                         after=[dcut_t[i], dx_t[8 * (t // 4):8 * (t // 4) + 8]])
                if len(pend) > (1 if i < 4 else 0):
                    turn_qk()
                if i == 4:
                    if t == 0:
                        rsqrt(gss, gss, 1.0 / 128, EPS2, [V.last])
                    o3 = h4(GO[:, t, :])
                    vc(nc.vector.tensor_tensor, o3, o3, b4(gss[:, 4 * t:4 * t + 4], 128), ALU.mult)
                if i >= 4:
                    bank_free[b] = a_(nc.scalar.copy, DV[:, t, 256 * (i - 4):256 * (i - 4) + 256], PS[:, b, 0:256],
                                      after=[pr])
                else:
                    sq = bc(1)[:, 256 * (k_ % 4):256 * (k_ % 4) + 256]
                    d4 = dss[:, 4 * (k_ % 4):4 * (k_ % 4) + 4]
                    x_ = a_(nc.scalar.activation, sq, PS[:, b, 0:256], ACT.Square, after=[pr, V.last])
                    v(nc.vector.tensor_reduce, d4, sq.rearrange("p (h n) -> p h n", h=4), AX, ALU.add, after=[x_])
                    r = rsqrt(d4, d4, 1.0 / 64, EPS2, [V.last])
                    bank_free[b] = r = v(nc.vector.tensor_tensor, DQT[k_ % 4].rearrange("p (h n) -> p h n", h=4),
                                         PS[:, b, 0:256].rearrange("p (h n) -> p h n", h=4), b4(d4, 64), ALU.mult,
                                         after=[r, tm_free[k_ % 4]])
                    pend.append((i, t, k_, r))
                if t == 0:
                    dfetch(i + 2)
                    if i:
                        dcut(i + 1)
            dw_free[i % 2] = P.last
        A.wait(*now())
        V.wait(*now())
        P.wait(*now())
        slot_free[7] = slot_free[8] = t_dap = now()
        t_rl = [dma(S, f"sp{t}", XRES[:, t, :], x_rows[:, t, :], after=[t_dap]) for t in range(4)]
        DO = slot(6).rearrange("p (t n) -> p t n", t=8)
        s23 = slot(8, 2)
        PB1 = [[s23[:, 0:1024], s23[:, 1024:2048]], [s23[:, 2048:3072], s23[:, 3072:4096]]]
        PC = [s23[:, 4096:5120], s23[:, 5120:6144]]
        PT2 = [s23[:, 6144:7168], s23[:, 7168:8192]]

        def da_qk(h, i, m, c0, c1):
            return (DQ[64 * m:64 * m + 64, h, 128 * i:128 * i + 128], DK[64 * m:64 * m + 64, h, c0:c1])

        class Combine:
            free = [None, None]

            def __call__(self, n, nk, pt):
                (t1, r1, _), (t2, r2, _) = pt
                c2 = st(f"c2{n % 2}", 1)
                v(nc.vector.tensor_tensor, c2, r2, nlam, ALU.mult, after=[t1, t2])
                pc = PC[n % 2][:, 0:nk]
                vc(nc.vector.tensor_scalar, pc, PB1[n % 2][1][:, 0:nk], c2, None, ALU.mult, after=[self.free[n % 2]])
                t = vc(nc.vector.scalar_tensor_tensor, out=pc, in0=PB1[n % 2][0][:, 0:nk], scalar=r1, in1=pc,
                       op0=ALU.mult, op1=ALU.add)
                return PC[n % 2], t

        dos = st("dos", 32).rearrange("p (t h) -> p t h", t=8)
        SQD = bc(1)[:, 0:128]

        def da_out(h, i, o, t, pt):
            x_ = a_(nc.scalar.activation, SQD, o, ACT.Square, accum_out=dos[:, i, h:h + 1], after=[t, A.last])
            return v(nc.vector.tensor_copy, DO[:, i, 128 * h:128 * h + 128], o, after=[x_])

        attention([(h, i) for i in range(8) for h in range(4)], da_qk, C("chm"), 64.0 ** -0.5, PB1, PT2,
                  lambda h, j: DV[:, j, 128 * h:128 * h + 128], 128, da_out, nmap=2, combine=Combine())
        dosf = dos.rearrange("p t h -> p (t h)")
        rsqrt(dosf, dosf, 1.0 / 128, EPS2, now())
        att_done = now()
        t_rl += [dma(S, f"sp{t}", XRES[:, t, :], x_rows[:, t, :], after=[att_done]) for t in range(4, 8)]
        dag = st("dag", 1)
        vc(nc.vector.tensor_scalar, dag, cols["daon"], 0.8, None, ALU.mult)
        dag_t = V.last
        do_t = [v(nc.vector.tensor_tensor, h4(DO[:, t, :]), h4(DO[:, t, :]), b4(dos[:, t, :], 128), ALU.mult)
                for t in range(8)]

        MIX2 = [DO, GO]
        A.wait(att_done, dag_t)
        V.wait(att_done)
        def add_res(t, n, ps, tk):
            x = XRES[:, t, 256 * n:256 * n + 256]
            return v(nc.vector.tensor_tensor, x, x, ps, ALU.add, after=[tk, t_rl[t]])

        MEM = BC[:, 2048:4096].rearrange("p (t d) -> p t d", t=2)
        tmem = dma(G, "mem", MEM, X["mem_2"][0].rearrange("(t p) d -> p t d", p=128), after=t_dap)
        mss = st("mss", 2)
        SQC = bc(0)
        for t in range(2):
            a_(nc.scalar.activation, SQC, MEM[:, t, :], ACT.Square, accum_out=mss[:, t:t + 1],
               after=[tmem, V.last, A.last])
        r = rsqrt(mss, mss, 1.0 / 1024, EPS2, [A.last])
        for t in range(2):
            v(nc.vector.tensor_scalar, MEM[:, t, :], MEM[:, t, :], mss[:, t:t + 1], None, ALU.mult, after=[r])
        tm = V.last
        QXH, QWL, QWR, QXL, QWH = (x[:, :] for x in layout(
            ("QXH", 2 * SL, F32R), ("QPAD", 2 * SL, F32), ("QWL", SL, F32R), ("QWR", SL, F32),
            ("QXL", 2 * SL, F32R), ("QWH", SL, F32R)) if "PAD" not in x.name)
        u = project(X["w_o_2"][0], lambda t, c: MIX2[c // 4][:, t, 128 * (c % 4):128 * (c % 4) + 128],
                    lambda c: dag if c < 4 else cols["glon"], add_res, do_t, t_dap, QXH, QXL, QWR, QWH, QWL, [None], rms_tile)
        for s_ in (6, 7, 8):
            slot_free[s_] = P.last

        MEMT = slot(9)[:, 2048:4096].rearrange("p (c n) -> p c n", c=8)
        CK = slot(10)[:, 0:2048].rearrange("p (c n) -> p c n", c=8)
        CV = slot(10)[:, 2048:4096].rearrange("p (t d) -> p t d", t=2)
        tmt = []
        for c in range(8):
            b = c % 4
            p_ = tr(b, [(PS[:, b, 128 * t:128 * t + 128], MEM[:, t, 128 * c:128 * c + 128]) for t in range(2)],
                    after=[tm])
            bank_free[b] = a_(nc.scalar.activation, MEMT[:, c, :], PS[:, b, 0:256], ACT.Copy,
                              scale=cols["nmem"][:, c:c + 1], after=[p_])
            tmt.append(bank_free[b])
        wkv = X["w_ckv_2"][0]
        css = st("css", 4)
        KTM2 = [bc(1)[:, 0:512], bc(1)[:, 512:1024]]
        ktm_free = [None, None]
        waiting = []

        def turn_k():
            n, t, r = waiting.pop(0)
            ktm_free[t] = p_ = tr(6, [(PS[:, 6, 128 * c:128 * c + 128], KTM2[t][:, 128 * c:128 * c + 128])
                                      for c in range(4)], after=[r])
            for dc in range(2):
                o = CK[:, 4 * dc + 2 * n:4 * dc + 2 * n + 2, 128 * t:128 * t + 128]
                i_ = PS[:, 6, :].rearrange("p (h d n) -> p h d n", h=2, d=2)[:, :, dc, :]
                bank_free[6] = a_(nc.scalar.activation, o, i_, ACT.Copy, scale=cols["ckn"][:, dc:dc + 1],
                                  after=[p_])

        for n in range(4):
            s = 6 + n % 3
            w, tw = wload(s, wkv[:, 512 * n:512 * n + 512])
            for t in range(2):
                b = 4 + t
                p_ = mm(b, PS[:, b, :], [(MEMT[:, k, 128 * t:128 * t + 128], w[:, k, :]) for k in range(8)],
                        after=[tw, tmt])
                if waiting:
                    turn_k()
                if n >= 2:
                    bank_free[b] = a_(nc.scalar.copy, CV[:, t, 512 * (n - 2):512 * (n - 2) + 512], PS[:, b, :],
                                      after=[p_])
                    continue
                for hh in range(2):
                    a_(nc.scalar.activation, SQC[:, 0:256], PS[:, b, 256 * hh:256 * hh + 256], ACT.Square,
                       accum_out=css[:, hh:hh + 1], after=[p_, A.last, V.last])
                r = rsqrt(css[:, 0:2], css[:, 0:2], 1.0 / 256, EPS2, [A.last])
                bank_free[b] = r = v(nc.vector.tensor_tensor, KTM2[t].rearrange("p (h n) -> p h n", h=2),
                                     PS[:, b, :].rearrange("p (h n) -> p h n", h=2), b4(css[:, 0:2], 256), ALU.mult,
                                     after=[r, ktm_free[t]])
                waiting.append((n, t, r))
            slot_free[s] = P.last
        nc_ = cols["ncr"]
        V.wait(P.last)
        A.wait(P.last)
        xt4, _ = to_fm(lambda t, c: U[:, t, 128 * c:128 * c + 128], lambda c: nc_[:, c:c + 1], None, u)
        wq_, twq_ = zip(*[wload(6 + n, X["w_cq_2"][0][:, 512 * n:512 * n + 512]) for n in range(2)])
        A.wait(*now())
        V.wait(*now())
        G.wait(*now())
        CQ = bc(0)
        CQT = bc(1).rearrange("p (d h n) -> p d h n", d=2, h=4)
        CP = bc(2).rearrange("p (h n) -> p h n", h=4)
        CPT = bc(3).rearrange("p (m h n) -> p m h n", m=2, h=4)
        cm, cr = st("cm", 4), st("cr", 4)
        s4_ = PS[:, 4:6, :].rearrange("p b n -> p (b n)").rearrange("p (h n) -> p h n", h=4)
        JUNK = slot(8)[:, 0:256]
        css_ = [st("cssa", 4), st("cssb", 4)]
        cr_ = [st("cra", 4), st("crb", 4)]
        tq_t, cq_t, cpt_t = {}, {}, {}
        pav = pcq = psc = cp_free = None

        def q_part(t, n):
            pq = mm(n, PS[:, n, :], [(XT[:, k, 128 * t:128 * t + 128], wq_[n][:, k, :]) for k in range(8)],
                    after=[twq_[n], xt4])
            for h in range(2 * n, 2 * n + 2):
                ac(nc.scalar.activation, JUNK, PS[:, n, 256 * (h % 2):256 * (h % 2) + 256], ACT.Square,
                   accum_out=css_[t % 2][:, h:h + 1], after=[pq, V.last])

        def q_norm(t):
            c_ = css_[t % 2]
            r = rsqrt(c_, c_, 1.0 / 256, EPS2, [A.last])
            bank_free[0] = bank_free[1] = cq_t[t] = v(
                nc.vector.tensor_tensor, CQ.rearrange("p (h n) -> p h n", h=4),
                PS[:, 0:2, :].rearrange("p b n -> p (b n)").rearrange("p (h n) -> p h n", h=4), b4(c_, 256), ALU.mult,
                after=[r, pcq])

        def values(t):
            for h in range(4):
                b = 6 + h // 2
                po = mm(b, PS[:, b, 256 * (h % 2):256 * (h % 2) + 256],
                        [(CPT[:, m, h, :], CV[:, m, 256 * h:256 * h + 256]) for m in range(2)], after=[cpt_t[t]])
            bank_free[6] = bank_free[7] = v(
                nc.vector.tensor_tensor, U[:, t, :].rearrange("p (h n) -> p h n", h=4),
                PS[:, 6:8, :].rearrange("p b n -> p (b n)").rearrange("p (h n) -> p h n", h=4), b4(cr_[t % 2], 256),
                ALU.mult, after=[po])
            return po

        q_part(0, 0)
        q_part(0, 1)
        q_norm(0)
        for t in range(8):
            if t:
                pav = values(t - 1)
            for dc in range(2):
                p_ = tr(2 + dc, [(PS[:, 2 + dc, 128 * h:128 * h + 128], CQ[:, 256 * h + 128 * dc:256 * h + 128 * dc + 128])
                                 for h in range(4)], after=[cq_t[t]])
                bank_free[2 + dc] = a_(nc.scalar.activation, CQT[:, dc, :, :], h4(PS[:, 2 + dc, :]), ACT.Copy,
                                       scale=cols["cqn"][:, dc:dc + 1], after=[p_, psc])
            pcq, tq = P.last, A.last
            if t < 7:
                q_part(t + 1, 0)
            for h in range(4):
                b = 4 + h // 2
                psc = mm(b, PS[:, b, 256 * (h % 2):256 * (h % 2) + 256],
                         [(CQT[:, dc, h, :], CK[:, 4 * dc + h, :]) for dc in range(2)], after=[tq])
            v(nc.vector.tensor_reduce, cm, s4_, AX, ALU.max, after=[psc, A.last])
            r = vc(nc.vector.tensor_scalar, cm, cm, -1.0 / 16, None, ALU.mult)
            for h in range(4):
                a_(nc.scalar.activation, CP[:, h, :], s4_[:, h, :], ACT.Exp, bias=cm[:, h:h + 1], scale=1.0 / 16,
                   accum_out=cr_[t % 2][:, h:h + 1], after=[r, cp_free])
            te = bank_free[4] = bank_free[5] = A.last
            r = v(nc.vector.reciprocal, cr_[t % 2], cr_[t % 2], after=[te])
            if t < 7:
                q_part(t + 1, 1)
            if t == 6:
                t_junk = [A.last, V.last, P.last]
            for m in range(2):
                p_ = tr(6 + m, [(PS[:, 6 + m, 128 * h:128 * h + 128], CP[:, h, 128 * m:128 * m + 128])
                                for h in range(4)], after=[te])
                bank_free[6 + m] = v(nc.vector.tensor_copy, CPT[:, m, :, :], h4(PS[:, 6 + m, :]), after=[p_, pav])
            cp_free, cpt_t[t] = P.last, V.last
            if t < 7:
                q_norm(t + 1)
        values(7)
        slot_free[6] = slot_free[7] = P.last
        A.wait(*now())
        V.wait(*now())
        XZ, YO = scr
        t_nf = dma(G, "bc0", bc(0), X["norm_ffn_2"][0].partition_broadcast(128), after=now())
        t_xz = []

        def expert_input(t, tok, t_src):
            r = rms_tile(t, tok, t_src)
            r = v(nc.vector.tensor_tensor, U[:, t, :], U[:, t, :], bc(0), ALU.mult, after=[r, t_nf])
            u.append(r)
            t_xz.append(dma(S, f"xz{t}", XZ.rearrange("(t p) d -> p t d", p=128)[:, t, :], U[:, t, :], after=[r]))
            if t >= 3:
                logits(t - 3)
            if t >= 2:
                turn_tile(t - 2)
            return r

        u = []
        RT = bc(3).rearrange("p (c n) -> p c n", c=8)
        rt_t = [None]

        def turn_tile(t):
            for hf in range(2):
                p_ = tr(hf, [(PS[:, hf, 128 * c:128 * c + 128], U[:, t, 512 * hf + 128 * c:512 * hf + 128 * c + 128])
                             for c in range(4)], after=[u[t]])
                rt_t[0] = bank_free[hf] = a_(nc.scalar.copy, RT[:, 4 * hf:4 * hf + 4, :],
                                             PS[:, hf, :].rearrange("p (c n) -> p c n", c=4), after=[p_])

        def logits(t):
            b = 2 + t // 4
            return mm(b, PS[:, b, 128 * (t % 4):128 * (t % 4) + 128],
                      [(RT[:, k, :], WRT[:, k, :]) for k in range(8)], after=[twr, rt_t[0]])

        WRT = bc(1).rearrange("p (k n) -> p k n", k=8)
        g_(nc.gpsimd.memset, WRT, 0.0, after=now())
        twr = [dma(G, "wr0", WRT[:, :, 0:4], X["w_group_2"][0].rearrange("(k p) n -> p k n", p=128), after=now()),
               dma(G, "wr1", WRT[:, :, 4:36], X["w_expert_2"][0].rearrange("(k p) n -> p k n", p=128))]
        BR = bc(2)[:, 0:36]
        tbr = [dma(G, "br0", BR[:, 0:4], X["b_group_2"][0].partition_broadcast(128)),
               dma(G, "br1", BR[:, 4:36], X["b_expert_2"][0].partition_broadcast(128))]
        RXH, RXL, RWR, RWH, RWL = (x[:, :] for x in layout(
            ("RXH", 2 * SL, F32R), ("RPAD", 2 * SL, F32), ("RXL", 2 * SL, F32R), ("RWR", SL, F32),
            ("RWH", SL, F32R), ("RWL", SL, F32R)) if "PAD" not in x.name)
        project(X["w_co_2"][0], lambda t, c: U[:, t, 128 * c:128 * c + 128], lambda c: one1, add_res, [now()] * 8, t_junk,
                    RXH, RXL, RWR, RWH, RWL, [None], expert_input)
        co_done = P.last

        logits(5)
        turn_tile(6)
        logits(6)
        turn_tile(7)
        pr = logits(7)
        W9, slot9 = slot(10), slot(9)
        cut_free = [pr, t_xz]
        MH, ML, MR, MX, MTH, MTL = layout(("MH", 2 * SL, F32R), ("ML", 2 * SL, F32R), ("MR", 3 * SL, F32),
                                          ("MX", SL, F32R), ("MTH", 512, F32R), ("MTL", 512, F32R))
        MTH, MTL = MTH[:, :], MTL[:, :]

        def hi4(ap, c):
            return ap[:, 128 * c:128 * c + 128]

        XB = [bc(0), bc(1)]
        assert CONSTS["ident"][0] == 0 and cst.shape[1] >= 1664
        HID = CT[:, 128:640]
        YB = [CT[:, 1152:1664], CSN[:, 0:512]]
        weg, weu, wed = X["w_e_gate_2"][0], X["w_e_up_2"][0], X["w_e_down_2"][0]
        MXH = [MX[:, 2048 * i:2048 * i + 1024].rearrange("p (c n) -> p c n", c=8) for i in range(2)]
        MXL = [MX[:, 2048 * i + 1024:2048 * i + 2048].rearrange("p (c n) -> p c n", c=8) for i in range(2)]

        def experts(blocks, raw_free, free):
            xb_free, xbt_free, yb_free = [None, None], [None, None], [None, None]
            hid_free = hit_free = None
            xb_t, xbt_t, hid_t, hit_t = {}, {}, {}, {}
            first, last = blocks[0], blocks[-1]
            order = []
            for b in [*blocks, last + 1]:
                if b <= last:
                    order += [(0, b, 0), (0, b, 1), (1, b, 0), (1, b, 1)]
                if b > first:
                    order += [(2, b - 1, 0), (2, b - 1, 1)]
            NR, NH = 6, 4
            raw_t, cut_t, used = {}, {}, {}

            def fetch(i):
                if i >= len(order):
                    return
                w_, b, hf = order[i]
                src = (weg, weu, wed)[w_]
                if b < 32:
                    src = src[b]
                else:
                    e_ = nc.sync.value_load(OVI[0:1, b - 32:b - 31], min_val=0, max_val=31)
                    src = src[bass.ds(e_, 1), :, :].rearrange("a k n -> (a k) n")
                k = src.shape[0] // 2
                o = MR[:, 2048 * (i % NR):2048 * (i % NR) + 2048].rearrange("p (k n) -> p k n", k=k // 128)
                raw_t[i] = dma(S, f"mw{i % NR}", o, src[k * hf:k * hf + k, :].rearrange("(k p) n -> p k n", p=128),
                               after=[cut_t[i - NR]] if i >= NR else [raw_free])

            def cut(i):
                if i < len(order):
                    x = MR[:, 2048 * (i % NR):2048 * (i % NR) + 2048]
                    o = (slice(None), slice(2048 * (i % NH), 2048 * (i % NH) + 2048))
                    t = a_(nc.scalar.copy, MH[o], x, after=[raw_t[i], used[i - NH] if i >= NH else free])
                    if i % 3 == 2 or i < 3:
                        t = g_(nc.gpsimd.tensor_tensor, ML[o], x, MH[o].bitcast(F32), ALU.subtract,
                               after=[t, used[i - NH] if i >= NH else free])
                    else:
                        t = v(nc.vector.tensor_tensor, ML[o], x, MH[o].bitcast(F32), ALU.subtract,
                              after=[t, used[i - NH] if i >= NH else free])
                    cut_t[i] = t

            def gather(b):
                name = branch[0] + f"gat{b % 2}"
                if name not in dsems:
                    dsems[name] = DmaSem("d_" + name)
                d = dsems[name]
                if d.n:
                    G.wait((d.sem, 16 * d.n))
                G.wait(xb_free[b % 2])
                nc.gpsimd.indirect_dma_start(
                    XB[b % 2], None, XZ,
                    bass.IndirectOffsetOnAxis(IDX.bitcast(U32)[:, b:b + 1], 0)).then_inc(d.sem, 16)
                d.n += 1
                xb_t[b] = (d.sem, 16 * d.n)

            def turn(b):
                for hf in range(2):
                    p_ = tr(hf, [(PS[:, hf, 128 * c:128 * c + 128],
                                  XB[b % 2][:, 512 * hf + 128 * c:512 * hf + 128 * c + 128]) for c in range(4)],
                            after=[xb_t[b]])
                    bank_free[hf] = split(MXH[b % 2][:, 4 * hf:4 * hf + 4, :], MXL[b % 2][:, 4 * hf:4 * hf + 4, :],
                                          h4(PS[:, hf, :]), after=[p_, xbt_free[b % 2]])
                xb_free[b % 2] = P.last
                xbt_t[b] = V.last

            at = [0]

            def use(k, products):
                i = at[0]
                at[0] += 1
                o = (slice(None), slice(2048 * (i % NH), 2048 * (i % NH) + 2048))
                P.wait(cut_t[i])
                used[i] = products(MH[o].rearrange("p (k n) -> p k n", k=k), ML[o].rearrange("p (k n) -> p k n", k=k))
                cut(i + 3)
                fetch(i + 3 + NR)
                return used[i]

            for i in range(NR):
                fetch(i)
            for i in range(3):
                cut(i)
                fetch(i + NR)
            yield
            gather(first)
            gather(first + 1)
            turn(first)
            for b in [*blocks, last + 1]:
                if b <= last:
                    xh, xl = MXH[b % 2], MXL[b % 2]
                    done = []
                    for bank in (2, 3):
                        for hf in range(2):
                            def gu(wh, wl):
                                return mm(bank, PS[:, bank, :],
                                          [pr_ for k in range(4) for pr_ in
                                           ((xh[:, 4 * hf + k, :], wh[:, k, :]), (xl[:, 4 * hf + k, :], wh[:, k, :]),
                                            (xh[:, 4 * hf + k, :], wl[:, k, :]))],
                                          after=[xbt_t[b]], start=(hf == 0))
                            done.append(use(4, gu))
                        if bank == 2:
                            t_silu = bank_free[2] = a_(nc.scalar.activation, HID, PS[:, 2, :], ACT.Silu,
                                                       after=[done[1], hid_free])
                    xbt_free[b % 2] = done[3]
                    hid_t[b] = bank_free[3] = v(nc.vector.tensor_tensor, HID, HID, PS[:, 3, :], ALU.mult,
                                                after=[t_silu, done[3]])
                    if b < last:
                        turn(b + 1)
                        if b + 1 < last:
                            gather(b + 2)
                if b > first:
                    for hf in range(2):
                        def dn(wh, wl):
                            for n in range(2):
                                r = mm(5 + n, PS[:, 5 + n, :],
                                       [pr_ for k in range(2) for pr_ in
                                        ((hi4(MTH, 2 * hf + k), wh[:, k, 512 * n:512 * n + 512]),
                                         (hi4(MTL, 2 * hf + k), wh[:, k, 512 * n:512 * n + 512]),
                                         (hi4(MTH, 2 * hf + k), wl[:, k, 512 * n:512 * n + 512]))],
                                       after=[hit_t[b - 1]], start=(hf == 0))
                            return r
                        use(2, dn)
                    hit_free = P.last
                    for n in range(2):
                        bank_free[5 + n] = a_(nc.scalar.copy, YB[n], PS[:, 5 + n, :], after=[hit_free, yb_free[n]])
                        yb_free[n] = dma(A, f"yo{n}", YO[128 * (b - 1):128 * b, 512 * n:512 * n + 512], YB[n],
                                         after=[A.last])
                if b <= last:
                    hid_free = tr(4, [(PS[:, 4, 128 * c:128 * c + 128], HID[:, 128 * c:128 * c + 128])
                                      for c in range(4)], after=[hid_t[b]])
                    hit_t[b] = bank_free[4] = split(MTH, MTL, PS[:, 4, :], after=[hid_free, hit_free])
            yield yb_free

        run_main = experts(range(32), co_done, cut_free)
        next(run_main)
        wat = [0]

        def wk_(n):
            a = wat[0]
            wat[0] += n
            assert wat[0] <= 4096
            return W9[:, a:a + n]

        TT = nc.vector.tensor_tensor
        TS = nc.vector.tensor_scalar
        LG = wk_(288).rearrange("p (t n) -> p t n", t=8)
        bank_free[2] = bank_free[3] = vc(TT, LG, PS[:, 2:4, :].rearrange("p b (t n) -> p (b t) n", t=4)[:, :, 0:36],
                          BR.unsqueeze(1).to_broadcast([128, 8, 36]), ALU.add, after=[pr, *tbr])
        io = C("io")

        def bt(ap, n):
            return ap.unsqueeze(2).to_broadcast([128, 8, n])

        def first_max(x, n):
            m_, i_ = wk_(8), wk_(8)
            eq = wk_(8 * n).rearrange("p (t n) -> p t n", t=8)
            vc(nc.vector.tensor_reduce, m_, x, AX, ALU.max)
            vc(TT, eq, x, bt(m_, n), ALU.is_equal)
            vc(TS, eq, eq, -100.0, 100.0, ALU.mult, ALU.add)
            vc(TT, eq, eq, io[:, 0:n].unsqueeze(1).to_broadcast([128, 8, n]), ALU.add)
            vc(nc.vector.tensor_reduce, i_, eq, AX, ALU.min)
            return m_, i_

        def one_hot(i_, n):
            o = wk_(8 * n).rearrange("p (t n) -> p t n", t=8)
            vc(TT, o, io[:, 0:n].unsqueeze(1).to_broadcast([128, 8, n]), bt(i_, n), ALU.is_equal)
            return o

        gm, gi = first_max(LG[:, :, 0:4], 4)
        ge = wk_(32).rearrange("p (t n) -> p t n", t=8)
        vc(TT, ge, LG[:, :, 0:4], bt(gm, 4), ALU.subtract)
        t = a_(nc.scalar.activation, ge, ge, ACT.Exp, after=[V.last])
        pg = wk_(8)
        v(nc.vector.tensor_reduce, pg, ge, AX, ALU.add, after=[t])
        vc(nc.vector.reciprocal, pg, pg)
        o4 = one_hot(gi, 4)
        em = wk_(256).rearrange("p (t g e) -> p t g e", t=8, g=4)
        vc(TT, em, LG[:, :, 4:36].rearrange("p t (g e) -> p t g e", g=4),
           o4.unsqueeze(3).to_broadcast([128, 8, 4, 8]), ALU.mult)
        ELG = wk_(64).rearrange("p (t n) -> p t n", t=8)
        vc(nc.vector.tensor_reduce, ELG, em.rearrange("p t g e -> p t e g"), AX, ALU.add)
        m1, i1 = first_max(ELG, 8)
        oh1 = one_hot(i1, 8)
        vc(nc.vector.scalar_tensor_tensor, out=ELG, in0=oh1, scalar=NEG, in1=ELG, op0=ALU.mult, op1=ALU.add)
        m2, i2 = first_max(ELG, 8)
        dd, g1, g2 = wk_(8), st("g1", 8), st("g2", 8)
        vc(TT, dd, m2, m1, ALU.subtract)
        t = a_(nc.scalar.activation, dd, dd, ACT.Exp, after=[V.last])
        v(TS, g1, dd, 1.0, None, ALU.add, after=[t])
        vc(nc.vector.reciprocal, g1, g1)
        vc(TT, g1, g1, pg, ALU.mult)
        vc(TT, g2, g1, dd, ALU.mult)
        ES = wk_(16)
        vc(nc.vector.scalar_tensor_tensor, out=ES[:, 0:8], in0=gi, scalar=8.0, in1=i1, op0=ALU.mult, op1=ALU.add)
        v(nc.vector.scalar_tensor_tensor, out=ES[:, 8:16], in0=gi, scalar=8.0, in1=i2, op0=ALU.mult, op1=ALU.add)
        OH = wk_(512).rearrange("p (k n) -> p k n", k=16)
        io32 = io[:, 0:32].unsqueeze(1).to_broadcast([128, 16, 32])
        vc(TT, OH, io32, ES.unsqueeze(2).to_broadcast([128, 16, 32]), ALU.is_equal)
        MM = wk_(256)
        M3 = MM.rearrange("p (t n) -> p t n", t=8)
        tm = vc(TT, M3, OH[:, 0:8, :], OH[:, 8:16, :], ALU.add)
        p1 = mm(5, PS[:, 5, 0:256], [(C("su"), MM)], after=[tm])
        p2 = mm(6, PS[:, 6, 0:256], [(C("one"), MM)])
        RS = [wk_(384).rearrange("p (t n) -> p t n", t=12) for _ in range(2)]
        for r_ in RS:
            v(nc.vector.memset, r_[:, 0:4, :], 0.0)
        vc(nc.vector.tensor_copy, RS[0][:, 4:12, :], PS[:, 6, 0:256].rearrange("p (t n) -> p t n", t=8), after=[p2])
        for k_, sft in enumerate((1, 2, 4)):
            x_, y_ = RS[k_ % 2], RS[(k_ + 1) % 2]
            vc(TT, y_[:, 4:12, :], x_[:, 4:12, :], x_[:, 4 - sft:12 - sft, :], ALU.add)
        RUN = RS[1]
        PRE = wk_(256).rearrange("p (t n) -> p t n", t=8)
        vc(TT, PRE, PS[:, 5, 0:256].rearrange("p (t n) -> p t n", t=8), RUN[:, 3:11, :], ALU.add, after=[p1])
        bank_free[5] = bank_free[6] = V.last
        run = RUN[:, 11, :]
        thr = C("thr")
        cmp_ = wk_(224).rearrange("p (e k) -> p e k", e=32)
        SC_ = [wk_(48) for _ in range(2)]
        for r_ in SC_:
            v(nc.vector.memset, r_[:, 0:16], 0.0)
        vc(nc.vector.scalar_tensor_tensor, out=cmp_, in0=run.unsqueeze(2).to_broadcast([128, 32, 7]), scalar=-1.0,
           in1=thr.unsqueeze(1).to_broadcast([128, 32, 7]), op0=ALU.add, op1=ALU.is_gt)
        ob = wk_(32)
        vc(nc.vector.tensor_reduce, ob, cmp_, AX, ALU.add)
        vc(nc.vector.tensor_copy, SC_[0][:, 16:48], ob)
        for k_, sft in enumerate((1, 2, 4, 8, 16)):
            x_, y_ = SC_[k_ % 2], SC_[(k_ + 1) % 2]
            vc(TT, y_[:, 16:48], x_[:, 16:48], x_[:, 16 - sft:48 - sft], ALU.add)
        a1 = SC_[1][:, 16:48]
        os_ = wk_(32)
        vc(TT, os_, a1, ob, ALU.subtract)
        prod = wk_(512).rearrange("p (k n) -> p k n", k=16)
        rk, osa, qq, cq, blk = wk_(16), wk_(16), wk_(16), wk_(16), wk_(16)
        vc(TT, prod.rearrange("p (k t) n -> p k t n", k=2), OH.rearrange("p (k t) n -> p k t n", k=2),
           PRE.unsqueeze(1).to_broadcast([128, 2, 8, 32]), ALU.mult)
        vc(nc.vector.tensor_reduce, rk, prod, AX, ALU.add)
        vc(TT, prod, OH, os_.unsqueeze(1).to_broadcast([128, 16, 32]), ALU.mult)
        vc(nc.vector.tensor_reduce, osa, prod, AX, ALU.add)
        cmq = wk_(112).rearrange("p (e k) -> p e k", e=16)
        vc(TT, cmq, rk.unsqueeze(2).to_broadcast([128, 16, 7]), thr.unsqueeze(1).to_broadcast([128, 16, 7]),
           ALU.is_gt)
        vc(nc.vector.tensor_reduce, qq, cmq, AX, ALU.add)
        vc(nc.vector.scalar_tensor_tensor, out=blk, in0=osa, scalar=31.0, in1=qq, op0=ALU.add, op1=ALU.add)
        vc(TT, blk, blk, ES, ALU.subtract)
        vc(TS, cq, qq, 1.0, None, ALU.min)
        vc(TT, blk, blk, cq, ALU.mult)
        vc(TT, blk, blk, ES, ALU.add)
        vc(nc.vector.scalar_tensor_tensor, out=rk, in0=qq, scalar=-128.0, in1=rk, op0=ALU.mult, op1=ALU.add)
        PH = slot9[:, 1152:3200].rearrange("p (k n) -> p k n", k=16)
        RB = slot9[:, 3200:3200 + 16 * NBLK].rearrange("p (k n) -> p k n", k=16)
        vc(TT, PH, io.unsqueeze(1).to_broadcast([128, 16, 128]), rk.unsqueeze(2).to_broadcast([128, 16, 128]),
           ALU.is_equal)
        vc(TT, RB, io[:, 0:NBLK].unsqueeze(1).to_broadcast([128, 16, NBLK]),
           blk.unsqueeze(2).to_broadcast([128, 16, NBLK]), ALU.is_equal)
        R4 = RB.rearrange("p (k t) n -> p k t n", k=2)
        t = vc(TT, R4, R4, C("tok").unsqueeze(1).unsqueeze(3).to_broadcast([128, 2, 8, NBLK]), ALU.mult)
        p_ = mm(7, PS[:, 7, 0:NBLK], [(PH[:, k, :], RB[:, k, :]) for k in range(16)], after=[t])
        IDX = st("idx", NBLK).bitcast(I32)
        t_idx = bank_free[7] = v(nc.vector.tensor_copy, IDX, PS[:, 7, 0:NBLK], after=[p_])
        G.wait(t_idx, t_xz)
        V.wait(V.last)
        SLOTS = st("slots", 16).bitcast(I32)
        vc(nc.vector.scalar_tensor_tensor, out=qq, in0=blk, scalar=128.0, in1=rk, op0=ALU.mult, op1=ALU.add)
        t_sl = vc(nc.vector.tensor_copy, SLOTS, qq)
        ov = wk_(NOVF)
        co_ = em.rearrange("p t g e -> p (t g e)")[:, 0:32]
        for jj in range(NOVF):
            v(TS, co_, a1, jj + 0.5, None, ALU.is_lt, after=[V.last])
            vc(nc.vector.tensor_reduce, ov[:, jj:jj + 1], co_, AX, ALU.add)
        vc(TS, ov, ov, 31.0, None, ALU.min)
        OVI = st("ovi", NOVF).bitcast(I32)
        vc(nc.vector.tensor_copy, OVI, ov)
        NOV = st("nov", 1).bitcast(I32)
        t_ovi = vc(nc.vector.tensor_copy, NOV, a1[:, 31:32])
        A.wait(*now())
        V.wait(*now())
        G.wait(*now())
        y_out = next(run_main)
        for q in (P, V, A, G, S):
            q.wait(t_ovi, t_sl, t_zy, *now(), *y_out)
        n_over = nc.values_load(NOV[0:1, 0:1], min_val=0, max_val=NOVF)
        with branch_of(n_over > 0):
            for _ in experts(range(32, NBLK), None, None):
                pass

        GB = MR[:, 0:8192].rearrange("p (n d) -> p n d", n=8)
        cg = [DmaSem(f"cg{i}") for i in range(8)]
        cg_free = [None] * 8
        odma = []
        for n in range(16):
            t, kk = n // 2, n % 2
            d = cg[n % 8]
            G.wait(cg_free[n % 8])
            if d.n:
                G.wait((d.sem, 16 * d.n))
            nc.gpsimd.indirect_dma_start(GB[:, n % 8, :], None, YO,
                                         bass.IndirectOffsetOnAxis(SLOTS.bitcast(U32)[:, 8 * kk + t:8 * kk + t + 1], 0)).then_inc(d.sem, 16)
            d.n += 1
            gt = (g1, g2)[kk]
            r = vc(nc.vector.scalar_tensor_tensor, out=XRES[:, t, :], in0=GB[:, n % 8, :], scalar=gt[:, t:t + 1],
                   in1=XRES[:, t, :], op0=ALU.mult, op1=ALU.add, after=[(d.sem, 16 * d.n)])
            cg_free[n % 8] = r
            if kk:
                odma.append(dma(S, f"o{t}", out[0].rearrange("(t p) d -> p t d", p=128)[:, t, :], XRES[:, t, :],
                                after=[r]))
        S.wait(*odma)


def kernel(**inputs):
    import concourse.bacc as _bacc
    from concourse.bass_utils import run_bass_kernel_spmd as _run

    nc = _bacc.Bacc("TRN2", target_bir_lowering=False, num_devices=1)
    arrays, X = {}, {}
    for name, val in inputs.items():
        a = np.ascontiguousarray(val)
        arrays[f"in_{name}"] = a
        X[name] = nc.dram_tensor(f"in_{name}", a.shape, mybir.dt.from_np(a.dtype), kind="ExternalInput").ap()
    table = const_table()
    arrays["in_table"] = table
    cst = nc.dram_tensor("in_table", table.shape, F32, kind="ExternalInput").ap()
    out = nc.dram_tensor("out_0", (1, 1024, 1024), F32, kind="ExternalOutput").ap()
    scr = (nc.dram_tensor("xz", (1024, 1024), F32).ap(), nc.dram_tensor("yo", (NBLK * 128, 1024), F32).ap())
    program(nc, X, out, cst, scr)
    r = _run(nc, [arrays], core_ids=[0])
    return r.results[0]["out_0"]
```
